# Optimizing a Trainium2 kernel written in Bass

```python
import jax, jax.numpy as jnp
from jax import lax
import numpy as np

D_MODEL = 1024
BATCH = 1
SEQ = 512
DEPTH = 2
DEC_BATCH = 8
DEC_SEQ = 1
PAST_LEN = 1024
PAGE_SIZE = 128

N_AB = (DEPTH + 1) // 2
N_C = DEPTH // 2
CONV_GROUPS = 8
D_CONV = D_MODEL // 2
CONV_W = 3
N_HEADS_B = 8
HEAD_DIM_B = 64
D_ATT = N_HEADS_B * HEAD_DIM_B
Q_BLOCK = 128
FORGET_BIAS_INIT = 3.0
D_IN_AB = 3 * D_CONV + 3 * D_ATT + N_HEADS_B
CHUNK = 128
SG_GROUPS = 8
D_SG = D_MODEL
SG_GROUP_DIM = D_SG // SG_GROUPS
PEER_HEADS = 8
PEER_NKEYS = 128
PEER_N = PEER_NKEYS * PEER_NKEYS
PEER_DK = 256
PEER_TOPK = 16
PEER_BLOCK = 256
DN_ALPHA = (2.0 * DEPTH) ** 0.25
DN_BETA = (8.0 * DEPTH) ** -0.25
LN_EPS = 1e-5

kernel_name = "hybrid_conv_fox_gmlp_peer_decode_step"

def _layer_norm(x, g, b):
    xf = x.astype(jnp.float32)
    mu = jnp.mean(xf, axis=-1, keepdims=True)
    var = jnp.mean(jnp.square(xf - mu), axis=-1, keepdims=True)
    return ((xf - mu) * lax.rsqrt(var + LN_EPS) * g + b).astype(x.dtype)

def _short_conv(z, prev, w):
    zp = jnp.concatenate([prev.astype(z.dtype), z], axis=1)
    t = z.shape[1]
    y = sum(w[j] * zp[:, j:j + t] for j in range(CONV_W))
    return y, zp[:, -(CONV_W - 1):]

def _fox_prompt(q, k, v, logf):
    n, t, h, d = q.shape
    nb = t // Q_BLOCK
    cum = jnp.cumsum(logf, axis=1)
    qb = q.reshape(n, nb, Q_BLOCK, h, d).transpose(1, 0, 2, 3, 4)
    cb = cum.reshape(n, nb, Q_BLOCK, h).transpose(1, 0, 2, 3)
    starts = jnp.arange(nb) * Q_BLOCK
    key_pos = jnp.arange(t)
    cum_k = cum.transpose(0, 2, 1)[:, :, None, :]
    scale = HEAD_DIM_B ** -0.5

    def block(args):
        qi, ci, s0 = args
        s = jnp.einsum('nqhd,nkhd->nhqk', qi, k, preferred_element_type=jnp.float32) * scale
        s = s + ci.transpose(0, 2, 1)[..., None] - cum_k
        qpos = s0 + jnp.arange(Q_BLOCK)
        s = jnp.where(key_pos[None, :] <= qpos[:, None], s, -jnp.inf)
        p = jax.nn.softmax(s, axis=-1).astype(v.dtype)
        return jnp.einsum('nhqk,nkhd->nqhd', p, v)

    o = lax.map(block, (qb, cb, starts))
    return o.transpose(1, 0, 2, 3, 4).reshape(n, t, h, d)

def _fox_sample(q, k, v, logf, pk, pv, plogf):
    n, t, h, d = q.shape
    p_len = pk.shape[1]
    keys = jnp.concatenate([pk.astype(k.dtype), k], axis=1)
    vals = jnp.concatenate([pv.astype(v.dtype), v], axis=1)
    cum = jnp.cumsum(jnp.concatenate([plogf.astype(jnp.float32), logf], axis=1), axis=1)
    s = jnp.einsum('nqhd,nkhd->nhqk', q, keys, preferred_element_type=jnp.float32) * (HEAD_DIM_B ** -0.5)
    s = s + cum[:, p_len:].transpose(0, 2, 1)[..., None] - cum.transpose(0, 2, 1)[:, :, None, :]
    mask = jnp.arange(p_len + t)[None, :] <= (p_len + jnp.arange(t))[:, None]
    s = jnp.where(mask, s, -jnp.inf)
    p = jax.nn.softmax(s, axis=-1).astype(v.dtype)
    return jnp.einsum('nhqk,nkhd->nqhd', p, vals)

def _ab_mixer(x, w_in, b_f, conv_w, w_o, conv_prev, past):
    n, t, _ = x.shape
    cuts = np.cumsum([D_CONV, D_CONV, D_CONV, D_ATT, D_ATT, D_ATT]).tolist()
    gb, gc, hc, q, k, v, fl = jnp.split(x @ w_in, cuts, axis=-1)
    z = gc * hc
    if conv_prev is None:
        conv_prev = jnp.zeros((n, CONV_W - 1, D_CONV), z.dtype)
    yc, conv_new = _short_conv(z, conv_prev, conv_w)
    a_out = gb * yc
    q = q.reshape(n, t, N_HEADS_B, HEAD_DIM_B)
    k = k.reshape(n, t, N_HEADS_B, HEAD_DIM_B)
    v = v.reshape(n, t, N_HEADS_B, HEAD_DIM_B)
    logf = jax.nn.log_sigmoid((fl + b_f).astype(jnp.float32))
    if past is None:
        o = _fox_prompt(q, k, v, logf)
    else:
        o = _fox_sample(q, k, v, logf, *past)
    out = jnp.concatenate([a_out, o.reshape(n, t, D_ATT)], axis=-1) @ w_o
    return out, k, v, logf, conv_new

def _chunk_spatial(v, w_s, b_s):
    n, t, c = v.shape
    nch = -(-t // CHUNK)
    tp = nch * CHUNK
    vp = jnp.pad(v, ((0, 0), (0, tp - t), (0, 0))).reshape(n, nch, CHUNK, SG_GROUPS, SG_GROUP_DIM)
    w = w_s * jnp.tril(jnp.ones((CHUNK, CHUNK), w_s.dtype))
    y = jnp.einsum('gij,nkjgc->nkigc', w, vp) + b_s.T[None, None, :, :, None]
    return y.reshape(n, tp, c)[:, :t]

def _chunk_mixer(x, w_in, ln_g, ln_b, w_s, b_s, w_o):
    u, v = jnp.split(jax.nn.gelu(x @ w_in), 2, axis=-1)
    v = _layer_norm(v, ln_g, ln_b)
    return (u * _chunk_spatial(v, w_s, b_s)) @ w_o, v

def _peer(x, wq, keys, u_tab, v_tab):
    shp = x.shape
    xf = x.reshape(-1, D_MODEL)
    n = xf.shape[0]
    q = (xf @ wq).reshape(n, PEER_HEADS, 2, PEER_DK // 2)
    s = jnp.einsum('nhpd,hpkd->nhpk', q, keys, preferred_element_type=jnp.float32)
    top_s, top_i = lax.top_k(s, PEER_TOPK)
    cand_s = top_s[:, :, 0, :, None] + top_s[:, :, 1, None, :]
    cand_i = top_i[:, :, 0, :, None] * PEER_NKEYS + top_i[:, :, 1, None, :]
    best_s, pos = lax.top_k(cand_s.reshape(n, PEER_HEADS, PEER_TOPK * PEER_TOPK), PEER_TOPK)
    experts = jnp.take_along_axis(cand_i.reshape(n, PEER_HEADS, PEER_TOPK * PEER_TOPK), pos, axis=-1)
    gate = jax.nn.softmax(best_s, axis=-1).astype(x.dtype)
    experts = experts.reshape(n, PEER_HEADS * PEER_TOPK)
    gate = gate.reshape(n, PEER_HEADS * PEER_TOPK)
    blk = min(PEER_BLOCK, n)
    nb = -(-n // blk)
    pad = nb * blk - n
    xb = jnp.pad(xf, ((0, pad), (0, 0))).reshape(nb, blk, D_MODEL)
    eb = jnp.pad(experts, ((0, pad), (0, 0))).reshape(nb, blk, -1)
    gb = jnp.pad(gate, ((0, pad), (0, 0))).reshape(nb, blk, -1)

    def one(args):
        xi, ei, gi = args
        hi = jax.nn.gelu(jnp.einsum('bed,bd->be', jnp.take(u_tab, ei, axis=0), xi))
        return jnp.einsum('be,bed->bd', gi * hi, jnp.take(v_tab, ei, axis=0))

    y = lax.map(one, (xb, eb, gb))
    return y.reshape(nb * blk, D_MODEL)[:n].reshape(shp)

def setup_inputs(seed: int = 0) -> dict:
    key = jax.random.key(seed)
    ks = jax.random.split(key, 32)
    nrm = lambda k, shp: jax.random.normal(k, shp, jnp.float32)
    n_pages = PAST_LEN // PAGE_SIZE
    n_used = DEC_BATCH * n_pages
    n_phys = n_used + max(1, n_used // 4)
    page_table = jax.random.permutation(ks[0], n_phys)[:n_used].reshape(DEC_BATCH, n_pages).astype(jnp.int32)
    x_prompt = nrm(ks[1], (BATCH, SEQ, D_MODEL))
    x_sample = nrm(ks[2], (DEC_BATCH, DEC_SEQ, D_MODEL))
    cache_k = nrm(ks[3], (n_phys, N_AB, PAGE_SIZE, N_HEADS_B, HEAD_DIM_B))
    cache_v = DN_BETA * nrm(ks[4], (n_phys, N_AB, PAGE_SIZE, N_HEADS_B, HEAD_DIM_B))
    cache_logf = jax.nn.log_sigmoid(FORGET_BIAS_INIT + nrm(ks[5], (n_phys, N_AB, PAGE_SIZE, N_HEADS_B)))
    state_conv = DN_BETA * nrm(ks[6], (DEC_BATCH, N_AB, CONV_W - 1, D_CONV))
    col_scale = np.concatenate([
        np.full(D_CONV, 1.0), np.full(D_CONV, 1.0), np.full(D_CONV, DN_BETA),
        np.full(D_ATT, 1.0), np.full(D_ATT, 1.0), np.full(D_ATT, DN_BETA),
        np.full(N_HEADS_B, 1.0)]) * D_MODEL ** -0.5
    w_in_ab = nrm(ks[7], (N_AB, D_MODEL, D_IN_AB)) * jnp.asarray(col_scale, jnp.float32)
    b_f = FORGET_BIAS_INIT + 0.1 * nrm(ks[8], (N_AB, N_HEADS_B))
    conv_w = nrm(ks[9], (N_AB, CONV_W, D_CONV)) * CONV_W ** -0.5
    w_o_ab = nrm(ks[10], (N_AB, D_CONV + D_ATT, D_MODEL)) * (D_CONV + D_ATT) ** -0.5 * DN_BETA
    w_in_c = nrm(ks[11], (N_C, D_MODEL, 2 * D_SG)) * D_MODEL ** -0.5
    sg_ln_g = 1.0 + 0.02 * nrm(ks[12], (N_C, D_SG))
    sg_ln_b = 0.02 * nrm(ks[13], (N_C, D_SG))
    w_s = nrm(ks[14], (N_C, SG_GROUPS, CHUNK, CHUNK)) * 0.5 * CHUNK ** -0.5
    b_s = 1.0 + 0.02 * nrm(ks[15], (N_C, SG_GROUPS, CHUNK))
    w_o_c = nrm(ks[16], (N_C, D_SG, D_MODEL)) * D_SG ** -0.5 * DN_BETA
    ln1_g = 1.0 + 0.02 * nrm(ks[17], (DEPTH, D_MODEL))
    ln1_b = 0.02 * nrm(ks[18], (DEPTH, D_MODEL))
    ln2_g = 1.0 + 0.02 * nrm(ks[19], (DEPTH, D_MODEL))
    ln2_b = 0.02 * nrm(ks[20], (DEPTH, D_MODEL))
    peer_wq = nrm(ks[21], (DEPTH, D_MODEL, PEER_HEADS * PEER_DK)) * D_MODEL ** -0.5
    peer_keys = nrm(ks[22], (DEPTH, PEER_HEADS, 2, PEER_NKEYS, PEER_DK // 2)) * (PEER_DK // 2) ** -0.5
    peer_u = nrm(ks[23], (DEPTH, PEER_N, D_MODEL)) * D_MODEL ** -0.5
    peer_v = nrm(ks[24], (DEPTH, PEER_N, D_MODEL)) * DN_BETA * PEER_HEADS ** -0.5
    return {"x_prompt": x_prompt, "x_sample": x_sample, "cache_k": cache_k, "cache_v": cache_v,
            "cache_logf": cache_logf, "state_conv": state_conv, "page_table": page_table,
            "w_in_ab": w_in_ab, "b_f": b_f, "conv_w": conv_w, "w_o_ab": w_o_ab,
            "w_in_c": w_in_c, "sg_ln_g": sg_ln_g, "sg_ln_b": sg_ln_b, "w_s": w_s, "b_s": b_s,
            "w_o_c": w_o_c, "ln1_g": ln1_g, "ln1_b": ln1_b, "ln2_g": ln2_g, "ln2_b": ln2_b,
            "peer_wq": peer_wq, "peer_keys": peer_keys, "peer_u": peer_u, "peer_v": peer_v}

def reference(x_prompt, x_sample, cache_k, cache_v, cache_logf, state_conv, page_table,
              w_in_ab, b_f, conv_w, w_o_ab, w_in_c, sg_ln_g, sg_ln_b, w_s, b_s, w_o_c,
              ln1_g, ln1_b, ln2_g, ln2_b, peer_wq, peer_keys, peer_u, peer_v):
    n_dec = x_sample.shape[0]
    p_len = page_table.shape[1] * PAGE_SIZE
    xp, xs = x_prompt, x_sample
    kp_l, vp_l, fp_l, cp_l = [], [], [], []
    ks_l, vs_l, fs_l, cs_l = [], [], [], []
    sv_l = []
    for l in range(DEPTH):
        i = l // 2
        if l % 2 == 0:
            mp, kp, vp, fp, cp = _ab_mixer(xp, w_in_ab[i], b_f[i], conv_w[i], w_o_ab[i], None, None)
            past = (cache_k[page_table, i].reshape(n_dec, p_len, N_HEADS_B, HEAD_DIM_B),
                    cache_v[page_table, i].reshape(n_dec, p_len, N_HEADS_B, HEAD_DIM_B),
                    cache_logf[page_table, i].reshape(n_dec, p_len, N_HEADS_B))
            ms, ks, vs, fs, cs = _ab_mixer(xs, w_in_ab[i], b_f[i], conv_w[i], w_o_ab[i], state_conv[:, i], past)
            kp_l.append(kp); vp_l.append(vp); fp_l.append(fp); cp_l.append(cp)
            ks_l.append(ks); vs_l.append(vs); fs_l.append(fs); cs_l.append(cs)
        else:
            mp, _ = _chunk_mixer(xp, w_in_c[i], sg_ln_g[i], sg_ln_b[i], w_s[i], b_s[i], w_o_c[i])
            ms, sv = _chunk_mixer(xs, w_in_c[i], sg_ln_g[i], sg_ln_b[i], w_s[i], b_s[i], w_o_c[i])
            sv_l.append(sv)
        xp = _layer_norm(DN_ALPHA * xp + mp, ln1_g[l], ln1_b[l])
        xs = _layer_norm(DN_ALPHA * xs + ms, ln1_g[l], ln1_b[l])
        xp = _layer_norm(DN_ALPHA * xp + _peer(xp, peer_wq[l], peer_keys[l], peer_u[l], peer_v[l]), ln2_g[l], ln2_b[l])
        xs = _layer_norm(DN_ALPHA * xs + _peer(xs, peer_wq[l], peer_keys[l], peer_u[l], peer_v[l]), ln2_g[l], ln2_b[l])
    new_k_prompt = jnp.stack(kp_l, axis=1)
    new_v_prompt = jnp.stack(vp_l, axis=1)
    new_logf_prompt = jnp.stack(fp_l, axis=1)
    new_k_sample = jnp.stack(ks_l, axis=1)
    new_v_sample = jnp.stack(vs_l, axis=1)
    new_logf_sample = jnp.stack(fs_l, axis=1)
    new_conv_prompt = jnp.stack(cp_l, axis=1)
    new_conv_sample = jnp.stack(cs_l, axis=1)
    new_sgv_sample = jnp.stack(sv_l, axis=1)
    return (xp, xs, new_k_prompt, new_v_prompt, new_logf_prompt, new_k_sample, new_v_sample,
            new_logf_sample, new_conv_prompt, new_conv_sample, new_sgv_sample)


_drawn_inputs = setup_inputs


def setup_inputs(seed=0):
    import zlib

    import numpy as np

    out = dict(_drawn_inputs(seed))
    spreads = {}
    factors = {'cache_logf': 17.81, 'sg_ln_g': 8.664, 'sg_ln_b': 8.091, 'b_s': 24.814}
    for name, (base, spread) in spreads.items():
        noise = np.random.default_rng([zlib.crc32(name.encode()), seed]).standard_normal(out[name].shape)
        drawn = base * np.exp(spread * noise) if base else spread * noise
        out[name] = __import__('jax').numpy.asarray(drawn.astype(out[name].dtype))
    for name, factor in factors.items():
        out[name] = (out[name] * factor).astype(out[name].dtype)
    return out
```

```python
from contextlib import ExitStack

import numpy as np

import concourse.bass as bass
from concourse import mybir

F32 = mybir.dt.float32
F32R = mybir.dt.float32r
U32 = mybir.dt.uint32
I32 = mybir.dt.int32
ALU = mybir.AluOpType
ACT = mybir.ActivationFunctionType
AX = mybir.AxisListType.X

P = 128
D_MODEL = 1024
KB = D_MODEL // P
SEQ = 512
DEC = 8
N = SEQ + DEC
HALF = N // 2
DEPTH = 2
ALPHA = (2.0 * DEPTH) ** 0.25
EPS = 1e-5
HEADS = 8
HD = 64
AB = 4
QT = SEQ // P
PAGES = 8
PAGE = 128
NPAIR = HEADS * 2
TOPK = 16
HJ = HEADS * TOPK
TT = 104
NT = N // TT
GH = 52
SUB = 4
GROUP = 4
NG = 128 // GROUP
NEG = -3.0e38
SCALE = HD ** -0.5

N_AB, N_WO, N_WQ, N_U, N_INC = 24, 8, 16, 128, 16
C_AB = 0
C_WO0 = C_AB + N_AB
C_WQ = [C_WO0 + N_WO, 0]
C_U = [C_WQ[0] + N_WQ, 0]
C_INC = C_U[0] + N_U
C_WOC = C_INC + N_INC
C_WQ[1] = C_WOC + N_WO
C_U[1] = C_WQ[1] + N_WQ
C_END = C_U[1] + N_U

IDENT, ONES, TRI, CMASK, IOTA, UTRI, MEAN, SELP, SELH = 0, 128, 256, 384, 512, 640, 768, 896, 1152
N_CST = SELH + HEADS * P
V_LN = 0
V_SG = 64
V_W00 = 80
V_B00 = 88
V_CONV = 96
V_BF = 108
N_VEC = 112


class Steps:

    def __init__(self, engine, sem, count=0):
        self.engine, self.sem, self.count, self.marked = engine, sem, count, 0

    def mark(self, instruction):
        instruction.then_inc(self.sem, 1)
        self.count = self.count + 1
        self.marked += 1

    def settle(self):
        self.engine.wait_ge(self.sem, self.count)


def spread(ap, axis, shape):
    return ap.unsqueeze(axis).to_broadcast(list(shape))


def halves(ap):
    return ap.rearrange("p (h n) -> p h n", h=2)


def trunk(nc, i, o, upto=99):
    with ExitStack() as ctx:
        used = [nc.sbuf_base + (-nc.sbuf_base) % 64]

        def place(name, shape, dtype, at=None):
            n = int(np.prod(shape[1:])) * 4
            if at is None:
                at = used[0]
                used[0] += (n + 31) // 32 * 32
            return nc.alloc_sbuf_tensor_at(name, list(shape), dtype, offset=at)

        cst = place("cst", [P, N_CST], F32)
        vec = place("vec", [P, N_VEC], F32)
        at_xt = used[0]
        xt = place("xt", [P, KB, N], F32)
        at_xh = used[0]
        xh = place("xh", [P, KB, N], F32R)
        xl = place("xl", [P, KB, N], F32R)
        res = place("res", [P, KB, N], F32)
        wraw = place("wraw", [P, 2, KB * P], F32)
        whi = place("whi", [P, 2, KB * P], F32R)
        wlo = place("wlo", [P, 2, KB * P], F32R)
        at_ln = used[0]
        used[0] += 8320
        rstd = place("rstd", [P, N], F32, at_ln)
        sq = place("sq", [P, 2, N], F32, at_ln + 4 * N)
        phase = used[0]

        kv = place("kv", [P, 2, PAGES * 512], F32, at_xh)
        proj = place("proj", [P, N_AB, N], F32)
        zp = place("zp", [P, AB, SEQ + 2], F32)
        zs = place("zs", [P, AB, DEC, 3], F32)
        wf = place("wf", [P, KB, HEADS], F32)
        lf = place("lf", [HEADS, N], F32)
        lt = place("lt", [HEADS, 2, N], F32)
        ncum = place("ncum", [HEADS, SEQ], F32)
        vn = place("vn", [P, QT, 512], F32)
        nb = place("nb", [P, 2, SEQ], F32)
        sc = place("sc", [P, 2, SEQ], F32)
        pr = place("pr", [P, 2, SEQ], F32)
        pt = place("pt", [P, 2, SEQ], F32)
        st = place("st", [P, 2, 4], F32)
        t1 = place("t1", [P, SEQ], F32)
        t2 = place("t2", [P, DEC], F32)
        pg = place("pg", [1, DEC * PAGES], I32)
        qd = place("qd", [P, DEC, AB, 2], F32)
        prd = place("prd", [P, DEC, AB], F32)
        lfc = place("lfc", [P, DEC, PAGES, HEADS], F32)
        later = place("later", [P, DEC, PAGES, HEADS], F32)
        ss = place("ss", [P, DEC, PAGES, HEADS], F32)
        sm = place("sm", [P, 8, DEC * HEADS], F32)
        t3 = place("t3", [P, AB, DEC], F32)
        assert used[0] <= nc.sbuf_usable_end, used[0]
        used[0] = phase
        scores = place("scores", [P, NPAIR, P], F32, at_xt)
        scores2 = place("scores2", [P, NPAIR, P], F32, at_xt + 8192)
        eq = place("eq", [P, HJ, TOPK], F32, at_ln)
        q_t = place("q_t", [P, NPAIR, N], F32)
        keys = place("keys", [P, NPAIR, P], F32)
        tv = place("tv", [P, NPAIR, TOPK], F32)
        ti = place("ti", [P, NPAIR, TOPK], U32)
        tif = place("tif", [P, NPAIR, TOPK], F32)
        bv = place("bv", [P, HEADS, TOPK], F32)
        bp = place("bp", [P, HJ], U32)
        bu = place("bu", [P, 2, HJ], U32)
        bf = place("bf", [P, 2, HJ], F32)
        pick = place("pick", [P, 3, HJ], F32)
        gs = place("gs", [P, 2, HEADS], F32)
        pickt = place("pickt", [P, 3, TT], F32)
        oh1 = place("oh1", [P, 2, SUB, P], F32)
        oh2 = place("oh2", [P, 2, SUB, P], F32)
        gst = place("gst", [P, P, GH], F32)
        assert used[0] <= nc.sbuf_usable_end, used[0]
        used[0] = phase
        vraw = place("vraw", [P, 4, GROUP * P], F32)
        vhi = place("vhi", [P, 4, GROUP * P], F32R)
        vlo = place("vlo", [P, 4, GROUP * P], F32R)
        wth = place("wth", [P, 2, GROUP, N], F32R)
        wtl = place("wtl", [P, 2, GROUP, N], F32R)
        gc = place("gc", [P, GROUP, N], F32)
        hid = place("hid", [P, 2, N], F32)
        wt = place("wt", [P, 2, N], F32)
        assert used[0] <= nc.sbuf_usable_end, used[0]
        used[0] = phase
        uv = place("uv", [P, 2 * KB, N], F32)
        vnt = place("vnt", [P, 2, QT * P], F32)
        ws = place("ws", [P, KB, P], F32)
        bs = place("bs", [P, KB, P], F32)
        sp = place("sp", [P, 2, SEQ], F32)
        sps = place("sps", [P, KB, DEC], F32)
        assert used[0] <= nc.sbuf_usable_end, used[0]

        gates = [nc.dram_tensor(f"gates{n}", (P, P, N), F32, kind="Internal").ap() for n in range(DEPTH)]

        pstr = ctx.enter_context(nc.psum_tensor("pstr", [P, 2, 2, 512], F32))
        aux = ctx.enter_context(nc.psum_tensor("aux", [P, 4, 512], F32))

        def sem(name):
            return ctx.enter_context(nc.semaphore(name))

        setup_in = sem("setup_in")
        pages_in = sem("pages_in")
        state_in = sem("state_in")
        logf_in = sem("logf_in")
        w_in = [sem(f"w_in{n}") for n in range(2)]
        kv_in = [sem(f"kv_in{n}") for n in range(2)]
        v_in = [sem(f"v_in{n}") for n in range(4)]
        g_in = [sem(f"g_in{n}") for n in range(4)]
        keys_in = sem("keys_in")
        sgu_in = sem("sgu_in")
        out_done = sem("out_done")
        gates_out = sem("gates_out")
        y_out = sem("y_out")
        w_hi = sem("w_hi")
        w_lo = sem("w_lo")
        chunk_done = sem("chunk_done")
        chunk_taken = sem("chunk_taken")
        x_hi = sem("x_hi")
        x_lo = sem("x_lo")
        ln_mean = sem("ln_mean")
        ln_centred = sem("ln_centred")
        ln_sq = sem("ln_sq")
        ln_var = sem("ln_var")
        ln_eps = sem("ln_eps")
        ln_root = sem("ln_root")
        ln_rstd = sem("ln_rstd")
        ln_normed = sem("ln_normed")
        ln_out = sem("ln_out")
        f_done = sem("f_done")
        f_abs = sem("f_abs")
        f_exp = sem("f_exp")
        f_ln = sem("f_ln")
        f_logf = sem("f_logf")
        f_ncum = sem("f_ncum")
        conv_done = sem("conv_done")
        z_done = sem("z_done")
        vt_done = sem("vt_done")
        vn_ready = sem("vn_ready")
        nb_done = sem("nb_done")
        nb_ready = sem("nb_ready")
        qk_done = sem("qk_done")
        s_taken = sem("s_taken")
        max_ready = sem("max_ready")
        exp_done = sem("exp_done")
        p_ready = sem("p_ready")
        pt_done = sem("pt_done")
        pt_ready = sem("pt_ready")
        pv_done = sem("pv_done")
        o_taken = sem("o_taken")
        smp_in = sem("smp_in")
        smp_pe = sem("smp_pe")
        smp_act = sem("smp_act")
        kv_used = sem("kv_used")
        cat_ready = sem("cat_ready")
        sc_done = sem("sc_done")
        sc_taken = sem("sc_taken")
        gate_shift = sem("gate_shift")
        gate_exp = sem("gate_exp")
        pick_ready = sem("pick_ready")
        pick_done = sem("pick_done")
        pick_taken = sem("pick_taken")
        oh_hot = sem("oh_hot")
        oh_ready = sem("oh_ready")
        gate_done = sem("gate_done")
        gate_taken = sem("gate_taken")
        g_used = sem("g_used")
        wt_hi = sem("wt_hi")
        wt_lo = sem("wt_lo")
        v_hi = sem("v_hi")
        v_lo = sem("v_lo")
        v_done = sem("v_done")
        v_taken = sem("v_taken")
        ws_masked = sem("ws_masked")
        st_done = sem("st_done")
        st_ready = sem("st_ready")
        sg_done = sem("sg_done")
        sg_taken = sem("sg_taken")
        mix_ready = sem("mix_ready")
        dve_step = sem("dve_step")
        topk_step = sem("topk_step")

        def c(at, n=P, rows=P):
            return cst[0:rows, at:at + n]

        def run_periods(e, layer, prep_u, prep_v, hidden, finish_wt, take_v):
            last = layer == DEPTH - 1 or upto < 3

            def period(g, par, do_h, do_v, then):
                steps = [("u", j) for j in range(GROUP) if do_h] + [("v", v) for v in range(8) if do_v]
                ahead = steps[2:] + then
                for n, (kind, j) in enumerate(steps):
                    nxt = ahead[n] if n < len(ahead) else None
                    if kind == "u":
                        hidden(g + 1, j)
                        if j:
                            finish_wt(g + 1, j - 1, 1 - par)
                    else:
                        take_v(g, j)
                    if nxt is not None:
                        if nxt[0] == "u":
                            prep_u(g + 1, nxt[1])
                        elif nxt[0] == "v":
                            prep_v(g, nxt[1])
                        elif nxt[0] == "u+":
                            prep_u(g + 2, nxt[1])
                        elif nxt[0] == "v+":
                            prep_v(g + 1, nxt[1])
                    if kind == "u" and j == GROUP - 1:
                        finish_wt(g + 1, j, 1 - par)

            nxt_u = [("u+", 0), ("u+", 1)]
            period(-1, 1, True, False, nxt_u)
            period(0, 0, True, True, nxt_u)
            with e.Fori(0, NG // 2 - 2) as q:
                period(q * 2 + 1, 1, True, True, nxt_u)
                period(q * 2 + 2, 0, True, True, nxt_u)
            period(NG - 3, 1, True, True, nxt_u)
            period(NG - 2, 0, True, True, [("v+", 0), ("v+", 1)])
            period(NG - 1, 1, False, True, [] if last else [("u", 0), ("u", 1)])


        block = ctx.enter_context(nc.Block())

        @block.sync
        def _(e):
            for dst, src in ((cst[:], i["cst"]), (vec[:], i["vec"]), (xt[:], i["xt"]), (wf[:], i["wf"])):
                e.dma_start(dst, src).then_inc(setup_in, 16)

            def load_chunk(pair, slot, src):
                if not (isinstance(pair, int) and pair == 0):
                    e.wait_ge(w_lo, 2 * pair + slot - 1)
                e.dma_start(wraw[:, slot, :], src.rearrange("a p k c -> p (a k c)")).then_inc(w_in[slot], 16)

            def load_stage(first, count, table, row0, peel=0):
                for slot in range(2 * peel):
                    load_chunk(first // 2, slot, table[row0 + slot:row0 + slot + 1])
                with e.Fori(peel, count // 2) as p:
                    for slot in range(2):
                        load_chunk(p + first // 2, slot, table[bass.ds(p * 2 + (row0 + slot), 1)])

            def load_v(layer, g, v):
                at = g * 8 + (layer * NG * 8 + v)
                if v >= 4 or layer or not isinstance(g, int) or g > 0:
                    e.wait_ge(v_lo, at - 3)
                e.dma_start(vraw[:, v % 4, :], i["v"][bass.ds(at, 1)].rearrange("a p c -> p (a c)")).then_inc(v_in[v % 4], 16)

            def load_u(layer, g, j):
                load_chunk(g * 2 + (C_U[layer] // 2 + j // 2), j % 2, i["u"][bass.ds(g * GROUP + (layer * P + j), 1)])

            def peer_tables(layer):
                for j in range(GROUP):
                    load_u(layer, 0, j)
                subs = GH // SUB
                with e.Fori(0, NT * 2) as half:
                    e.wait_ge(gate_taken, half * subs + (layer * NT * 2 * subs + subs))
                    e.dma_start(gates[layer][:, :, bass.ds(half * GH, GH)].rearrange("a b n -> b a n"), gst[:]).then_inc(gates_out, 16)
                e.wait_ge(gates_out, 16 * 2 * NT * (layer + 1))
                def period(g, more):
                    if more:
                        for j in range(GROUP):
                            load_u(layer, g + 1, j)
                    for v in range(8):
                        load_v(layer, g, v)
                period(0, True)
                with e.Fori(1, NG - 1) as g:
                    period(g, True)
                period(NG - 1, False)

            load_stage(C_AB, N_AB, i["w"], 0, peel=1)
            load_stage(C_WO0, N_WO, i["w"], 24)
            load_stage(C_WQ[0], N_WQ, i["w"], 32)
            if upto >= 1:
                peer_tables(0)
            if upto >= 3:
                load_stage(C_INC, N_INC, i["w"], 48)
                load_stage(C_WOC, N_WO, i["w"], 64)
                load_stage(C_WQ[1], N_WQ, i["w"], 72)
                peer_tables(1)
                for k in range(KB):
                    e.wait_ge(ln_out, 8 * 4 + k + 1)
                    e.dma_start(o["y"][:, k, :], xt[:, k, :]).then_inc(y_out, 16)
                e.wait_ge(y_out, 16 * KB)

        @block.gpsimd
        def _(e):
            e.dma_start(pg[:], i["pt"]).then_inc(pages_in, 16)
            e.dma_start(zs[:, :, :, 0:2], i["state"]).then_inc(state_in, 16)
            e.wait_ge(pages_in, 16)
            with e.Fori(0, DEC) as b:
                for g in range(PAGES):
                    r = e.value_load(pg[0:1, bass.ds(b * PAGES + g, 1)], min_val=0, max_val=i["clf"].shape[0] - 1)
                    e.dma_start(lfc[:, bass.ds(b, 1), g, :], i["clf"][bass.ds(r, 1)].rearrange("a p h -> p a h")).then_inc(logf_in, 16)
            e.wait_ge(chunk_done, C_WO0)

            def load_pages(b, slot, table, wait):
                if wait is not None:
                    e.wait_ge(kv_used, wait)
                for g in range(PAGES):
                    r = e.value_load(pg[0:1, bass.ds(b * PAGES + g, 1)], min_val=0, max_val=table.shape[0] - 1)
                    e.dma_start(kv[:, slot, g * 512:(g + 1) * 512], table[bass.ds(r, 1)].rearrange("a p c -> p (a c)")).then_inc(kv_in[slot], 16)

            for b in range(2):
                load_pages(b, b, i["ck"], None)
            with e.Fori(1, DEC // 2) as bp_:
                for s in range(2):
                    load_pages(bp_ * 2 + s, s, i["ck"], bp_ * 2 + (s - 1))
            with e.Fori(0, DEC // 2) as bp_:
                for s in range(2):
                    load_pages(bp_ * 2 + s, s, i["cv"], bp_ * 2 + (DEC + s - 1))
            e.wait_ge(chunk_taken, C_WO0)
            e.dma_start(o["k"], proj[:, 16:20, :]).then_inc(out_done, 16)
            e.dma_start(o["v"], proj[:, 20:24, :]).then_inc(out_done, 16)
            e.wait_ge(f_logf, 1)
            e.dma_start(o["lf"], lf[:]).then_inc(out_done, 16)
            e.wait_ge(z_done, 2 * AB)
            e.wait_ge(state_in, 16)
            e.dma_start(o["cp"], zp[:, :, SEQ:SEQ + 2]).then_inc(out_done, 16)
            e.dma_start(o["cs"], zs[:, :, :, 1:3]).then_inc(out_done, 16)
            e.wait_ge(out_done, 16 * 5)

            def peer(layer):
                e.wait_ge(chunk_done, C_WQ[layer])
                e.dma_start(keys[:], i["keys"][layer]).then_inc(keys_in, 16)
                e.wait_ge(gates_out, 16 * 2 * NT * (layer + 1))
                for j in range(GROUP):
                    load_g(layer, 0, j)
                with e.Fori(1, NG) as g:
                    for j in range(GROUP):
                        load_g(layer, g, j)

            def load_g(layer, g, j):
                at = g * GROUP + (layer * P + j)
                if not (isinstance(g, int) and layer == 0):
                    e.wait_ge(g_used, at - 3)
                e.dma_start(gc[:, j, :], gates[layer][bass.ds(g * GROUP + j, 1)].rearrange("a p n -> p (a n)")).then_inc(g_in[j], 16)

            if upto >= 1:
                peer(0)
            if upto >= 3:
                e.wait_ge(v_taken, NG * 8)
                e.dma_start(ws[:], i["ws"]).then_inc(sgu_in, 16)
                e.dma_start(bs[:], i["bs"]).then_inc(sgu_in, 16)
                e.wait_ge(ln_out, 8 * 3)
                e.dma_start(o["sgv"], uv[:, KB:2 * KB, SEQ:N]).then_inc(out_done, 16)
                e.wait_ge(out_done, 16 * 6)
                peer(1)

        @block.scalar
        def _(e):
            def round_chunk(pair, slot):
                e.wait_ge(w_in[slot], 16 * pair + 16)
                if not (isinstance(pair, int) and pair == 0):
                    e.wait_ge(chunk_done, 2 * pair + (slot - 1))
                e.activation(whi[:, slot, :], wraw[:, slot, :], ACT.Copy).then_inc(w_hi, 1)

            def take_stage(first, count, dst, func, col):
                with e.Fori(0, count // 2) as p:
                    for slot in range(2):
                        e.wait_ge(chunk_done, 2 * p + (first + slot + 1))
                        out = dst[:, bass.ds(p * 2 + (col + slot), 1), :].rearrange("p a (h n) -> p (a h) n", h=2)
                        e.activation(out, pstr[:, slot, :, 0:HALF], func).then_inc(chunk_taken, 1)
                        round_chunk(p + (first // 2 + 1), slot)

            def round_stage(first, count):
                with e.Fori(0, count // 2) as p:
                    for slot in range(2):
                        round_chunk(p + (first // 2 + 1), slot)

            def round_x(src, ready):
                for k in range(KB):
                    ready(k)
                    e.activation(xh[:, k, :], src[:, k, :], ACT.Copy).then_inc(x_hi, 1)

            def norm(n, src, gcol, bcol, dst):
                for k in range(KB):
                    e.wait_ge(ln_centred, 8 * n + k + 1)
                    if k >= 2:
                        e.wait_ge(ln_var, 8 * n + k - 1)
                    e.activation(sq[:, k % 2, :], src[:, k, :], ACT.Square).then_inc(ln_sq, 1)
                e.wait_ge(ln_eps, n + 1)
                e.activation(rstd[:], rstd[:], ACT.Sqrt).then_inc(ln_root, 1)
                for k in range(KB):
                    e.wait_ge(ln_normed, 8 * n + k + 1)
                    e.activation(dst[:, k, :], src[:, k, :], ACT.Identity, bias=vec[:, bcol + k:bcol + k + 1],
                                 scale=vec[:, gcol + k:gcol + k + 1]).then_inc(ln_out, 1)

            e.wait_ge(setup_in, 64)
            round_x(xt, lambda k: None)
            round_chunk(0, 0)
            round_chunk(0, 1)
            take_stage(C_AB, N_AB, proj, ACT.Copy, 0)

            e.wait_ge(f_abs, 1)
            e.activation(lt[:, 0, :], lt[:, 0, :], ACT.Abs).then_inc(f_exp, 1)
            e.wait_ge(f_exp, 1)
            e.activation(lt[:, 0, :], lt[:, 0, :], ACT.Exp, scale=-1.0).then_inc(f_exp, 1)
            e.wait_ge(f_exp, 2)
            e.activation(lt[:, 0, :], lt[:, 0, :], ACT.Ln, bias=1.0).then_inc(f_ln, 1)

            for t in range(QT):
                e.wait_ge(vt_done, t + 1)
                e.activation(vn[:, t, :], pstr[:, t // 2, t % 2, :], ACT.Copy).then_inc(vn_ready, 1)

            def take_nb(h):
                e.wait_ge(nb_done, h + 1)
                if h >= 2:
                    e.wait_ge(s_taken, QT * (h - 1))
                e.activation(nb[:, h % 2, :], pstr[:, 1, 0, :], ACT.Copy).then_inc(nb_ready, 1)

            def exp_unit(u):
                w = (u % QT + 1) * P
                e.wait_ge(max_ready, u + 1)
                if u >= 2:
                    e.wait_ge(pt_done, u - 1)
                e.activation(pr[:, u % 2, 0:w], sc[:, u % 2, 0:w], ACT.Exp, bias=st[:, u % 2, 0:1],
                             accum_out=st[:, u % 2, 1:2]).then_inc(exp_done, 1)

            def take_pt(u):
                w = (u % QT + 1) * P
                e.wait_ge(pt_done, u + 1)
                if u >= 2:
                    e.wait_ge(pv_done, u - 1)
                e.activation(pt[:, u % 2, 0:w], aux[:, 2 + u % 2, 0:w], ACT.Copy).then_inc(pt_ready, 1)

            def take_o(u):
                h, q = divmod(u, QT)
                rows = slice(HD * (h % 2), HD * (h % 2) + HD)
                e.wait_ge(pv_done, u + 1)
                e.activation(proj[rows, AB + h // 2, q * P:(q + 1) * P], pstr[rows, 0, u % 2, 0:P],
                             ACT.Copy).then_inc(o_taken, 1)

            units = HEADS * QT
            take_nb(0)
            exp_unit(0)
            for u in range(units):
                if (u + 2) % QT == 0 and (u + 2) // QT < HEADS:
                    take_nb((u + 2) // QT)
                if u + 1 < units:
                    exp_unit(u + 1)
                if u >= 1:
                    take_o(u - 1)
                take_pt(u)
            take_o(units - 1)

            e.wait_ge(smp_in, 5)
            e.activation(ss[:], ss[:], ACT.Exp).then_inc(smp_act, 1)
            e.activation(sm[:, 0, :], sm[:, 0, :], ACT.Exp).then_inc(smp_act, 1)

            e.wait_ge(kv_used, 2 * DEC)
            e.wait_ge(cat_ready, 2)
            round_x(proj, lambda k: None)
            round_stage(C_WO0, N_WO)
            norm(0, res, V_LN, V_LN + 8, xt)
            def own_ln(n):
                return lambda k: e.wait_ge(ln_out, 8 * n + k + 1)
            round_x(xt, own_ln(0))

            def peer(layer):
                e.wait_ge(out_done, 16 * (5 + layer))
                take_stage(C_WQ[layer], N_WQ, q_t, ACT.Copy, 0)
                subs = GH // SUB
                for t in range(NT):
                    tt = t + layer * NT
                    e.wait_ge(sc_done, tt + 1)
                    e.activation(scores[0:TT, :, :].rearrange("p (b c) k -> p b (c k)", b=4),
                                 pstr[0:TT].rearrange("p a b n -> p (a b) n"), ACT.Copy).then_inc(sc_taken, 1)
                    e.wait_ge(gate_shift, tt + 1)
                    e.activation(bv[0:TT, :, :], bv[0:TT, :, :], ACT.Exp).then_inc(gate_exp, 1)
                    e.wait_ge(pick_done, tt + 1)
                    e.activation(pickt[:].rearrange("p a n -> p (a n)"), aux[:, 3, 0:3 * TT], ACT.Copy).then_inc(pick_taken, 1)
                    for n in range(2 * subs):
                        if n % subs == 0 and tt + n > 0:
                            e.wait_ge(gates_out, tt * 32 + 16 * (n // subs))
                        e.wait_ge(gate_done, tt * (2 * subs) + (n + 1))
                        e.activation(gst[:, :, n % subs * SUB:(n % subs + 1) * SUB].rearrange("p a n -> p n a"),
                                     aux[:, n % 2, :].rearrange("p (n a) -> p n a", n=SUB), ACT.Copy).then_inc(gate_taken, 1)
                e.wait_ge(gates_out, 32 * NT * (layer + 1))

                def round_v(g, v):
                    at = g * 8 + (layer * NG * 8 + v)
                    e.wait_ge(v_in[v % 4], g * 32 + 16 * (layer * NG * 2 + v // 4 + 1))
                    if v >= 4 or layer or not isinstance(g, int) or g > 0:
                        e.wait_ge(v_done, at - 3)
                    e.activation(vhi[:, v % 4, :], vraw[:, v % 4, :], ACT.Copy).then_inc(v_hi, 1)

                def round_u(g, j):
                    round_chunk(g * 2 + (C_U[layer] // 2 + j // 2), j % 2)

                def hidden(g, j):
                    at = g * GROUP + (layer * P + j)
                    e.wait_ge(chunk_done, g * GROUP + (C_U[layer] + j + 1))
                    if not (isinstance(g, int) and g == 0 and j < 2 and layer == 0):
                        e.wait_ge(g_used, at - 1)
                    e.activation(halves(hid[:, j % 2, :]), pstr[:, j % 2, :, 0:HALF], ACT.Gelu_apprx_tanh).then_inc(chunk_taken, 1)

                def round_wt(g, j, par):
                    e.wait_ge(g_used, g * GROUP + (layer * P + j + 1))
                    e.activation(wth[:, par, j, :], wt[:, j % 2, :], ACT.Copy).then_inc(wt_hi, 1)

                run_periods(e, layer, round_u, round_v, hidden, round_wt, lambda g, v: None)

            if upto >= 1:
                peer(0)
            if upto >= 3:
                norm(1, res, V_LN + 16, V_LN + 24, xt)
                round_x(xt, own_ln(1))
                take_stage(C_INC, N_INC, uv, ACT.Gelu_apprx_tanh, 0)
                norm(2, uv[:, KB:2 * KB, :], V_SG, V_SG + 8, uv[:, KB:2 * KB, :])
                for g in range(KB):
                    e.wait_ge(st_done, g + 1)
                    if g >= 2:
                        e.wait_ge(sg_done, g - 1)
                    e.activation(vnt[:, g % 2, :], aux[:, g % 2, :], ACT.Copy).then_inc(st_ready, 1)
                e.wait_ge(mix_ready, 2 * KB)
                round_x(uv, lambda k: None)
                round_stage(C_WOC, N_WO)
                norm(3, res, V_LN + 32, V_LN + 40, xt)
                round_x(xt, own_ln(3))
                peer(1)
                norm(4, res, V_LN + 48, V_LN + 56, xt)

        @block.vector
        def _(e):
            own = Steps(e, dve_step)

            def split_chunk(pair, slot):
                e.wait_ge(w_hi, 2 * pair + (slot + 1))
                e.tensor_tensor(wlo[:, slot, :], wraw[:, slot, :], whi[:, slot, :].bitcast(F32), ALU.subtract).then_inc(w_lo, 1)

            def split_stage(first, count):
                with e.Fori(0, count // 2) as p:
                    for slot in range(2):
                        split_chunk(p + (first // 2 + 1), slot)

            def split_x(n, src, residual):
                for k in range(KB):
                    e.wait_ge(x_hi, 8 * n + k + 1)
                    e.tensor_tensor(xl[:, k, :], src[:, k, :], xh[:, k, :].bitcast(F32), ALU.subtract).then_inc(x_lo, 1)
                    if residual:
                        own.mark(e.tensor_scalar(res[:, k, :], src[:, k, :], ALPHA, None, ALU.mult))
                own.settle()

            def add_stage(first):
                with e.Fori(0, N_WO // 2) as p:
                    for slot in range(2):
                        e.wait_ge(chunk_done, 2 * p + (first + slot + 1))
                        r = res[:, bass.ds(p * 2 + slot, 1), :].rearrange("p a (h n) -> p (a h) n", h=2)
                        e.tensor_tensor(r, r, pstr[:, slot, :, 0:HALF], ALU.add).then_inc(chunk_taken, 1)
                        split_chunk(p + (first // 2 + 1), slot)

            def norm(n, src):
                e.wait_ge(ln_mean, n + 1)
                for k in range(KB):
                    s = halves(src[:, k, :])
                    e.tensor_tensor(s, s, aux[:, 0:2, 0:HALF], ALU.subtract).then_inc(ln_centred, 1)
                e.wait_ge(ln_var, 8 * n + 8)
                e.tensor_scalar(halves(rstd[:]), aux[:, 2:4, 0:HALF], EPS, None, ALU.add).then_inc(ln_eps, 1)
                e.wait_ge(ln_root, n + 1)
                e.reciprocal(rstd[:], rstd[:]).then_inc(ln_rstd, 1)
                e.wait_ge(ln_rstd, n + 1)
                for k in range(KB):
                    e.tensor_tensor(src[:, k, :], src[:, k, :], rstd[:], ALU.mult).then_inc(ln_normed, 1)

            e.wait_ge(setup_in, 64)
            split_x(0, xt, True)
            split_chunk(0, 0)
            split_chunk(0, 1)
            split_stage(C_AB, N_AB)

            e.wait_ge(f_done, 1)
            for r in range(2):
                own.mark(e.tensor_scalar(halves(lt[:, r, :]), aux[0:HEADS, 0:2, 0:HALF], vec[0:HEADS, V_BF:V_BF + 1], None, ALU.add))
            own.settle()
            e.tensor_scalar(lt[:, 1, :], lt[:, 1, :], 0.0, None, ALU.min).then_inc(f_abs, 1)
            e.wait_ge(f_abs, 1)
            e.wait_ge(f_ln, 1)
            e.tensor_tensor(lf[:], lt[:, 1, :], lt[:, 0, :], ALU.subtract).then_inc(f_logf, 1)
            e.wait_ge(f_logf, 1)
            own.mark(e.tensor_tensor_scan(ncum[:], cst[0:HEADS, ONES:ONES + 1].to_broadcast([HEADS, SEQ]), lf[:, 0:SEQ],
                                          0.0, ALU.mult, ALU.add))
            own.settle()
            e.tensor_scalar(ncum[:], ncum[:], -1.0, None, ALU.mult).then_inc(f_ncum, 1)

            def unit_max(u):
                h, q = divmod(u, QT)
                w = (q + 1) * P
                e.wait_ge(qk_done, u + 1)
                if q == 0:
                    e.wait_ge(nb_ready, h + 1)
                if u >= 2:
                    e.wait_ge(exp_done, u - 1)
                s = sc[:, u % 2, 0:w]
                e.scalar_tensor_tensor(s, aux[:, u % 2, 0:w], SCALE, nb[:, h % 2, 0:w], ALU.mult, ALU.add).then_inc(s_taken, 1)
                e.wait_ge(s_taken, u + 1)
                diag = sc[:, u % 2, w - P:w]
                own.mark(e.tensor_tensor(diag, diag, c(CMASK), ALU.add))
                own.settle()
                own.mark(e.tensor_reduce(st[:, u % 2, 2:3], s, AX, ALU.max))
                own.settle()
                e.tensor_scalar(st[:, u % 2, 0:1], st[:, u % 2, 2:3], -1.0, None, ALU.mult).then_inc(max_ready, 1)

            def unit_norm(u):
                w = (u % QT + 1) * P
                e.wait_ge(exp_done, u + 1)
                own.mark(e.reciprocal(st[:, u % 2, 3:4], st[:, u % 2, 1:2]))
                own.settle()
                p = pr[:, u % 2, 0:w]
                e.tensor_scalar(p, p, st[:, u % 2, 3:4], None, ALU.mult).then_inc(p_ready, 1)

            e.wait_ge(chunk_taken, C_WO0)
            e.wait_ge(state_in, 16)
            own.mark(e.memset(zp[:, :, 0:2], 0.0))
            for b in range(AB):
                e.tensor_tensor(zp[:, b, 2:SEQ + 2], proj[:, AB + b, 0:SEQ], proj[:, 2 * AB + b, 0:SEQ], ALU.mult).then_inc(z_done, 1)
                e.tensor_tensor(zs[:, b, :, 2], proj[:, AB + b, SEQ:N], proj[:, 2 * AB + b, SEQ:N], ALU.mult).then_inc(z_done, 1)
            own.settle()

            def conv(b):
                e.wait_ge(z_done, 2 * (b + 1))
                for dst, taps, gate in ((t1[:], [zp[:, b, j:j + SEQ] for j in range(3)], proj[:, b, 0:SEQ]),
                                        (t2[:], [zs[:, b, :, j] for j in range(3)], proj[:, b, SEQ:N])):
                    for j in range(3):
                        w = vec[:, V_CONV + j * AB + b:V_CONV + j * AB + b + 1]
                        if j == 0:
                            own.mark(e.tensor_scalar(dst, taps[j], w, None, ALU.mult))
                        else:
                            own.mark(e.scalar_tensor_tensor(dst, taps[j], w, dst, ALU.mult, ALU.add))
                        own.settle()
                    own.mark(e.tensor_tensor(gate, gate, dst, ALU.mult))
                own.settle()

            units = HEADS * QT
            unit_max(0)
            for u in range(units):
                if u + 1 < units:
                    unit_max(u + 1)
                unit_norm(u)
                if u % QT == QT - 1 and u // QT < AB:
                    conv(u // QT)

            q_s = proj[:, 3 * AB:4 * AB, SEQ:N].rearrange("p k b -> p b k")
            k_s = proj[:, 4 * AB:5 * AB, SEQ:N].rearrange("p k b -> p b k")
            own.mark(e.memset(qd[:], 0.0))
            own.settle()
            for par in range(2):
                rows = slice(HD * par, HD * par + HD)
                own.mark(e.tensor_scalar(qd[rows, :, :, par], q_s[rows], SCALE, None, ALU.mult))
            own.mark(e.tensor_tensor(prd[:], q_s, k_s, ALU.mult))
            own.settle()
            own.mark(e.tensor_scalar(prd[:], prd[:], SCALE, None, ALU.mult))
            e.wait_ge(logf_in, 16 * DEC * PAGES)
            own.mark(e.memset(later[:, :, PAGES - 1, :], 0.0))
            own.settle()
            for g in range(PAGES - 2, -1, -1):
                own.mark(e.tensor_tensor(later[:, :, g, :], later[:, :, g + 1, :], lfc[:, :, g + 1, :], ALU.add))
                own.settle()
            e.tensor_tensor(sm[0:HEADS, 1, :].rearrange("p (b h) -> p b h", b=DEC),
                            spread(lf[:, SEQ:N], 2, (HEADS, DEC, HEADS)),
                            spread(cst[0:HEADS, IDENT:IDENT + HEADS], 1, (HEADS, DEC, HEADS)), ALU.mult).then_inc(smp_in, 1)

            def bh(k):
                return sm[:, k, :].rearrange("p (b h) -> p b h", b=DEC)

            e.wait_ge(smp_pe, 3)
            for par in range(2):
                own.mark(e.tensor_copy(sm[:, 0, :].rearrange("p (b k r) -> p b k r", b=DEC, r=2)[:, :, :, par],
                                       aux[:, 2, 32 * par:32 * par + 32].rearrange("p (b k) -> p b k", b=DEC)))
            own.mark(e.tensor_copy(sm[:, 2, :], aux[:, 2, 64:128]))
            own.mark(e.tensor_copy(ss[:], aux[:, 1, :].rearrange("p (b g h) -> p b g h", b=DEC, g=PAGES)))
            own.settle()
            own.mark(e.tensor_tensor(ss[:], ss[:], spread(bh(2), 2, (P, DEC, PAGES, HEADS)), ALU.add))
            own.settle()
            e.wait_ge(kv_used, DEC)
            own.mark(e.tensor_tensor(ss[:], ss[:], aux[:, 0, :].rearrange("p (b g h) -> p b g h", b=DEC, g=PAGES), ALU.add))
            own.settle()
            e.tensor_reduce(bh(3), ss[:].rearrange("p b g h -> p b h g"), AX, ALU.max).then_inc(smp_in, 1)
            e.wait_ge(smp_pe, 4)
            own.mark(e.tensor_reduce(sm[0:64, 4, 0:1], aux[0:64, 2, 128:256], AX, ALU.max))
            own.settle()
            e.tensor_scalar(sm[0:64, 5, :], cst[0:64, IDENT:IDENT + 64], sm[0:64, 4, 0:1], None, ALU.mult).then_inc(smp_in, 1)
            e.wait_ge(smp_pe, 5)
            own.mark(e.tensor_tensor(sm[:, 6, :], sm[:, 0, :], aux[:, 2, 256:320], ALU.max))
            own.settle()
            e.tensor_tensor(ss[:], ss[:], spread(bh(6), 2, (P, DEC, PAGES, HEADS)), ALU.subtract).then_inc(smp_in, 1)
            e.tensor_tensor(sm[:, 0, :], sm[:, 0, :], sm[:, 6, :], ALU.subtract).then_inc(smp_in, 1)
            e.wait_ge(smp_act, 2)
            e.tensor_reduce(bh(3), ss[:].rearrange("p b g h -> p b h g"), AX, ALU.add).then_inc(smp_in, 1)
            e.wait_ge(smp_pe, 6)
            own.mark(e.tensor_tensor(sm[:, 6, :], sm[:, 0, :], aux[:, 2, 320:384], ALU.add))
            own.settle()
            own.mark(e.reciprocal(sm[:, 7, :], sm[:, 6, :]))
            own.settle()
            e.tensor_tensor(ss[:], ss[:], spread(bh(7), 2, (P, DEC, PAGES, HEADS)), ALU.mult).then_inc(smp_in, 1)
            own.mark(e.tensor_tensor(sm[:, 0, :], sm[:, 0, :], sm[:, 7, :], ALU.mult))
            own.settle()
            own_p = sm[:, 0, :].rearrange("p (b k r) -> p k b r", b=DEC, r=2)
            for par in range(2):
                rows = slice(HD * par, HD * par + HD)
                own.mark(e.tensor_tensor(t3[rows], proj[rows, 5 * AB:6 * AB, SEQ:N], own_p[rows, :, :, par], ALU.mult))
            own.settle()
            e.wait_ge(kv_used, 2 * DEC)
            e.wait_ge(o_taken, units)
            for par in range(2):
                rows = slice(HD * par, HD * par + HD)
                e.tensor_tensor(proj[rows, AB:2 * AB, SEQ:N], t3[rows],
                                aux[rows, 3, 0:64].rearrange("p (k b r) -> p k b r", k=AB, r=2)[:, :, :, par], ALU.add).then_inc(cat_ready, 1)

            split_x(1, proj, False)
            add_stage(C_WO0)
            norm(0, res)
            split_x(2, xt, True)

            def peer(layer):
                split_stage(C_WQ[layer], N_WQ)
                subs = GH // SUB
                per = 5 * NPAIR + 5 * HEADS + 14
                for t in range(NT):
                    tt = t + layer * NT
                    topk(tt, Steps(e, topk_step, tt * per), per)
                    e.wait_ge(pick_taken, tt + 1)
                    for n in range(2 * subs):
                        one_hots(tt * (2 * subs) + n, n % 2, n * SUB)

                def split_v(g, v):
                    e.wait_ge(v_hi, g * 8 + (layer * NG * 8 + v + 1))
                    e.tensor_tensor(vlo[:, v % 4, :], vraw[:, v % 4, :], vhi[:, v % 4, :].bitcast(F32), ALU.subtract).then_inc(v_lo, 1)

                def split_u(g, j):
                    split_chunk(g * 2 + (C_U[layer] // 2 + j // 2), j % 2)

                def gated(g, j):
                    at = g * GROUP + (layer * P + j)
                    e.wait_ge(chunk_taken, g * GROUP + (C_U[layer] + j + 1))
                    e.wait_ge(g_in[j], g * 16 + 16 * (layer * NG + 1))
                    if not (isinstance(g, int) and g == 0 and j < 2 and layer == 0):
                        e.wait_ge(wt_lo, at - 1)
                    e.tensor_tensor(wt[:, j % 2, :], hid[:, j % 2, :], gc[:, j, :], ALU.mult).then_inc(g_used, 1)

                def split_wt(g, j, par):
                    e.wait_ge(wt_hi, g * GROUP + (layer * P + j + 1))
                    e.tensor_tensor(wtl[:, par, j, :], wt[:, j % 2, :], wth[:, par, j, :].bitcast(F32), ALU.subtract).then_inc(wt_lo, 1)

                def take_v(g, v):
                    at = g * 8 + (layer * NG * 8 + v)
                    e.wait_ge(v_done, at + 1)
                    if not (isinstance(g, int) and g == 0):
                        e.wait_ge(v_taken, at - 7)
                    r = halves(res[:, v, :])
                    e.tensor_tensor(r, r, aux[:, 2 * (v % 2):2 * (v % 2) + 2, 0:HALF], ALU.add).then_inc(v_taken, 1)

                run_periods(e, layer, split_u, split_v, gated, split_wt, take_v)

            def topk(tt, s, per):
                R = slice(0, TT)
                e.wait_ge(sc_taken, tt + 1)
                for q in range(NPAIR):
                    s.mark(e.max(tv[R, q, 0:8], scores[R, q, :]))
                s.settle()
                for q in range(NPAIR):
                    s.mark(e.match_replace(scores2[R, q, :], tv[R, q, 0:8], scores[R, q, :], NEG))
                for q in range(NPAIR):
                    s.mark(e.max_index(ti[R, q, 0:8], tv[R, q, 0:8], scores[R, q, :]))
                s.settle()
                for q in range(NPAIR):
                    s.mark(e.max(tv[R, q, 8:16], scores2[R, q, :]))
                s.settle()
                for q in range(NPAIR):
                    s.mark(e.max_index(ti[R, q, 8:16], tv[R, q, 8:16], scores2[R, q, :]))
                s.settle()
                s.mark(e.tensor_copy(tif[R], ti[R]))
                pairs = tv[R].rearrange("p (h a) k -> p h a k", a=2)
                cand = scores[R].rearrange("p (h x) k -> p h (x k)", x=2)
                cand2 = scores2[R].rearrange("p (h x) k -> p h (x k)", x=2)
                s.mark(e.tensor_tensor(cand.rearrange("p h (a b) -> p h a b", a=TOPK),
                                       spread(pairs[:, :, 0, :], 3, (TT, HEADS, TOPK, TOPK)),
                                       spread(pairs[:, :, 1, :], 2, (TT, HEADS, TOPK, TOPK)), ALU.add))
                s.settle()
                for h in range(HEADS):
                    s.mark(e.max(bv[R, h, 0:8], cand[:, h, :]))
                s.settle()
                for h in range(HEADS):
                    s.mark(e.match_replace(cand2[:, h, :], bv[R, h, 0:8], cand[:, h, :], NEG))
                    s.mark(e.max_index(bp[R, h * TOPK:h * TOPK + 8], bv[R, h, 0:8], cand[:, h, :]))
                s.settle()
                for h in range(HEADS):
                    s.mark(e.max(bv[R, h, 8:16], cand2[:, h, :]))
                s.settle()
                for h in range(HEADS):
                    s.mark(e.max_index(bp[R, h * TOPK + 8:h * TOPK + 16], bv[R, h, 8:16], cand2[:, h, :]))
                s.settle()
                s.mark(e.tensor_copy(gs[R, 0, :], bv[R, :, 0]))
                s.settle()
                e.tensor_tensor(bv[R], bv[R], spread(gs[R, 0, :], 2, (TT, HEADS, TOPK)), ALU.subtract).then_inc(gate_shift, 1)
                s.mark(e.tensor_scalar(bu[R, 0, :], bp[R], 4, None, ALU.logical_shift_right))
                s.mark(e.tensor_scalar(bu[R, 1, :], bp[R], 15, None, ALU.bitwise_and))
                s.settle()
                s.mark(e.tensor_copy(bf[R], bu[R]))
                s.settle()
                lists = tif[R].rearrange("p (h a) k -> p h a k", a=2)
                for a in range(2):
                    s.mark(e.tensor_tensor(eq[R], spread(cst[R, IOTA:IOTA + TOPK], 1, (TT, HJ, TOPK)),
                                           spread(bf[R, a, :], 2, (TT, HJ, TOPK)), ALU.is_equal))
                    s.settle()
                    by_head = eq[R].rearrange("p (h r) k -> p h r k", h=HEADS)
                    s.mark(e.tensor_tensor(by_head, by_head, spread(lists[:, :, a, :], 2, (TT, HEADS, TOPK, TOPK)), ALU.mult))
                    s.settle()
                    s.mark(e.tensor_reduce(pick[R, a, :], eq[R], AX, ALU.add))
                    s.settle()
                e.wait_ge(gate_exp, tt + 1)
                s.mark(e.tensor_reduce(gs[R, 0, :], bv[R], AX, ALU.add))
                s.settle()
                s.mark(e.reciprocal(gs[R, 1, :], gs[R, 0, :]))
                s.settle()
                e.tensor_tensor(pick[R, 2, :].rearrange("p (h r) -> p h r", h=HEADS), bv[R],
                                spread(gs[R, 1, :], 2, (TT, HEADS, TOPK)), ALU.mult).then_inc(pick_ready, 1)
                assert s.marked == per

            def one_hots(n, slot, at):
                shape = (P, SUB, P)
                if n >= 2:
                    e.wait_ge(gate_done, n - 1)
                for k, dst in ((0, oh1), (1, oh2)):
                    e.tensor_tensor(dst[:, slot], spread(c(IOTA), 1, shape), spread(pickt[:, k, at:at + SUB], 2, shape),
                                    ALU.is_equal).then_inc(oh_hot, 1)
                e.wait_ge(oh_hot, n * 2 + 2)
                e.tensor_tensor(oh1[:, slot], oh1[:, slot], spread(pickt[:, 2, at:at + SUB], 2, shape), ALU.mult).then_inc(oh_ready, 1)

            if upto >= 1:
                peer(0)
            if upto >= 3:
                norm(1, res)
                split_x(3, xt, True)
                split_stage(C_INC, N_INC)
                e.wait_ge(sgu_in, 32)
                e.tensor_tensor(ws[:], ws[:], spread(c(UTRI), 1, (P, KB, P)), ALU.mult).then_inc(ws_masked, 1)
                norm(2, uv[:, KB:2 * KB, :])
                e.wait_ge(ln_out, 8 * 3)
                for g in range(KB):
                    own.mark(e.tensor_scalar(sps[:, g, :], uv[:, KB + g, SEQ:N], vec[:, V_W00 + g:V_W00 + g + 1],
                                             vec[:, V_B00 + g:V_B00 + g + 1], ALU.mult, ALU.add))
                own.settle()
                for g in range(KB):
                    e.tensor_tensor(uv[:, g, SEQ:N], uv[:, g, SEQ:N], sps[:, g, :], ALU.mult).then_inc(mix_ready, 1)
                for g in range(KB):
                    e.wait_ge(sg_done, g + 1)
                    e.tensor_tensor(sp[:, g % 2, :].rearrange("p (t n) -> p t n", t=QT),
                                    aux[:, 2 + g % 2, :].rearrange("p (t n) -> p t n", t=QT),
                                    spread(bs[:, g, :], 1, (P, QT, P)), ALU.add).then_inc(sg_taken, 1)
                    e.wait_ge(sg_taken, g + 1)
                    e.tensor_tensor(uv[:, g, 0:SEQ], uv[:, g, 0:SEQ], sp[:, g % 2, :], ALU.mult).then_inc(mix_ready, 1)
                    e.wait_ge(mix_ready, KB + g + 1)
                split_x(4, uv, False)
                add_stage(C_WOC)
                norm(3, res)
                split_x(5, xt, True)
                peer(1)
                norm(4, res)

        @block.tensor
        def _(e):
            def chunk(pair, slot):
                e.wait_ge(w_lo, 2 * pair + (slot + 1))
                if not (isinstance(pair, int) and pair == 0):
                    e.wait_ge(chunk_taken, 2 * pair + (slot - 1))
                for k in range(KB):
                    for w, x in ((whi, xh), (whi, xl), (wlo, xh)):
                        for h in range(2):
                            mm = e.matmul(pstr[:, slot, h, 0:HALF], w[:, slot, k * P:(k + 1) * P],
                                          x[:, k, h * HALF:(h + 1) * HALF],
                                          start=k == 0 and w is whi and x is xh, stop=k == KB - 1 and w is wlo)
                mm.then_inc(chunk_done, 1)

            def stage(first, count, splits, peel=0):
                e.wait_ge(x_lo, 8 * splits)
                for slot in range(2 * peel):
                    chunk(first // 2, slot)
                with e.Fori(peel, count // 2) as p:
                    for slot in range(2):
                        chunk(p + first // 2, slot)

            def norm(n, src):
                for h in range(2):
                    for k in range(KB):
                        mm = e.matmul(aux[:, h, 0:HALF], c(MEAN), src[:, k, h * HALF:(h + 1) * HALF],
                                      start=k == 0, stop=k == KB - 1)
                mm.then_inc(ln_mean, 1)
                for k in range(KB):
                    e.wait_ge(ln_sq, 8 * n + k + 1)
                    for h in range(2):
                        mm = e.matmul(aux[:, 2 + h, 0:HALF], c(MEAN), sq[:, k % 2, h * HALF:(h + 1) * HALF],
                                      start=k == 0, stop=k == KB - 1)
                    mm.then_inc(ln_var, 1)

            e.wait_ge(setup_in, 64)
            for h in range(2):
                for k in range(KB):
                    mm = e.matmul(aux[0:HEADS, h, 0:HALF], wf[:, k, :], xt[:, k, h * HALF:(h + 1) * HALF],
                                  start=k == 0, stop=k == KB - 1)
            mm.then_inc(f_done, 1)
            stage(C_AB, N_AB, 1, peel=1)

            e.wait_ge(chunk_taken, C_WO0)
            for t in range(QT):
                for b in range(AB):
                    mm = e.transpose(pstr[:, t // 2, t % 2, b * P:(b + 1) * P], proj[:, 5 * AB + b, t * P:(t + 1) * P], c(IDENT))
                mm.then_inc(vt_done, 1)

            def spread_ncum(h):
                if h == 0:
                    e.wait_ge(f_ncum, 1)
                    e.wait_ge(vn_ready, QT)
                else:
                    e.wait_ge(nb_ready, h)
                e.matmul(pstr[:, 1, 0, :], c(SELH + h * P, P, HEADS), ncum[:], start=True, stop=True).then_inc(nb_done, 1)

            def scores_unit(u):
                h, q = divmod(u, QT)
                rows = slice(HD * (h % 2), HD * (h % 2) + HD)
                if u >= 2:
                    e.wait_ge(s_taken, u - 1)
                e.matmul(aux[:, u % 2, 0:(q + 1) * P], proj[rows, 3 * AB + h // 2, q * P:(q + 1) * P],
                         proj[rows, 4 * AB + h // 2, 0:(q + 1) * P], start=True, stop=True).then_inc(qk_done, 1)

            def values_unit(u):
                h, q = divmod(u, QT)
                rows = slice(HD * (h % 2), HD * (h % 2) + HD)
                e.wait_ge(p_ready, u + 1)
                if u >= 2:
                    e.wait_ge(pt_ready, u - 1)
                for b in range(q + 1):
                    mm = e.transpose(aux[:, 2 + u % 2, b * P:(b + 1) * P], pr[:, u % 2, b * P:(b + 1) * P], c(IDENT))
                mm.then_inc(pt_done, 1)

            def out_unit(u):
                h, q = divmod(u, QT)
                rows = slice(HD * (h % 2), HD * (h % 2) + HD)
                e.wait_ge(pt_ready, u + 1)
                if u >= 2:
                    e.wait_ge(o_taken, u - 1)
                for b in range(q + 1):
                    mm = e.matmul(pstr[rows, 0, u % 2, 0:P], vn[:, b, h * HD:(h + 1) * HD], pt[:, u % 2, b * P:(b + 1) * P],
                                  start=b == 0, stop=b == q)
                mm.then_inc(pv_done, 1)

            units = HEADS * QT
            spread_ncum(0)
            scores_unit(0)
            scores_unit(1)
            for u in range(units):
                values_unit(u)
                if (u + 2) % QT == 0 and u + 2 < units:
                    spread_ncum((u + 2) // QT)
                if u + 2 < units:
                    scores_unit(u + 2)
                out_unit(u)

            e.wait_ge(smp_in, 1)
            for par in range(2):
                mm = e.matmul(aux[:, 2, 32 * par:32 * par + 32], c(SELP + par * P), prd[:].rearrange("p b k -> p (b k)"),
                              start=True, stop=True)
            mm.then_inc(smp_pe, 1)
            e.matmul(aux[:, 2, 64:128], c(ONES, P, HEADS), sm[0:HEADS, 1, :], start=True, stop=True).then_inc(smp_pe, 1)
            flat = "p b g h -> p (b g h)"
            e.matmul(aux[:, 1, :], c(TRI), lfc[:].rearrange(flat), start=True, stop=False)
            e.matmul(aux[:, 1, :], c(ONES), later[:].rearrange(flat), start=False, stop=True).then_inc(smp_pe, 1)
            with e.Fori(0, DEC // 2) as bp_:
                for s in range(2):
                    b = bp_ * 2 + s
                    e.wait_ge(kv_in[s], bp_ * (16 * PAGES) + 16 * PAGES)
                    for g in range(PAGES):
                        for k in range(AB):
                            mm = e.matmul(aux[:, 0, bass.ds(b * (PAGES * HEADS) + (g * HEADS + 2 * k), 2)],
                                          kv[:, s, (g * AB + k) * P:(g * AB + k + 1) * P],
                                          qd[:, bass.ds(b, 1), k, :].rearrange("p a r -> p (a r)"), start=True, stop=True)
                    mm.then_inc(kv_used, 1)
            e.wait_ge(smp_in, 2)
            e.transpose(aux[0:64, 2, 128:256], sm[:, 3, :], c(IDENT)).then_inc(smp_pe, 1)
            e.wait_ge(smp_in, 3)
            e.matmul(aux[:, 2, 256:320], c(ONES, P, 64), sm[0:64, 5, :], start=True, stop=True).then_inc(smp_pe, 1)
            e.wait_ge(smp_in, 6)
            e.matmul(aux[:, 2, 320:384], c(ONES), sm[:, 3, :], start=True, stop=True).then_inc(smp_pe, 1)
            e.wait_ge(smp_in, 7)
            with e.Fori(0, DEC // 2) as bp_:
                for s in range(2):
                    b = bp_ * 2 + s
                    e.wait_ge(kv_in[s], bp_ * (16 * PAGES) + 16 * PAGES * (1 + DEC // 2))
                    for k in range(AB):
                        for g in range(PAGES):
                            mm = e.matmul(aux[:, 3, bass.ds(b * 2 + k * 2 * DEC, 2)],
                                          kv[:, s, g * 512 + k * P:g * 512 + (k + 1) * P],
                                          ss[:, bass.ds(b, 1), g, 2 * k:2 * k + 2].rearrange("p a r -> p (a r)"),
                                          start=g == 0, stop=g == PAGES - 1)
                    mm.then_inc(kv_used, 1)

            stage(C_WO0, N_WO, 2)
            e.wait_ge(chunk_taken, C_WO0 + N_WO)
            norm(0, res)

            def peer(layer, splits):
                stage(C_WQ[layer], N_WQ, splits)
                e.wait_ge(chunk_taken, C_WQ[layer] + N_WQ)
                e.wait_ge(keys_in, 16 * (layer + 1))
                subs = GH // SUB

                def gate_pair(tt, s):
                    for slot in range(2):
                        n = s * 2 + (tt * 2 * subs + slot)
                        e.wait_ge(oh_ready, n + 1)
                        if not isinstance(n, int) or n >= 2:
                            e.wait_ge(gate_taken, n - 1)
                        for r in range(SUB):
                            mm = e.matmul(aux[:, slot, r * P:(r + 1) * P], oh2[:, slot, r, :], oh1[:, slot, r, :],
                                          start=True, stop=True)
                        mm.then_inc(gate_done, 1)

                for t in range(NT):
                    tt = t + layer * NT
                    if tt:
                        e.wait_ge(sc_taken, tt)
                    for q in range(NPAIR):
                        mm = e.matmul(pstr[0:TT, q // 8, (q // 4) % 2, (q % 4) * P:(q % 4 + 1) * P],
                                      q_t[:, q, t * TT:(t + 1) * TT], keys[:, q, :], start=True, stop=True)
                    mm.then_inc(sc_done, 1)
                    e.wait_ge(pick_ready, tt + 1)
                    for a in range(3):
                        mm = e.transpose(aux[:, 3, a * TT:(a + 1) * TT], pick[0:TT, a, :], cst[0:TT, IDENT:IDENT + TT])
                    mm.then_inc(pick_done, 1)
                    gate_pair(tt, 0)
                    with e.Fori(1, subs) as s:
                        gate_pair(tt, s)

                def first_table(g, j):
                    chunk(g * 2 + (C_U[layer] // 2 + j // 2), j % 2)

                def second_table(g, v, par):
                    at = g * 8 + (layer * NG * 8 + v)
                    e.wait_ge(v_lo, at + 1)
                    if v == 0:
                        e.wait_ge(wt_lo, g * GROUP + (layer * P + GROUP))
                    if v >= 2 or layer or not isinstance(g, int) or g > 0:
                        e.wait_ge(v_taken, at - 1)
                    for j in range(GROUP):
                        for w, x in ((vhi, wth), (vhi, wtl), (vlo, wth)):
                            for h in range(2):
                                mm = e.matmul(aux[:, 2 * (v % 2) + h, 0:HALF], w[:, v % 4, j * P:(j + 1) * P],
                                              x[:, par, j, h * HALF:(h + 1) * HALF],
                                              start=j == 0 and w is vhi and x is wth, stop=j == GROUP - 1 and w is vlo)
                    mm.then_inc(v_done, 1)

                def period(g, par, more):
                    if more:
                        for j in range(GROUP):
                            first_table(g + 1, j)
                    for v in range(8):
                        second_table(g, v, par)

                for j in range(GROUP):
                    first_table(0, j)
                period(0, 0, True)
                with e.Fori(0, NG // 2 - 1) as q:
                    period(q * 2 + 1, 1, True)
                    period(q * 2 + 2, 0, True)
                period(NG - 1, 1, False)

            if upto >= 1:
                peer(0, 3)
            if upto >= 3:
                e.wait_ge(v_taken, NG * 8)
                norm(1, res)
                stage(C_INC, N_INC, 4)
                e.wait_ge(chunk_taken, C_INC + N_INC)
                norm(2, uv[:, KB:2 * KB, :])
                e.wait_ge(ln_out, 8 * 3)
                e.wait_ge(ws_masked, 1)

                def turn(g):
                    if g >= 2:
                        e.wait_ge(st_ready, g - 1)
                    for t in range(QT):
                        mm = e.transpose(aux[:, g % 2, t * P:(t + 1) * P], uv[:, KB + g, t * P:(t + 1) * P], c(IDENT))
                    mm.then_inc(st_done, 1)

                turn(0)
                for g in range(KB):
                    if g + 1 < KB:
                        turn(g + 1)
                    e.wait_ge(st_ready, g + 1)
                    if g >= 2:
                        e.wait_ge(sg_taken, g - 1)
                    for t in range(QT):
                        mm = e.matmul(aux[:, 2 + g % 2, t * P:(t + 1) * P], vnt[:, g % 2, t * P:(t + 1) * P], ws[:, g, :],
                                      start=True, stop=True)
                    mm.then_inc(sg_done, 1)
                stage(C_WOC, N_WO, 5)
                e.wait_ge(chunk_taken, C_WOC + N_WO)
                norm(3, res)
                peer(1, 6)
                e.wait_ge(v_taken, 2 * NG * 8)
                norm(4, res)


OUTS = {"y": (P, KB, N), "k": (P, AB, N), "v": (P, AB, N), "lf": (HEADS, N), "cp": (P, AB, 2),
        "cs": (P, AB, DEC, 2), "sgv": (P, KB, DEC)}


def constants():
    cst = np.zeros((P, N_CST), np.float32)
    r = np.arange(P)
    cst[:, IDENT:IDENT + P] = np.eye(P)
    cst[:, ONES:ONES + P] = 1.0
    cst[:, TRI:TRI + P] = r[:, None] > r[None, :]
    cst[:, CMASK:CMASK + P] = np.where(r[None, :] <= r[:, None], 0.0, -1.0e30)
    cst[:, IOTA:IOTA + P] = r[None, :]
    cst[:, UTRI:UTRI + P] = r[None, :] >= r[:, None]
    cst[:, MEAN:MEAN + P] = 1.0 / D_MODEL
    for par in range(2):
        cst[HD * par:HD * par + HD, SELP + par * P:SELP + (par + 1) * P] = 1.0
    for h in range(HEADS):
        cst[h, SELH + h * P:SELH + (h + 1) * P] = 1.0
    return cst


def lay_out(x_prompt, x_sample, cache_k, cache_v, cache_logf, state_conv, page_table, w_in_ab, b_f, conv_w,
            w_o_ab, w_in_c, sg_ln_g, sg_ln_b, w_s, b_s, w_o_c, ln1_g, ln1_b, ln2_g, ln2_b,
            peer_wq, peer_keys, peer_u, peer_v):
    f = np.ascontiguousarray
    phys = cache_k.shape[0]

    def chunks(w):
        return w.reshape(KB, P, -1, P).transpose(2, 1, 0, 3)

    x = np.concatenate([x_prompt.reshape(SEQ, D_MODEL), x_sample.reshape(DEC, D_MODEL)])
    cols = 6 * AB * P
    vec = np.zeros((P, N_VEC), np.float32)
    for layer in range(DEPTH):
        for n, a in enumerate((ln1_g, ln1_b, ln2_g, ln2_b)):
            at = V_LN + 32 * layer + 8 * n
            vec[:, at:at + KB] = a[layer].reshape(KB, P).T
    vec[:, V_SG:V_SG + KB] = sg_ln_g[0].reshape(KB, P).T
    vec[:, V_SG + 8:V_SG + 8 + KB] = sg_ln_b[0].reshape(KB, P).T
    vec[:, V_W00:V_W00 + KB] = w_s[0, :, 0, 0][None, :]
    vec[:, V_B00:V_B00 + KB] = b_s[0, :, 0][None, :]
    vec[:, V_CONV:V_CONV + 3 * AB] = conv_w[0].reshape(3 * AB, P).T
    vec[0:HEADS, V_BF] = b_f[0]
    return {
        "cst": constants(),
        "vec": vec,
        "xt": f(x.T.reshape(KB, P, N).transpose(1, 0, 2)),
        "wf": f(w_in_ab[0][:, cols:].reshape(KB, P, HEADS).transpose(1, 0, 2)),
        "w": f(np.concatenate([chunks(w_in_ab[0][:, :cols]), chunks(w_o_ab[0]), chunks(peer_wq[0]),
                               chunks(w_in_c[0]), chunks(w_o_c[0]), chunks(peer_wq[1])])),
        "u": f(peer_u.reshape(DEPTH * P, P, KB, P).transpose(0, 3, 2, 1)),
        "v": f(peer_v.reshape(DEPTH, NG, GROUP, P, KB, P).transpose(0, 1, 4, 3, 2, 5)).reshape(DEPTH * NG * KB, P, GROUP * P),
        "keys": f(peer_keys.transpose(0, 4, 1, 2, 3)).reshape(DEPTH, P, NPAIR, P),
        "pt": f(page_table.reshape(1, DEC * PAGES)),
        "state": f(state_conv[:, 0].transpose(2, 0, 1).reshape(AB, P, DEC, 2).transpose(1, 0, 2, 3)),
        "clf": f(cache_logf[:, 0]),
        "ck": f(cache_k[:, 0].reshape(phys, PAGE, AB, P).transpose(0, 3, 2, 1)).reshape(phys, P, 512),
        "cv": f(cache_v[:, 0].reshape(phys, PAGE, 512)),
        "ws": f(w_s[0].transpose(2, 0, 1)),
        "bs": f(np.broadcast_to(b_s[0], (P, KB, P))),
    }


def arrange(r):
    def rows(a):
        return a.transpose(2, 1, 0).reshape(a.shape[2], -1)

    y, k, v = rows(r["y"]), rows(r["k"]), rows(r["v"])
    lf = r["lf"].T
    cp = rows(r["cp"])
    cs = r["cs"].transpose(2, 3, 1, 0).reshape(DEC, 1, 2, 512)
    return (y[:SEQ].reshape(1, SEQ, D_MODEL), y[SEQ:].reshape(DEC, 1, D_MODEL),
            k[:SEQ].reshape(1, 1, SEQ, HEADS, HD), v[:SEQ].reshape(1, 1, SEQ, HEADS, HD), lf[:SEQ].reshape(1, 1, SEQ, HEADS),
            k[SEQ:].reshape(DEC, 1, 1, HEADS, HD), v[SEQ:].reshape(DEC, 1, 1, HEADS, HD), lf[SEQ:].reshape(DEC, 1, 1, HEADS),
            cp.reshape(1, 1, 2, 512), cs, rows(r["sgv"]).reshape(DEC, 1, 1, D_MODEL))


def kernel(**inputs):
    import concourse.bacc as bacc
    from concourse.bass_utils import run_bass_kernel_spmd

    arrays = lay_out(**{n: np.asarray(a) for n, a in inputs.items()})
    nc = bacc.Bacc("TRN2", target_bir_lowering=False, num_devices=1)
    ins = {n: nc.dram_tensor(f"in_{n}", a.shape, mybir.dt.from_np(a.dtype), kind="ExternalInput").ap() for n, a in arrays.items()}
    outs = {n: nc.dram_tensor(f"out_{n}", s, F32, kind="ExternalOutput").ap() for n, s in OUTS.items()}
    trunk(nc, ins, outs)
    r = run_bass_kernel_spmd(nc, [{f"in_{n}": a for n, a in arrays.items()}], core_ids=[0])
    return arrange({n: r.results[0][f"out_{n}"] for n in OUTS})
```

```python
from contextlib import ExitStack

import numpy as np

import concourse.bass as bass
from concourse import mybir

F32 = mybir.dt.float32
F32R = mybir.dt.float32r
U32 = mybir.dt.uint32
I32 = mybir.dt.int32
ALU = mybir.AluOpType
ACT = mybir.ActivationFunctionType
AX = mybir.AxisListType.X

P = 128
D_MODEL = 1024
KB = D_MODEL // P
SEQ = 512
DEC = 8
N = SEQ + DEC
HALF = N // 2
DEPTH = 2
ALPHA = (2.0 * DEPTH) ** 0.25
EPS = 1e-5
HEADS = 8
HD = 64
AB = 4
QT = SEQ // P
PAGES = 8
PAGE = 128
NPAIR = HEADS * 2
TOPK = 16
HJ = HEADS * TOPK
TT = 104
NT = N // TT
GH = 52
SUB = 4
GROUP = 4
NG = 128 // GROUP
PLAN = [(6, 0, 0), (0, 11, 1), (0, 11, 1), (0, 9, 2), (0, 9, 2), (0, 1, 6)]
TAIL = 5
GROUPS = TT // SUB
EXP_AT = 17
RANK_PARTS = 48
RANK_IN = 22
PIECES = 4
assert (sum(map(sum, PLAN)) + TAIL) * 2 == P and len(PLAN) == NT + 1
assert all(2 * one + 4 * two == GROUPS for _, one, two in PLAN[1:])
NEG = -3.0e38
SCALE = HD ** -0.5

N_AB, N_WO, N_WQ, N_U, N_INC = 24, 8, 16, 128, 16
C_AB = 0
C_WO0 = C_AB + N_AB
C_WQ = [C_WO0 + N_WO, 0]
C_U = [C_WQ[0] + N_WQ, 0]
C_INC = C_U[0] + N_U
C_WOC = C_INC + N_INC
C_WQ[1] = C_WOC + N_WO
C_U[1] = C_WQ[1] + N_WQ
C_END = C_U[1] + N_U

SMP = {"operands": 0, "bias": 1, "keys": 2, "max": 17, "exp": 19, "norm": 19, "turn": 20, "turned": 20, "values": 21}
CONV_AT = [3, 6, 9, 12]

IDENT, ONES, IOTA, UTRI, MEAN, N_CST = 0, 128, 256, 384, 512, 640
TRI, CMASK, HMASK, SELB, SELH = 0, 128, 256, 768, 800
N_CAB = SELH + HEADS * P
BH = DEC * HEADS
V_LN = 0
V_SG = 64
V_W00 = 80
V_B00 = 88
V_CONV = 96
V_BF = 108
N_VEC = 112


class Steps:

    def __init__(self, engine, sem, count=0):
        self.engine, self.sem, self.count, self.marked = engine, sem, count, 0

    def mark(self, instruction):
        instruction.then_inc(self.sem, 1)
        self.count = self.count + 1
        self.marked += 1

    def settle(self):
        self.engine.wait_ge(self.sem, self.count)


def spread(ap, axis, shape):
    return ap.unsqueeze(axis).to_broadcast(list(shape))


def halves(ap):
    return ap.rearrange("p (h n) -> p h n", h=2)


def trunk(nc, i, o, upto=99):
    with ExitStack() as ctx:
        used = [nc.sbuf_base + (-nc.sbuf_base) % 64]

        def place(name, shape, dtype, at=None):
            n = int(np.prod(shape[1:])) * 4
            if at is None:
                at = used[0]
                used[0] += (n + 31) // 32 * 32
            return nc.alloc_sbuf_tensor_at(name, list(shape), dtype, offset=at)

        cst = place("cst", [P, N_CST], F32)
        vec = place("vec", [P, N_VEC], F32)
        at_xt = used[0]
        xt = place("xt", [P, KB, N], F32)
        at_xh = used[0]
        xh = place("xh", [P, KB, N], F32R)
        xl = place("xl", [P, KB, N], F32R)
        res = place("res", [P, KB, N], F32)
        wraw = place("wraw", [P, 2, KB * P], F32)
        whi = place("whi", [P, 2, KB * P], F32R)
        wlo = place("wlo", [P, 2, KB * P], F32R)
        at_ln = used[0]
        used[0] += 8320
        rstd = place("rstd", [P, N], F32, at_ln)
        sq = place("sq", [P, 2, N], F32, at_ln + 4 * N)
        phase = used[0]

        kv = place("kv", [P, 2, PAGES * 512], F32, at_xh)
        cab = place("cab", [P, N_CAB], F32)
        proj = place("proj", [P, N_AB, N], F32)
        zp = place("zp", [P, AB, SEQ + 2], F32)
        zs = place("zs", [P, AB, DEC, 3], F32)
        wf = place("wf", [P, KB, HEADS], F32)
        lf = place("lf", [HEADS, N], F32)
        lt = place("lt", [HEADS, 2, N], F32)
        ncum = place("ncum", [HEADS, SEQ], F32)
        vn = place("vn", [P, QT, 512], F32)
        nb = place("nb", [P, 2, SEQ], F32)
        sc = place("sc", [P, 2, SEQ], F32)
        pr = place("pr", [P, 2, SEQ], F32)
        pt = place("pt", [P, 2, SEQ], F32)
        st = place("st", [P, 2, 4], F32)
        t1 = place("t1", [P, SEQ], F32)
        t2 = place("t2", [P, DEC], F32)
        pg = place("pg", [1, DEC * PAGES], I32)
        qd = place("qd", [P, DEC, AB, BH], F32, at_ln)
        prd = place("prd", [P, DEC, AB], F32)
        prdh = place("prdh", [P, AB, BH], F32)
        lfc = place("lfc", [P, PAGES, DEC, HEADS], F32)
        later = place("later", [P, PAGES, DEC, HEADS], F32, at_xt + 0)
        lfn = place("lfn", [HEADS, BH], F32, at_xt + 13312)
        ps = place("ps", [BH, PAGES * PAGE], F32, at_xt + 2048)
        psd = place("psd", [BH, BH], F32, at_xt + 13568)
        sm = place("sm", [BH, 8], F32)
        ptp = place("ptp", [P, PAGES, 96], F32, at_xt + 10240)
        om = place("om", [P, 2, 512], F32, at_xt + 6144)
        t3 = place("t3", [P, AB, DEC], F32)
        print("mixer end", used[0], nc.sbuf_usable_end)
        assert used[0] <= nc.sbuf_usable_end, used[0]
        used[0] = phase
        scores = place("scores", [P, NPAIR, P], F32, at_xt)
        keys = place("keys", [P, NPAIR, P], F32, at_xt + 8192)
        eq = place("eq", [P, HJ, TOPK], F32, at_ln)
        q_t = place("q_t", [P, NPAIR, N], F32)
        tv = place("tv", [P, NPAIR, TOPK], F32)
        ti = place("ti", [P, NPAIR, TOPK], U32)
        tif = place("tif", [P, NPAIR, TOPK], F32)
        bv = place("bv", [P, HEADS, TOPK], F32)
        bp = place("bp", [P, HJ], U32)
        bu = place("bu", [P, 2, HJ], U32)
        bf = place("bf", [P, 2, HJ], F32)
        pick = place("pick", [P, 3, HJ], F32)
        gs = place("gs", [P, 2, HEADS], F32)
        pickt = place("pickt", [P, 3, TT], F32)
        oh1 = place("oh1", [P, 2, SUB, P], F32)
        oh2 = place("oh2", [P, 2, SUB, P], F32)
        gst = place("gst", [P, 2, P, GH], F32)
        choice_end = used[0]
        used[0] = phase
        vraw = place("vraw", [P, 4, GROUP * P], F32)
        vhi = place("vhi", [P, 4, GROUP * P], F32R)
        vlo = place("vlo", [P, 4, GROUP * P], F32R)
        wth = place("wth", [P, 2, GROUP, N], F32R)
        wtl = place("wtl", [P, 2, GROUP, N], F32R)
        gc = place("gc", [P, GROUP, N], F32)
        hl = place("hl", [P, GROUP, N], F32)
        wt = place("wt", [P, 2, N], F32)
        hid = place("hid", [P, 2, N], F32, max(used[0], choice_end))
        used[0] = max(used[0], choice_end) + 2 * 4 * N
        assert used[0] <= nc.sbuf_usable_end, used[0]
        used[0] = phase
        uv = place("uv", [P, 2 * KB, N], F32)
        vnt = place("vnt", [P, 2, QT * P], F32)
        ws = place("ws", [P, KB, P], F32)
        bs = place("bs", [P, KB, P], F32)
        sp = place("sp", [P, 2, SEQ], F32)
        sps = place("sps", [P, KB, DEC], F32)
        assert used[0] <= nc.sbuf_usable_end, used[0]

        gates = [nc.dram_tensor(f"gates{n}", (P, P, N), F32, kind="Internal").ap() for n in range(DEPTH)]

        hidden = [nc.dram_tensor(f"hidden{n}", (P, P, N), F32, kind="Internal").ap() for n in range(DEPTH)]

        pstr = ctx.enter_context(nc.psum_tensor("pstr", [P, 2, 2, 512], F32))
        aux = ctx.enter_context(nc.psum_tensor("aux", [P, 4, 512], F32))

        def sem(name):
            return ctx.enter_context(nc.semaphore(name))

        setup_in = sem("setup_in")
        pages_in = sem("pages_in")
        state_in = sem("state_in")
        logf_in = sem("logf_in")
        w_in = [sem(f"w_in{n}") for n in range(2)]
        kv_in = [sem(f"kv_in{n}") for n in range(2)]
        v_in = [sem(f"v_in{n}") for n in range(4)]
        g_in = [sem(f"g_in{n}") for n in range(4)]
        h_out = [sem(f"h_out{n}") for n in range(2)]
        h_in = [sem(f"h_in{n}") for n in range(GROUP)]
        keys_in = sem("keys_in")
        sgu_in = sem("sgu_in")
        out_done = sem("out_done")
        gates_out = [sem(f"gates_out{n}") for n in range(2)]
        y_out = sem("y_out")
        w_hi = sem("w_hi")
        w_lo = sem("w_lo")
        u_lo = sem("u_lo")
        chunk_done = sem("chunk_done")
        chunk_taken = sem("chunk_taken")
        x_hi = sem("x_hi")
        x_lo = sem("x_lo")
        ln_mean = sem("ln_mean")
        ln_centred = sem("ln_centred")
        ln_sq = sem("ln_sq")
        ln_var = sem("ln_var")
        ln_eps = sem("ln_eps")
        ln_root = sem("ln_root")
        ln_rstd = sem("ln_rstd")
        ln_normed = sem("ln_normed")
        ln_out = sem("ln_out")
        f_done = sem("f_done")
        f_abs = sem("f_abs")
        f_exp = sem("f_exp")
        f_ln = sem("f_ln")
        f_logf = sem("f_logf")
        f_ncum = sem("f_ncum")
        conv_done = sem("conv_done")
        z_done = sem("z_done")
        vt_done = sem("vt_done")
        vn_ready = sem("vn_ready")
        nb_done = sem("nb_done")
        nb_ready = sem("nb_ready")
        qk_done = sem("qk_done")
        s_taken = sem("s_taken")
        max_ready = sem("max_ready")
        exp_done = sem("exp_done")
        p_ready = sem("p_ready")
        pt_done = sem("pt_done")
        pt_ready = sem("pt_ready")
        pv_done = sem("pv_done")
        o_taken = sem("o_taken")
        smp_in = sem("smp_in")
        smp_pe = sem("smp_pe")
        smp_act = sem("smp_act")
        kv_used = sem("kv_used")
        cat_ready = sem("cat_ready")
        sc_done = sem("sc_done")
        sc_taken = sem("sc_taken")
        gate_shift = sem("gate_shift")
        gate_exp = sem("gate_exp")
        pick_ready = sem("pick_ready")
        pick_done = sem("pick_done")
        pick_taken = sem("pick_taken")
        oh_ready = sem("oh_ready")
        gate_done = sem("gate_done")
        gate_taken = sem("gate_taken")
        g_used = sem("g_used")
        wt_hi = sem("wt_hi")
        wt_lo = sem("wt_lo")
        v_hi = sem("v_hi")
        v_lo = sem("v_lo")
        v_done = sem("v_done")
        v_taken = sem("v_taken")
        ws_masked = sem("ws_masked")
        st_done = sem("st_done")
        st_ready = sem("st_ready")
        sg_done = sem("sg_done")
        sg_taken = sem("sg_taken")
        mix_ready = sem("mix_ready")
        dve_step = sem("dve_step")
        topk_step = sem("topk_step")

        def c(at, n=P, rows=P):
            return cst[0:rows, at:at + n]

        def ca(at, rows=P):
            return cab[0:rows, at:at + P]

        def lo_ready(e, first, pair, slot):
            by_pool = P - 2
            if first in C_U and (not isinstance(pair, int) or pair > 0):
                e.wait_ge(u_lo, pair * 2 + (C_U.index(first) * by_pool + slot - 1))
            else:
                e.wait_ge(w_lo, pair * 2 + (first + slot + 1 - (by_pool if first > C_U[0] else 0)))


        block = ctx.enter_context(nc.Block())

        @block.sync
        def _(e):
            for dst, src in ((cst[:], i["cst"]), (vec[:], i["vec"]), (cab[:], i["cab"]), (xt[:], i["xt"]), (wf[:], i["wf"])):
                e.dma_start(dst, src).then_inc(setup_in, 16)

            def load_chunk(before, pair, slot, src):
                if before is not None:
                    lo_ready(e, *before, slot)
                e.dma_start(wraw[:, slot, :], src.rearrange("a p k c -> p (a k c)")).then_inc(w_in[slot], 16)

            def load_stage(first, count, table, row0, before, done=0):
                if not done:
                    for slot in range(2):
                        load_chunk(before, first // 2, slot, table[row0 + slot:row0 + slot + 1])
                if count == 2:
                    return
                with e.Fori(1, count // 2) as p:
                    for slot in range(2):
                        load_chunk((first, p - 1), p + first // 2, slot, table[bass.ds(p * 2 + (row0 + slot), 1)])

            def load_cache():
                e.wait_ge(pages_in, 16)
                e.wait_ge(chunk_done, C_WO0)

                def load_pages(b, slot, table, used):
                    if used is not None:
                        e.wait_ge(kv_used, used)
                    for g in range(PAGES):
                        r = e.value_load(pg[0:1, bass.ds(b * PAGES + g, 1)], min_val=0, max_val=table.shape[0] - 1)
                        e.dma_start(kv[:, slot, g * 512:(g + 1) * 512],
                                    table[bass.ds(r, 1)].rearrange("a p c -> p (a c)")).then_inc(kv_in[slot], 16)

                for slot in range(2):
                    load_pages(slot, slot, i["ck"], None)
                with e.Fori(1, DEC // 2) as p:
                    for slot in range(2):
                        load_pages(p * 2 + slot, slot, i["ck"], p * 2 + (slot - 1))
                with e.Fori(0, DEC // 2) as p:
                    for slot in range(2):
                        load_pages(p * 2 + slot, slot, i["cv"], p * 2 + (DEC + slot - 1))

            def load_v(layer, g, v):
                at = g * 8 + (layer * NG * 8 + v)
                if v >= 4 or layer or not isinstance(g, int) or g > 0:
                    e.wait_ge(v_lo, at - 3)
                e.dma_start(vraw[:, v % 4, :], i["v"][bass.ds(at, 1)].rearrange("a p c -> p (a c)")).then_inc(v_in[v % 4], 16)

            def peer_tables(layer):
                subs = GH // SUB
                base = C_U[layer]

                def load_u(pair):
                    before = (C_WQ[layer], N_WQ // 2 - 1) if isinstance(pair, int) and pair == 0 else (base, pair - 1)
                    for slot in range(2):
                        load_chunk(before, pair + base // 2, slot, i["u"][bass.ds(pair * 2 + (layer * P + slot), 1)])

                def store_h(pair):
                    for slot in range(2):
                        e.wait_ge(chunk_taken, pair * 2 + (base + slot + 1))
                        e.dma_start(hidden[layer][bass.ds(pair * 2 + slot, 1)].rearrange("a p n -> p (a n)"),
                                    hid[:, slot, :]).then_inc(h_out[slot], 16)

                def store_gates(half, part):
                    n = P // PIECES
                    e.wait_ge(gate_taken, (half + 1 + layer * NT * 2) * subs)
                    e.dma_start(gates[layer][part * n:(part + 1) * n, :, half * GH:(half + 1) * GH].rearrange("a b n -> b a n"),
                                gst[:, half % 2, part * n:(part + 1) * n, :]).then_inc(gates_out[half % 2], 16)

                def load_h(g, j):
                    at = g * GROUP + (layer * P + j)
                    if layer or not isinstance(g, int) or g > 0:
                        e.wait_ge(g_used, at - 3)
                    e.dma_start(hl[:, j, :], hidden[layer][bass.ds(g * GROUP + j, 1)].rearrange("a p n -> p (a n)")).then_inc(h_in[j], 16)
                    e.dma_start(gc[:, j, :], gates[layer][bass.ds(g * GROUP + j, 1)].rearrange("a p n -> p (a n)")).then_inc(g_in[j], 16)

                load_u(0)
                store = {}
                start = 0
                for w, (zero, one, two) in enumerate(PLAN):
                    if w:
                        done = next(r for r in range(one + two) if 2 * (r + 1) + 2 * max(0, r + 1 - one) >= subs)
                        for part in range(PIECES):
                            store.setdefault(start + done + 1 + part // 2, []).append((2 * w - 2, part))
                            store.setdefault(start + one + two + part // 2, []).append((2 * w - 1, part))
                    start += zero + one + two
                pair = 0
                while pair < P // 2:
                    if pair + 1 < P // 2:
                        load_u(pair + 1)
                    for half, part in store.get(pair, ()):
                        store_gates(half, part)
                    if pair == P // 2 - 3:
                        for par in range(2):
                            e.wait_ge(gates_out[par], 16 * PIECES * NT * (layer + 1))
                        for j in range(GROUP):
                            load_h(0, j)
                        for v in range(4):
                            load_v(layer, 0, v)
                    store_h(pair)
                    pair += 1
                    if pair == 1:
                        with e.Fori(1, PLAN[0][0]) as p:
                            load_u(p + 1)
                            store_h(p)
                        pair = PLAN[0][0]

                for slot in range(2):
                    e.wait_ge(h_out[slot], 16 * (P // 2) * (layer + 1))

                def period(g, more):
                    for v in range(8):
                        if not (isinstance(g, int) and g == 0 and v < 4):
                            load_v(layer, g, v)
                        if more and v < GROUP:
                            load_h(g + 1, v)

                period(0, True)
                with e.Fori(1, NG - 1) as g:
                    period(g, True)
                period(NG - 1, False)

            load_stage(C_AB, N_AB, i["w"], 0, None)
            load_stage(C_WO0, 2, i["w"], 24, (C_AB, N_AB // 2 - 1))
            load_cache()
            load_stage(C_WO0, N_WO, i["w"], 24, (C_AB, N_AB // 2 - 1), done=2)
            load_stage(C_WQ[0], N_WQ, i["w"], 32, (C_WO0, N_WO // 2 - 1))
            if upto >= 1:
                peer_tables(0)
            if upto >= 3:
                load_stage(C_INC, N_INC, i["w"], 48, (C_U[0], P // 2 - 1))
                load_stage(C_WOC, N_WO, i["w"], 64, (C_INC, N_INC // 2 - 1))
                load_stage(C_WQ[1], N_WQ, i["w"], 72, (C_WOC, N_WO // 2 - 1))
                peer_tables(1)
                for k in range(KB):
                    e.wait_ge(ln_out, 8 * 4 + k + 1)
                    e.dma_start(o["y"][:, k, :], xt[:, k, :]).then_inc(y_out, 16)
                e.wait_ge(y_out, 16 * KB)

        @block.gpsimd
        def _(e):
            e.dma_start(pg[:], i["pt"]).then_inc(pages_in, 16)
            e.dma_start(zs[:, :, :, 0:2], i["state"]).then_inc(state_in, 16)
            e.wait_ge(pages_in, 16)
            with e.Fori(0, DEC) as b:
                for g in range(PAGES):
                    r = e.value_load(pg[0:1, bass.ds(b * PAGES + g, 1)], min_val=0, max_val=i["clf"].shape[0] - 1)
                    e.dma_start(lfc[:, g, bass.ds(b, 1), :], i["clf"][bass.ds(r, 1)].rearrange("a p h -> p a h")).then_inc(logf_in, 16)
            e.wait_ge(chunk_taken, C_WO0)
            e.dma_start(o["k"], proj[:, 16:20, :]).then_inc(out_done, 16)
            e.dma_start(o["v"], proj[:, 20:24, :]).then_inc(out_done, 16)
            e.wait_ge(f_logf, 1)
            e.dma_start(o["lf"], lf[:]).then_inc(out_done, 16)
            e.wait_ge(z_done, 2 * AB)
            e.wait_ge(state_in, 16)
            e.dma_start(o["cp"], zp[:, :, SEQ:SEQ + 2]).then_inc(out_done, 16)
            e.dma_start(o["cs"], zs[:, :, :, 1:3]).then_inc(out_done, 16)
            e.wait_ge(out_done, 16 * 5)

            def peer(layer):
                lo_ready(e, C_WQ[layer], 1, 0)
                e.dma_start(keys[:], i["keys"][layer]).then_inc(keys_in, 16)
                with e.Fori(1, P // 2) as p:
                    for slot in range(2):
                        pair = p + C_U[layer] // 2
                        e.wait_ge(w_hi, pair * 2 + (slot + 1))
                        e.tensor_tensor(wlo[:, slot, :], wraw[:, slot, :], whi[:, slot, :].bitcast(F32),
                                        ALU.subtract).then_inc(u_lo, 1)

            if upto >= 1:
                peer(0)
            if upto >= 3:
                e.wait_ge(v_taken, NG * 8)
                e.dma_start(ws[:], i["ws"]).then_inc(sgu_in, 16)
                e.dma_start(bs[:], i["bs"]).then_inc(sgu_in, 16)
                e.wait_ge(ln_out, 8 * 3)
                e.dma_start(o["sgv"], uv[:, KB:2 * KB, SEQ:N]).then_inc(out_done, 16)
                e.wait_ge(out_done, 16 * 6)
                peer(1)

        @block.scalar
        def _(e):
            def round_chunk(pair, slot):
                e.wait_ge(w_in[slot], 16 * pair + 16)
                if not (isinstance(pair, int) and pair == 0):
                    e.wait_ge(chunk_done, 2 * pair + (slot - 1))
                e.activation(whi[:, slot, :], wraw[:, slot, :], ACT.Copy).then_inc(w_hi, 1)

            def take_stage(first, count, dst, func, col):
                with e.Fori(0, count // 2) as p:
                    for slot in range(2):
                        e.wait_ge(chunk_done, 2 * p + (first + slot + 1))
                        out = dst[:, bass.ds(p * 2 + (col + slot), 1), :].rearrange("p a (h n) -> p (a h) n", h=2)
                        e.activation(out, pstr[:, slot, :, 0:HALF], func).then_inc(chunk_taken, 1)
                        round_chunk(p + (first // 2 + 1), slot)

            def round_stage(first, count):
                with e.Fori(0, count // 2) as p:
                    for slot in range(2):
                        round_chunk(p + (first // 2 + 1), slot)

            def round_x(src, ready):
                for k in range(KB):
                    ready(k)
                    e.activation(xh[:, k, :], src[:, k, :], ACT.Copy).then_inc(x_hi, 1)

            def norm(n, src, gcol, bcol, dst):
                for k in range(KB):
                    e.wait_ge(ln_centred, 8 * n + k + 1)
                    if k >= 2:
                        e.wait_ge(ln_var, 8 * n + k - 1)
                    e.activation(sq[:, k % 2, :], src[:, k, :], ACT.Square).then_inc(ln_sq, 1)
                e.wait_ge(ln_eps, n + 1)
                e.activation(rstd[:], rstd[:], ACT.Sqrt).then_inc(ln_root, 1)
                for k in range(KB):
                    e.wait_ge(ln_normed, 8 * n + k + 1)
                    e.activation(dst[:, k, :], src[:, k, :], ACT.Identity, bias=vec[:, bcol + k:bcol + k + 1],
                                 scale=vec[:, gcol + k:gcol + k + 1]).then_inc(ln_out, 1)

            e.wait_ge(setup_in, 80)
            round_x(xt, lambda k: None)
            round_chunk(0, 0)
            round_chunk(0, 1)
            take_stage(C_AB, N_AB, proj, ACT.Copy, 0)

            e.wait_ge(f_abs, 1)
            e.activation(lt[:, 0, :], lt[:, 0, :], ACT.Abs).then_inc(f_exp, 1)
            e.wait_ge(f_exp, 1)
            e.activation(lt[:, 0, :], lt[:, 0, :], ACT.Exp, scale=-1.0).then_inc(f_exp, 1)
            e.wait_ge(f_exp, 2)
            e.activation(lt[:, 0, :], lt[:, 0, :], ACT.Ln, bias=1.0).then_inc(f_ln, 1)

            for t in range(QT):
                e.wait_ge(vt_done, t + 1)
                e.activation(vn[:, t, :], pstr[:, t // 2, t % 2, :], ACT.Copy).then_inc(vn_ready, 1)

            def take_nb(h):
                e.wait_ge(nb_done, h + 1)
                if h >= 2:
                    e.wait_ge(s_taken, QT * (h - 1))
                e.activation(nb[:, h % 2, :], pstr[:, 0, 1, :], ACT.Copy).then_inc(nb_ready, 1)

            def exp_unit(u):
                w = (u % QT + 1) * P
                e.wait_ge(max_ready, u + 1)
                if u >= 2:
                    e.wait_ge(pt_done, u - 1)
                e.activation(pr[:, u % 2, 0:w], sc[:, u % 2, 0:w], ACT.Exp, bias=st[:, u % 2, 0:1],
                             accum_out=st[:, u % 2, 1:2]).then_inc(exp_done, 1)

            def take_pt(u):
                w = (u % QT + 1) * P
                e.wait_ge(pt_done, u + 1)
                if u >= 2:
                    e.wait_ge(pv_done, u - 1)
                e.activation(pt[:, u % 2, 0:w], aux[:, 2 + u % 2, 0:w], ACT.Copy).then_inc(pt_ready, 1)

            def take_o(u):
                h, q = divmod(u, QT)
                rows = slice(HD * (h % 2), HD * (h % 2) + HD)
                e.wait_ge(pv_done, u + 1)
                e.activation(proj[rows, AB + h // 2, q * P:(q + 1) * P], pstr[rows, 0, 0, u % 2 * P:(u % 2 + 1) * P],
                             ACT.Copy).then_inc(o_taken, 1)

            units = HEADS * QT
            take_nb(0)
            exp_unit(0)
            for u in range(units):
                if (u + 2) % QT == 0 and (u + 2) // QT < HEADS:
                    take_nb((u + 2) // QT)
                if u + 1 < units:
                    exp_unit(u + 1)
                if u >= 1:
                    take_o(u - 1)
                take_pt(u)
                if u == SMP["exp"]:
                    e.wait_ge(smp_in, 2)
                    e.activation(ps[:], pstr[0:BH, 1, :, :].rearrange("p a n -> p (a n)"), ACT.Exp, bias=sm[:, 2:3],
                                 accum_out=sm[:, 3:4]).then_inc(smp_act, 1)
                    e.activation(sm[:, 4:5], sm[:, 0:1], ACT.Exp, bias=sm[:, 2:3]).then_inc(smp_act, 1)
            take_o(units - 1)

            e.wait_ge(kv_used, 2 * DEC)
            e.wait_ge(cat_ready, 1)
            round_x(proj, lambda k: None)
            round_stage(C_WO0, N_WO)
            norm(0, res, V_LN, V_LN + 8, xt)
            def own_ln(n):
                return lambda k: e.wait_ge(ln_out, 8 * n + k + 1)
            round_x(xt, own_ln(0))

            def peer(layer):
                e.wait_ge(out_done, 16 * (5 + layer))
                take_stage(C_WQ[layer], N_WQ, q_t, ACT.Copy, 0)
                subs = GH // SUB
                base = C_U[layer]

                def hidden_one(pair, slot):
                    e.wait_ge(chunk_done, pair * 2 + (base + slot + 1))
                    if layer or not isinstance(pair, int) or pair > 0:
                        e.wait_ge(h_out[slot], pair * 16 + 16 * (layer * P // 2))
                    e.activation(halves(hid[:, slot, :]), pstr[:, slot, :, 0:HALF], ACT.Gelu_apprx_tanh).then_inc(chunk_taken, 1)
                    if not isinstance(pair, int) or pair + 1 < P // 2:
                        round_chunk(pair + (base // 2 + 1), slot)

                def hidden_pair(pair):
                    for slot in range(2):
                        hidden_one(pair, slot)

                def take_gates(tt, n):
                    half = tt * 2 + n // subs
                    if n % subs == 0 and half >= 2:
                        e.wait_ge(gates_out[half % 2], 16 * PIECES * (half // 2))
                    e.wait_ge(gate_done, tt * GROUPS + (n + 1))
                    e.activation(gst[:, half % 2, :, n % subs * SUB:(n % subs + 1) * SUB].rearrange("p a n -> p n a"),
                                 aux[:, n % 2, :].rearrange("p (n a) -> p n a", n=SUB), ACT.Copy).then_inc(gate_taken, 1)

                def gate_exponentials(tt):
                    e.wait_ge(gate_shift, tt + 1)
                    e.activation(bv[0:TT, :, :], bv[0:TT, :, :], ACT.Exp).then_inc(gate_exp, 1)

                pair = 0
                for w, (zero, one, two) in enumerate(PLAN):
                    tt = w + layer * NT
                    if w < NT:
                        for b in range(4):
                            e.wait_ge(sc_done, tt * 4 + b + 1)
                            e.activation(scores[0:TT, 4 * b:4 * b + 4, :].rearrange("p a k -> p (a k)"),
                                         aux[0:TT, 2 + b % 2, :], ACT.Copy).then_inc(sc_taken, 1)
                    if zero:
                        hidden_pair(pair)
                        with e.Fori(pair + 1, pair + zero - 2) as p:
                            hidden_pair(p)
                        gate_exponentials(tt)
                        for p in range(pair + zero - 2, pair + zero):
                            hidden_pair(p)
                    n = 0
                    for q in range(one + two):
                        for slot in range(2):
                            hidden_one(pair + zero + q, slot)
                            for _ in range(1 if q < one else 2):
                                if n == EXP_AT and w < NT:
                                    gate_exponentials(tt)
                                take_gates(tt - 1, n)
                                n += 1
                    if w < NT:
                        e.wait_ge(pick_done, tt + 1)
                        e.activation(pickt[:].rearrange("p a n -> p (a n)"), aux[:, 3, 0:3 * TT], ACT.Copy).then_inc(pick_taken, 1)
                    pair += zero + one + two
                with e.Fori(pair, P // 2 - 1) as p:
                    hidden_pair(p)

                for par in range(2):
                    e.wait_ge(gates_out[par], 16 * PIECES * NT * (layer + 1))

                def round_v(g, v):
                    at = g * 8 + (layer * NG * 8 + v)
                    e.wait_ge(v_in[v % 4], g * 32 + 16 * (layer * NG * 2 + v // 4 + 1))
                    if v >= 4 or layer or not isinstance(g, int) or g > 0:
                        e.wait_ge(v_done, at - 3)
                    e.activation(vhi[:, v % 4, :], vraw[:, v % 4, :], ACT.Copy).then_inc(v_hi, 1)

                def round_wt(g, j, par):
                    e.wait_ge(g_used, g * GROUP + (layer * P + j + 1))
                    if j == 0 and (not isinstance(g, int) or g > 1):
                        e.wait_ge(v_done, g * 8 + (layer * NG * 8 - 8))
                    e.activation(wth[:, par, j, :], wt[:, j % 2, :], ACT.Copy).then_inc(wt_hi, 1)

                def period(g, par, more):
                    for v in range(8):
                        if more and v < GROUP:
                            round_wt(g + 1, v, 1 - par)
                        if v < 6:
                            round_v(g, v + 2)
                        elif more:
                            round_v(g + 1, v - 6)

                for j in range(GROUP):
                    round_wt(0, j, 0)
                round_v(0, 0)
                round_v(0, 1)
                hidden_pair(P // 2 - 1)
                period(0, 0, True)
                with e.Fori(0, NG // 2 - 1) as q:
                    period(q * 2 + 1, 1, True)
                    period(q * 2 + 2, 0, True)
                period(NG - 1, 1, False)
                if layer + 1 < DEPTH:
                    for slot in range(2):
                        round_chunk(C_INC // 2, slot)

            if upto >= 1:
                peer(0)
            if upto >= 3:
                norm(1, res, V_LN + 16, V_LN + 24, xt)
                round_x(xt, own_ln(1))
                take_stage(C_INC, N_INC, uv, ACT.Gelu_apprx_tanh, 0)
                norm(2, uv[:, KB:2 * KB, :], V_SG, V_SG + 8, uv[:, KB:2 * KB, :])
                for g in range(KB):
                    e.wait_ge(st_done, g + 1)
                    if g >= 2:
                        e.wait_ge(sg_done, g - 1)
                    e.activation(vnt[:, g % 2, :], aux[:, g % 2, :], ACT.Copy).then_inc(st_ready, 1)
                e.wait_ge(mix_ready, 2 * KB)
                round_x(uv, lambda k: None)
                round_stage(C_WOC, N_WO)
                norm(3, res, V_LN + 32, V_LN + 40, xt)
                round_x(xt, own_ln(3))
                peer(1)
                norm(4, res, V_LN + 48, V_LN + 56, xt)

        @block.vector
        def _(e):
            own = Steps(e, dve_step)

            def split_chunk(pair, slot):
                e.wait_ge(w_hi, 2 * pair + (slot + 1))
                e.tensor_tensor(wlo[:, slot, :], wraw[:, slot, :], whi[:, slot, :].bitcast(F32), ALU.subtract).then_inc(w_lo, 1)

            def split_stage(first, count):
                with e.Fori(0, count // 2) as p:
                    for slot in range(2):
                        split_chunk(p + (first // 2 + 1), slot)

            def split_x(n, src, residual):
                for k in range(KB):
                    e.wait_ge(x_hi, 8 * n + k + 1)
                    e.tensor_tensor(xl[:, k, :], src[:, k, :], xh[:, k, :].bitcast(F32), ALU.subtract).then_inc(x_lo, 1)
                    if residual:
                        own.mark(e.tensor_scalar(res[:, k, :], src[:, k, :], ALPHA, None, ALU.mult))
                own.settle()

            def add_stage(first):
                with e.Fori(0, N_WO // 2) as p:
                    for slot in range(2):
                        e.wait_ge(chunk_done, 2 * p + (first + slot + 1))
                        r = res[:, bass.ds(p * 2 + slot, 1), :].rearrange("p a (h n) -> p (a h) n", h=2)
                        e.tensor_tensor(r, r, pstr[:, slot, :, 0:HALF], ALU.add).then_inc(chunk_taken, 1)
                        split_chunk(p + (first // 2 + 1), slot)

            def norm(n, src):
                e.wait_ge(ln_mean, n + 1)
                for k in range(KB):
                    s = halves(src[:, k, :])
                    e.tensor_tensor(s, s, aux[:, 0:2, 0:HALF], ALU.subtract).then_inc(ln_centred, 1)
                e.wait_ge(ln_var, 8 * n + 8)
                e.tensor_scalar(halves(rstd[:]), aux[:, 2:4, 0:HALF], EPS, None, ALU.add).then_inc(ln_eps, 1)
                e.wait_ge(ln_root, n + 1)
                e.reciprocal(rstd[:], rstd[:]).then_inc(ln_rstd, 1)
                e.wait_ge(ln_rstd, n + 1)
                for k in range(KB):
                    e.tensor_tensor(src[:, k, :], src[:, k, :], rstd[:], ALU.mult).then_inc(ln_normed, 1)

            e.wait_ge(setup_in, 80)
            for zero in (qd, prdh):
                own.mark(e.memset(zero[:], 0.0))
            split_x(0, xt, True)
            split_chunk(0, 0)
            split_chunk(0, 1)
            split_stage(C_AB, N_AB)

            e.wait_ge(f_done, 1)
            for r in range(2):
                own.mark(e.tensor_scalar(halves(lt[:, r, :]), aux[0:HEADS, 0:2, 0:HALF], vec[0:HEADS, V_BF:V_BF + 1], None, ALU.add))
            own.settle()
            e.tensor_scalar(lt[:, 1, :], lt[:, 1, :], 0.0, None, ALU.min).then_inc(f_abs, 1)
            e.wait_ge(f_abs, 1)
            e.wait_ge(f_ln, 1)
            e.tensor_tensor(lf[:], lt[:, 1, :], lt[:, 0, :], ALU.subtract).then_inc(f_logf, 1)
            e.wait_ge(f_logf, 1)
            own.mark(e.tensor_tensor_scan(ncum[:], cst[0:HEADS, ONES:ONES + 1].to_broadcast([HEADS, SEQ]), lf[:, 0:SEQ],
                                          0.0, ALU.mult, ALU.add))
            own.settle()
            e.tensor_scalar(ncum[:], ncum[:], -1.0, None, ALU.mult).then_inc(f_ncum, 1)

            def unit_max(u):
                h, q = divmod(u, QT)
                w = (q + 1) * P
                e.wait_ge(qk_done, u + 1)
                if q == 0:
                    e.wait_ge(nb_ready, h + 1)
                if u >= 2:
                    e.wait_ge(exp_done, u - 1)
                s = sc[:, u % 2, 0:w]
                e.scalar_tensor_tensor(s, aux[:, u % 2, 0:w], SCALE, nb[:, h % 2, 0:w], ALU.mult, ALU.add).then_inc(s_taken, 1)
                e.wait_ge(s_taken, u + 1)
                diag = sc[:, u % 2, w - P:w]
                own.mark(e.tensor_tensor(diag, diag, ca(CMASK), ALU.add))
                own.settle()
                own.mark(e.tensor_reduce(st[:, u % 2, 2:3], s, AX, ALU.max))
                own.settle()
                e.tensor_scalar(st[:, u % 2, 0:1], st[:, u % 2, 2:3], -1.0, None, ALU.mult).then_inc(max_ready, 1)

            def unit_norm(u):
                w = (u % QT + 1) * P
                e.wait_ge(exp_done, u + 1)
                own.mark(e.reciprocal(st[:, u % 2, 3:4], st[:, u % 2, 1:2]))
                own.settle()
                p = pr[:, u % 2, 0:w]
                e.tensor_scalar(p, p, st[:, u % 2, 3:4], None, ALU.mult).then_inc(p_ready, 1)

            e.wait_ge(chunk_taken, C_WO0)
            e.wait_ge(state_in, 16)
            own.mark(e.memset(zp[:, :, 0:2], 0.0))
            for b in range(AB):
                e.tensor_tensor(zp[:, b, 2:SEQ + 2], proj[:, AB + b, 0:SEQ], proj[:, 2 * AB + b, 0:SEQ], ALU.mult).then_inc(z_done, 1)
                e.tensor_tensor(zs[:, b, :, 2], proj[:, AB + b, SEQ:N], proj[:, 2 * AB + b, SEQ:N], ALU.mult).then_inc(z_done, 1)
            own.settle()

            def conv(b):
                e.wait_ge(z_done, 2 * (b + 1))
                for dst, taps, gate in ((t1[:], [zp[:, b, j:j + SEQ] for j in range(3)], proj[:, b, 0:SEQ]),
                                        (t2[:], [zs[:, b, :, j] for j in range(3)], proj[:, b, SEQ:N])):
                    for j in range(3):
                        w = vec[:, V_CONV + j * AB + b:V_CONV + j * AB + b + 1]
                        if j == 0:
                            own.mark(e.tensor_scalar(dst, taps[j], w, None, ALU.mult))
                        else:
                            own.mark(e.scalar_tensor_tensor(dst, taps[j], w, dst, ALU.mult, ALU.add))
                        own.settle()
                    own.mark(e.tensor_tensor(gate, gate, dst, ALU.mult))
                own.settle()

            cached = pstr[:, 1, :, :]
            small = pstr[:, 0, 0, 2 * P:4 * P]

            def sample_operands():
                q_s = proj[:, 3 * AB:4 * AB, SEQ:N].rearrange("p k b -> p b k")
                k_s = proj[:, 4 * AB:5 * AB, SEQ:N].rearrange("p k b -> p b k")
                e.wait_ge(logf_in, 16 * DEC * PAGES)
                own.mark(e.memset(ptp[:], 0.0))
                own.mark(e.memset(later[:, PAGES - 1, :, :], 0.0))
                own.mark(e.scalar_tensor_tensor(prd[:], q_s, SCALE, k_s, ALU.mult, ALU.mult))
                own.settle()
                for par in range(2):
                    rows = slice(HD * par, HD * par + HD)
                    for b in range(DEC):
                        at = b * HEADS + par
                        own.mark(e.tensor_scalar(qd[rows, b].rearrange("p k c -> p (k c)")[:, at:at + 3 * BH + 7:BH + 2],
                                                 q_s[rows, b], SCALE, None, ALU.mult))
                    for k in range(AB):
                        at = 2 * k + par
                        own.mark(e.tensor_copy(prdh[rows, k, at:BH:HEADS], prd[rows, :, k]))
                for g in range(PAGES - 2, -1, -1):
                    own.mark(e.tensor_tensor(later[:, g], later[:, g + 1], lfc[:, g + 1], ALU.add))
                    own.settle()
                e.tensor_tensor(lfn[:].rearrange("p (b h) -> p b h", b=DEC),
                                spread(lf[:, SEQ:N], 2, (HEADS, DEC, HEADS)),
                                spread(cst[0:HEADS, IDENT:IDENT + HEADS], 1, (HEADS, DEC, HEADS)), ALU.mult).then_inc(smp_in, 1)

            def sample_max():
                e.wait_ge(smp_pe, 1)
                e.wait_ge(kv_used, DEC)
                own.mark(e.tensor_copy(sm[:, 0:1], small[0:BH, 0:1]))
                own.mark(e.tensor_reduce(sm[:, 1:2], cached[0:BH].rearrange("p a n -> p (a n)"), AX, ALU.max))
                own.settle()
                own.mark(e.tensor_tensor(sm[:, 1:2], sm[:, 1:2], sm[:, 0:1], ALU.max))
                own.settle()
                e.tensor_scalar(sm[:, 2:3], sm[:, 1:2], -1.0, None, ALU.mult).then_inc(smp_in, 1)

            def sample_norm():
                e.wait_ge(smp_act, 2)
                own.mark(e.tensor_tensor(sm[:, 5:6], sm[:, 3:4], sm[:, 4:5], ALU.add))
                own.settle()
                own.mark(e.reciprocal(sm[:, 6:7], sm[:, 5:6]))
                own.settle()
                e.tensor_scalar(ps[:], ps[:], sm[:, 6:7], None, ALU.mult).then_inc(smp_in, 1)
                own.mark(e.tensor_tensor(sm[:, 7:8], sm[:, 4:5], sm[:, 6:7], ALU.mult))
                own.settle()
                e.tensor_scalar(psd[:], cst[0:BH, IDENT:IDENT + BH], sm[:, 7:8], None, ALU.mult).then_inc(smp_in, 1)

            def sample_turned():
                e.wait_ge(smp_pe, 2)
                e.tensor_copy(ptp[:, :, 0:BH], cached[:, 0, :].rearrange("p (g c) -> p g c", g=PAGES)).then_inc(smp_in, 1)
                e.wait_ge(smp_pe, 3)
                own_p = small[:, 0:BH].rearrange("p (b k r) -> p k b r", b=DEC, r=2)
                for par in range(2):
                    rows = slice(HD * par, HD * par + HD)
                    own.mark(e.tensor_tensor(t3[rows], proj[rows, 5 * AB:6 * AB, SEQ:N], own_p[rows, :, :, par], ALU.mult))

            units = HEADS * QT
            sample = {SMP["operands"]: sample_operands, SMP["max"]: sample_max, SMP["norm"]: sample_norm,
                      SMP["turned"]: sample_turned}
            unit_max(0)
            for u in range(units):
                if u + 1 < units:
                    unit_max(u + 1)
                unit_norm(u)
                if u in sample:
                    sample[u]()
                elif u in CONV_AT:
                    conv(CONV_AT.index(u))
            own.settle()
            e.wait_ge(kv_used, 2 * DEC)
            e.wait_ge(o_taken, units)
            e.tensor_tensor(om[:], cached, spread(cab[:, HMASK:HMASK + 512], 1, (P, 2, 512)), ALU.mult).then_inc(smp_in, 1)
            e.wait_ge(smp_pe, 4)
            e.tensor_tensor(proj[:, AB:2 * AB, SEQ:N], t3[:], small[:, P:P + AB * DEC].rearrange("p (k b) -> p k b", k=AB),
                            ALU.add).then_inc(cat_ready, 1)

            split_x(1, proj, False)
            add_stage(C_WO0)
            norm(0, res)
            split_x(2, xt, True)

            def peer(layer):
                split_stage(C_WQ[layer], N_WQ)
                subs = GH // SUB
                per = 5 * NPAIR + 5 * HEADS + 14
                for w in range(NT + 1):
                    tt = w + layer * NT
                    ranking = topk(tt, Steps(e, topk_step, tt * per), per) if w < NT else iter(())
                    if w:
                        e.wait_ge(pick_taken, tt)
                        for n in range(GROUPS):
                            one_hots((tt - 1) * GROUPS + n, n % 2, n * SUB)
                            for _ in range((n + 1) * RANK_PARTS // RANK_IN - n * RANK_PARTS // RANK_IN):
                                next(ranking, None)
                    for _ in ranking:
                        pass

                def split_v(g, v):
                    e.wait_ge(v_hi, g * 8 + (layer * NG * 8 + v + 1))
                    e.tensor_tensor(vlo[:, v % 4, :], vraw[:, v % 4, :], vhi[:, v % 4, :].bitcast(F32), ALU.subtract).then_inc(v_lo, 1)

                def gated(g, j):
                    at = g * GROUP + (layer * P + j)
                    e.wait_ge(g_in[j], g * 16 + 16 * (layer * NG + 1))
                    e.wait_ge(h_in[j], g * 16 + 16 * (layer * NG + 1))
                    if j >= 2 or layer or not isinstance(g, int) or g > 0:
                        e.wait_ge(wt_lo, at - 1)
                    e.tensor_tensor(wt[:, j % 2, :], hl[:, j, :], gc[:, j, :], ALU.mult).then_inc(g_used, 1)

                def split_wt(g, j, par):
                    e.wait_ge(wt_hi, g * GROUP + (layer * P + j + 1))
                    e.tensor_tensor(wtl[:, par, j, :], wt[:, j % 2, :], wth[:, par, j, :].bitcast(F32), ALU.subtract).then_inc(wt_lo, 1)

                def take_v(g, v):
                    at = g * 8 + (layer * NG * 8 + v)
                    e.wait_ge(v_done, at + 1)
                    if not (isinstance(g, int) and g == 0):
                        e.wait_ge(v_taken, at - 7)
                    r = halves(res[:, v, :])
                    e.tensor_tensor(r, r, aux[:, 2 * (v % 2):2 * (v % 2) + 2, 0:HALF], ALU.add).then_inc(v_taken, 1)

                def period(g, par, more):
                    for v in range(8):
                        if more and v < GROUP:
                            gated(g + 1, v)
                        if more and 1 <= v <= GROUP:
                            split_wt(g + 1, v - 1, 1 - par)
                        if v < 6:
                            split_v(g, v + 2)
                        elif more:
                            split_v(g + 1, v - 6)
                        take_v(g, v)

                for j in range(GROUP):
                    gated(0, j)
                    if j:
                        split_wt(0, j - 1, 0)
                split_wt(0, GROUP - 1, 0)
                split_v(0, 0)
                split_v(0, 1)
                period(0, 0, True)
                with e.Fori(0, NG // 2 - 1) as q:
                    period(q * 2 + 1, 1, True)
                    period(q * 2 + 2, 0, True)
                period(NG - 1, 1, False)
                if layer + 1 < DEPTH:
                    for slot in range(2):
                        split_chunk(C_INC // 2, slot)

            def topk(tt, s, per):
                R = slice(0, TT)
                e.wait_ge(sc_taken, 4 * (tt + 1))
                for q in range(NPAIR):
                    if q % 4 == 0:
                        yield
                    s.mark(e.max(tv[R, q, 0:8], scores[R, q, :]))
                s.settle()
                for q in range(NPAIR):
                    if q % 4 == 0:
                        yield
                    s.mark(e.max_index(ti[R, q, 0:8], tv[R, q, 0:8], scores[R, q, :]))
                s.settle()
                for q in range(NPAIR):
                    if q % 4 == 0:
                        yield
                    s.mark(e.match_replace(scores[R, q, :], tv[R, q, 0:8], scores[R, q, :], NEG))
                s.settle()
                for q in range(NPAIR):
                    if q % 4 == 0:
                        yield
                    s.mark(e.max(tv[R, q, 8:16], scores[R, q, :]))
                s.settle()
                for q in range(NPAIR):
                    if q % 4 == 0:
                        yield
                    s.mark(e.max_index(ti[R, q, 8:16], tv[R, q, 8:16], scores[R, q, :]))
                s.settle()
                yield
                s.mark(e.tensor_copy(tif[R], ti[R]))
                pairs = tv[R].rearrange("p (h a) k -> p h a k", a=2)
                cand = scores[R].rearrange("p (h x) k -> p h (x k)", x=2)
                s.mark(e.tensor_tensor(cand.rearrange("p h (a b) -> p h a b", a=TOPK),
                                       spread(pairs[:, :, 0, :], 3, (TT, HEADS, TOPK, TOPK)),
                                       spread(pairs[:, :, 1, :], 2, (TT, HEADS, TOPK, TOPK)), ALU.add))
                s.settle()
                for h in range(HEADS):
                    if h % 2 == 0:
                        yield
                    s.mark(e.max(bv[R, h, 0:8], cand[:, h, :]))
                s.settle()
                for h in range(HEADS):
                    if h % 2 == 0:
                        yield
                    s.mark(e.max_index(bp[R, h * TOPK:h * TOPK + 8], bv[R, h, 0:8], cand[:, h, :]))
                s.settle()
                for h in range(HEADS):
                    if h % 2 == 0:
                        yield
                    s.mark(e.match_replace(cand[:, h, :], bv[R, h, 0:8], cand[:, h, :], NEG))
                s.settle()
                for h in range(HEADS):
                    if h % 2 == 0:
                        yield
                    s.mark(e.max(bv[R, h, 8:16], cand[:, h, :]))
                s.settle()
                for h in range(HEADS):
                    if h % 2 == 0:
                        yield
                    s.mark(e.max_index(bp[R, h * TOPK + 8:h * TOPK + 16], bv[R, h, 8:16], cand[:, h, :]))
                s.settle()
                s.mark(e.tensor_copy(gs[R, 0, :], bv[R, :, 0]))
                s.settle()
                e.tensor_tensor(bv[R], bv[R], spread(gs[R, 0, :], 2, (TT, HEADS, TOPK)), ALU.subtract).then_inc(gate_shift, 1)
                s.mark(e.tensor_scalar(bu[R, 0, :], bp[R], 4, None, ALU.logical_shift_right))
                s.mark(e.tensor_scalar(bu[R, 1, :], bp[R], 15, None, ALU.bitwise_and))
                s.settle()
                s.mark(e.tensor_copy(bf[R], bu[R]))
                s.settle()
                lists = tif[R].rearrange("p (h a) k -> p h a k", a=2)
                for a in range(2):
                    yield
                    s.mark(e.tensor_tensor(eq[R], spread(cst[R, IOTA:IOTA + TOPK], 1, (TT, HJ, TOPK)),
                                           spread(bf[R, a, :], 2, (TT, HJ, TOPK)), ALU.is_equal))
                    s.settle()
                    yield
                    by_head = eq[R].rearrange("p (h r) k -> p h r k", h=HEADS)
                    s.mark(e.tensor_tensor(by_head, by_head, spread(lists[:, :, a, :], 2, (TT, HEADS, TOPK, TOPK)), ALU.mult))
                    s.settle()
                    yield
                    s.mark(e.tensor_reduce(pick[R, a, :], eq[R], AX, ALU.add))
                    s.settle()
                yield
                e.wait_ge(gate_exp, tt + 1)
                s.mark(e.tensor_reduce(gs[R, 0, :], bv[R], AX, ALU.add))
                s.settle()
                s.mark(e.reciprocal(gs[R, 1, :], gs[R, 0, :]))
                s.settle()
                e.tensor_tensor(pick[R, 2, :].rearrange("p (h r) -> p h r", h=HEADS), bv[R],
                                spread(gs[R, 1, :], 2, (TT, HEADS, TOPK)), ALU.mult).then_inc(pick_ready, 1)
                assert s.marked == per

            def one_hots(n, slot, at):
                shape = (P, SUB, P)
                if n >= 2:
                    e.wait_ge(gate_done, n - 1)
                e.tensor_tensor(oh2[:, slot], spread(c(IOTA), 1, shape), spread(pickt[:, 1, at:at + SUB], 2, shape),
                                ALU.is_equal).then_inc(oh_ready, 1)
                for r in range(SUB):
                    e.tensor_scalar(oh1[:, slot, r, :], c(IOTA), pickt[:, 0, at + r:at + r + 1],
                                    pickt[:, 2, at + r:at + r + 1], ALU.is_equal, ALU.mult).then_inc(oh_ready, 1)

            if upto >= 1:
                peer(0)
            if upto >= 3:
                norm(1, res)
                split_x(3, xt, True)
                split_stage(C_INC, N_INC)
                e.wait_ge(sgu_in, 32)
                e.tensor_tensor(ws[:], ws[:], spread(c(UTRI), 1, (P, KB, P)), ALU.mult).then_inc(ws_masked, 1)
                norm(2, uv[:, KB:2 * KB, :])
                e.wait_ge(ln_out, 8 * 3)
                for g in range(KB):
                    own.mark(e.tensor_scalar(sps[:, g, :], uv[:, KB + g, SEQ:N], vec[:, V_W00 + g:V_W00 + g + 1],
                                             vec[:, V_B00 + g:V_B00 + g + 1], ALU.mult, ALU.add))
                own.settle()
                for g in range(KB):
                    e.tensor_tensor(uv[:, g, SEQ:N], uv[:, g, SEQ:N], sps[:, g, :], ALU.mult).then_inc(mix_ready, 1)
                for g in range(KB):
                    e.wait_ge(sg_done, g + 1)
                    e.tensor_tensor(sp[:, g % 2, :].rearrange("p (t n) -> p t n", t=QT),
                                    aux[:, 2 + g % 2, :].rearrange("p (t n) -> p t n", t=QT),
                                    spread(bs[:, g, :], 1, (P, QT, P)), ALU.add).then_inc(sg_taken, 1)
                    e.wait_ge(sg_taken, g + 1)
                    e.tensor_tensor(uv[:, g, 0:SEQ], uv[:, g, 0:SEQ], sp[:, g % 2, :], ALU.mult).then_inc(mix_ready, 1)
                    e.wait_ge(mix_ready, KB + g + 1)
                split_x(4, uv, False)
                add_stage(C_WOC)
                norm(3, res)
                split_x(5, xt, True)
                peer(1)
                norm(4, res)

        @block.tensor
        def _(e):
            def chunk(first, pair, slot):
                lo_ready(e, first, pair, slot)
                if first or not isinstance(pair, int) or pair > 0:
                    e.wait_ge(chunk_taken, pair * 2 + (first + slot - 1))
                for k in range(KB):
                    for w, x in ((whi, xh), (whi, xl), (wlo, xh)):
                        for h in range(2):
                            mm = e.matmul(pstr[:, slot, h, 0:HALF], w[:, slot, k * P:(k + 1) * P],
                                          x[:, k, h * HALF:(h + 1) * HALF],
                                          start=k == 0 and w is whi and x is xh, stop=k == KB - 1 and w is wlo)
                mm.then_inc(chunk_done, 1)

            def stage(first, count, splits):
                e.wait_ge(x_lo, 8 * splits)
                for slot in range(2):
                    chunk(first, 0, slot)
                with e.Fori(1, count // 2) as p:
                    for slot in range(2):
                        chunk(first, p, slot)

            def norm(n, src):
                for h in range(2):
                    for k in range(KB):
                        mm = e.matmul(aux[:, h, 0:HALF], c(MEAN), src[:, k, h * HALF:(h + 1) * HALF],
                                      start=k == 0, stop=k == KB - 1)
                mm.then_inc(ln_mean, 1)
                for k in range(KB):
                    e.wait_ge(ln_sq, 8 * n + k + 1)
                    for h in range(2):
                        mm = e.matmul(aux[:, 2 + h, 0:HALF], c(MEAN), sq[:, k % 2, h * HALF:(h + 1) * HALF],
                                      start=k == 0, stop=k == KB - 1)
                    mm.then_inc(ln_var, 1)

            e.wait_ge(setup_in, 80)
            for h in range(2):
                for k in range(KB):
                    mm = e.matmul(aux[0:HEADS, h, 0:HALF], wf[:, k, :], xt[:, k, h * HALF:(h + 1) * HALF],
                                  start=k == 0, stop=k == KB - 1)
            mm.then_inc(f_done, 1)
            stage(C_AB, N_AB, 1)

            e.wait_ge(chunk_taken, C_WO0)
            for t in range(QT):
                for b in range(AB):
                    mm = e.transpose(pstr[:, t // 2, t % 2, b * P:(b + 1) * P], proj[:, 5 * AB + b, t * P:(t + 1) * P], c(IDENT))
                mm.then_inc(vt_done, 1)

            def spread_ncum(h):
                if h == 0:
                    e.wait_ge(f_ncum, 1)
                    e.wait_ge(vn_ready, QT)
                else:
                    e.wait_ge(nb_ready, h)
                e.matmul(pstr[:, 0, 1, :], ca(SELH + h * P, HEADS), ncum[:], start=True, stop=True).then_inc(nb_done, 1)

            def scores_unit(u):
                h, q = divmod(u, QT)
                rows = slice(HD * (h % 2), HD * (h % 2) + HD)
                if u >= 2:
                    e.wait_ge(s_taken, u - 1)
                e.matmul(aux[:, u % 2, 0:(q + 1) * P], proj[rows, 3 * AB + h // 2, q * P:(q + 1) * P],
                         proj[rows, 4 * AB + h // 2, 0:(q + 1) * P], start=True, stop=True).then_inc(qk_done, 1)

            def values_unit(u):
                h, q = divmod(u, QT)
                rows = slice(HD * (h % 2), HD * (h % 2) + HD)
                e.wait_ge(p_ready, u + 1)
                if u >= 2:
                    e.wait_ge(pt_ready, u - 1)
                for b in range(q + 1):
                    mm = e.transpose(aux[:, 2 + u % 2, b * P:(b + 1) * P], pr[:, u % 2, b * P:(b + 1) * P], c(IDENT))
                mm.then_inc(pt_done, 1)

            def out_unit(u):
                h, q = divmod(u, QT)
                rows = slice(HD * (h % 2), HD * (h % 2) + HD)
                e.wait_ge(pt_ready, u + 1)
                if u >= 2:
                    e.wait_ge(o_taken, u - 1)
                for b in range(q + 1):
                    mm = e.matmul(pstr[rows, 0, 0, u % 2 * P:(u % 2 + 1) * P], vn[:, b, h * HD:(h + 1) * HD], pt[:, u % 2, b * P:(b + 1) * P],
                                  start=b == 0, stop=b == q)
                mm.then_inc(pv_done, 1)

            cached = pstr[:, 1, :, :]
            small = pstr[:, 0, 0, 2 * P:4 * P]

            def sample_bias():
                e.wait_ge(smp_in, 1)
                for half in range(2):
                    e.matmul(cached[0:BH, half, :], lfn[:], cst[0:HEADS, ONES:ONES + 1].to_broadcast([HEADS, 512]),
                             start=True, stop=False)
                for g in range(PAGES):
                    dst = cached[0:BH, g // 4, g % 4 * P:(g % 4 + 1) * P]
                    e.matmul(dst, lfc[:, g].rearrange("p b h -> p (b h)"), ca(TRI), start=False, stop=False)
                    e.matmul(dst, later[:, g].rearrange("p b h -> p (b h)"), c(ONES), start=False, stop=False)
                for k in range(AB):
                    mm = e.matmul(small[0:BH, 0:1], prdh[:, k, :], c(ONES, 1), start=k == 0, stop=k == AB - 1)
                mm.then_inc(smp_pe, 1)

            def sample_keys(b, half):
                e.wait_ge(kv_in[b % 2], 16 * PAGES * (b // 2 + 1))
                pages = kv[:, b % 2, half * 4 * 512:(half + 1) * 4 * 512].rearrange("p (g c) -> p g c", g=4)
                for k in range(AB):
                    mm = e.matmul(cached[0:BH, half, :].rearrange("p (g c) -> p g c", g=4), qd[:, b, k, :],
                                  pages[:, :, k * P:(k + 1) * P], start=False, stop=b == DEC - 1 and k == AB - 1)
                if half:
                    mm.then_inc(kv_used, 1)

            def sample_turn():
                e.wait_ge(smp_in, 3)
                for g in range(PAGES):
                    mm = e.transpose(cached[:, 0, g * BH:(g + 1) * BH], ps[:, g * P:(g + 1) * P], cst[0:BH, IDENT:IDENT + BH])
                mm.then_inc(smp_pe, 1)
                e.wait_ge(smp_in, 4)
                e.matmul(small[:, 0:BH], c(ONES, P, BH), psd[:], start=True, stop=True).then_inc(smp_pe, 1)

            def sample_values(b, half):
                if b == 0:
                    e.wait_ge(smp_in, 5)
                e.wait_ge(kv_in[b % 2], 16 * PAGES * (b // 2 + 1 + DEC // 2))
                rows = slice(32 * (b % 4), 32 * (b % 4) + 32)
                for g in range(half * 4, half * 4 + 4):
                    mm = e.matmul(cached[rows, b // 4, :], ptp[:, g, b * HEADS:b * HEADS + 32], kv[:, b % 2, g * 512:(g + 1) * 512],
                                  start=g == 0, stop=g == PAGES - 1)
                if half:
                    mm.then_inc(kv_used, 1)

            units = HEADS * QT
            spread_ncum(0)
            scores_unit(0)
            scores_unit(1)
            for u in range(units):
                values_unit(u)
                if (u + 2) % QT == 0 and u + 2 < units:
                    spread_ncum((u + 2) // QT)
                if u + 2 < units:
                    scores_unit(u + 2)
                out_unit(u)
                if u == SMP["bias"]:
                    sample_bias()
                if SMP["keys"] <= u < SMP["keys"] + 2 * DEC:
                    sample_keys(*divmod(u - SMP["keys"], 2))
                if u == SMP["turn"]:
                    sample_turn()
                if u >= SMP["values"]:
                    sample_values(*divmod(u - SMP["values"], 2))
            for n in range(units - SMP["values"], 2 * DEC):
                sample_values(*divmod(n, 2))
            e.wait_ge(smp_in, 6)
            for k in range(AB):
                for half in range(2):
                    at = P + (k * 2 + half) * 4
                    mm = e.matmul(small[:, at:at + 4], om[:, half, k * P:(k + 1) * P], cab[:, SELB:SELB + 4],
                                  start=True, stop=True)
            mm.then_inc(smp_pe, 1)

            stage(C_WO0, N_WO, 2)
            e.wait_ge(chunk_taken, C_WO0 + N_WO)
            norm(0, res)

            def peer(layer, splits):
                stage(C_WQ[layer], N_WQ, splits)
                e.wait_ge(chunk_taken, C_WQ[layer] + N_WQ)
                e.wait_ge(keys_in, 16 * (layer + 1))

                def gate_group(n, slot):
                    e.wait_ge(oh_ready, (n + 1) * (SUB + 1))
                    if not isinstance(n, int) or n >= 2:
                        e.wait_ge(gate_taken, n - 1)
                    for r in range(SUB):
                        mm = e.matmul(aux[:, slot, r * P:(r + 1) * P], oh2[:, slot, r, :], oh1[:, slot, r, :],
                                      start=True, stop=True)
                    mm.then_inc(gate_done, 1)

                def first_table(pair):
                    for slot in range(2):
                        chunk(C_U[layer], pair, slot)

                pair = 0
                for w, (zero, one, two) in enumerate(PLAN):
                    tt = w + layer * NT
                    if w < NT:
                        for b in range(4):
                            if b == 1 and tt:
                                e.wait_ge(pick_taken, tt)
                            elif tt or b >= 2:
                                e.wait_ge(sc_taken, tt * 4 + b - 1)
                            for q in range(4 * b, 4 * b + 4):
                                mm = e.matmul(aux[0:TT, 2 + b % 2, q % 4 * P:(q % 4 + 1) * P],
                                              q_t[:, q, w * TT:(w + 1) * TT], keys[:, q, :], start=True, stop=True)
                            mm.then_inc(sc_done, 1)
                    if zero:
                        first_table(pair)
                        with e.Fori(pair + 1, pair + zero) as p:
                            first_table(p)
                        pair += zero
                    n = (tt - 1) * GROUPS
                    if one:
                        def one_group_each(q):
                            for slot in range(2):
                                chunk(C_U[layer], q + pair, slot)
                                gate_group(q * 2 + (n + slot), slot)

                        if n == 0:
                            one_group_each(0)
                        with e.Fori(1 if n == 0 else 0, one) as q:
                            one_group_each(q)
                        pair += one
                        n += 2 * one
                    if two:
                        with e.Fori(0, two) as q:
                            for slot in range(2):
                                chunk(C_U[layer], q + pair, slot)
                                for k in range(2):
                                    gate_group(q * 4 + (n + 2 * slot + k), k)
                        pair += two
                    if w < NT:
                        e.wait_ge(pick_ready, tt + 1)
                        for a in range(3):
                            mm = e.transpose(aux[:, 3, a * TT:(a + 1) * TT], pick[0:TT, a, :], cst[0:TT, IDENT:IDENT + TT])
                        mm.then_inc(pick_done, 1)
                with e.Fori(pair, P // 2) as p:
                    first_table(p)

                def second_table(g, v, par):
                    at = g * 8 + (layer * NG * 8 + v)
                    e.wait_ge(v_lo, at + 1)
                    if v == 0:
                        e.wait_ge(wt_lo, g * GROUP + (layer * P + GROUP))
                    if v >= 2 or layer or not isinstance(g, int) or g > 0:
                        e.wait_ge(v_taken, at - 1)
                    for j in range(GROUP):
                        for w, x in ((vhi, wth), (vhi, wtl), (vlo, wth)):
                            for h in range(2):
                                mm = e.matmul(aux[:, 2 * (v % 2) + h, 0:HALF], w[:, v % 4, j * P:(j + 1) * P],
                                              x[:, par, j, h * HALF:(h + 1) * HALF],
                                              start=j == 0 and w is vhi and x is wth, stop=j == GROUP - 1 and w is vlo)
                    mm.then_inc(v_done, 1)

                def period(g, par):
                    for v in range(8):
                        second_table(g, v, par)

                period(0, 0)
                with e.Fori(0, NG // 2 - 1) as q:
                    period(q * 2 + 1, 1)
                    period(q * 2 + 2, 0)
                period(NG - 1, 1)

            if upto >= 1:
                peer(0, 3)
            if upto >= 3:
                e.wait_ge(v_taken, NG * 8)
                norm(1, res)
                stage(C_INC, N_INC, 4)
                e.wait_ge(chunk_taken, C_INC + N_INC)
                norm(2, uv[:, KB:2 * KB, :])
                e.wait_ge(ln_out, 8 * 3)
                e.wait_ge(ws_masked, 1)

                def turn(g):
                    if g >= 2:
                        e.wait_ge(st_ready, g - 1)
                    for t in range(QT):
                        mm = e.transpose(aux[:, g % 2, t * P:(t + 1) * P], uv[:, KB + g, t * P:(t + 1) * P], c(IDENT))
                    mm.then_inc(st_done, 1)

                turn(0)
                for g in range(KB):
                    if g + 1 < KB:
                        turn(g + 1)
                    e.wait_ge(st_ready, g + 1)
                    if g >= 2:
                        e.wait_ge(sg_taken, g - 1)
                    for t in range(QT):
                        mm = e.matmul(aux[:, 2 + g % 2, t * P:(t + 1) * P], vnt[:, g % 2, t * P:(t + 1) * P], ws[:, g, :],
                                      start=True, stop=True)
                    mm.then_inc(sg_done, 1)
                stage(C_WOC, N_WO, 5)
                e.wait_ge(chunk_taken, C_WOC + N_WO)
                norm(3, res)
                peer(1, 6)
                e.wait_ge(v_taken, 2 * NG * 8)
                norm(4, res)


OUTS = {"y": (P, KB, N), "k": (P, AB, N), "v": (P, AB, N), "lf": (HEADS, N), "cp": (P, AB, 2),
        "cs": (P, AB, DEC, 2), "sgv": (P, KB, DEC)}


def constants():
    cst = np.zeros((P, N_CST), np.float32)
    cab = np.zeros((P, N_CAB), np.float32)
    r = np.arange(P)
    cst[:, IDENT:IDENT + P] = np.eye(P)
    cst[:, ONES:ONES + P] = 1.0
    cst[:, IOTA:IOTA + P] = r[None, :]
    cst[:, UTRI:UTRI + P] = r[None, :] >= r[:, None]
    cst[:, MEAN:MEAN + P] = 1.0 / D_MODEL
    cab[:, TRI:TRI + P] = r[:, None] > r[None, :]
    cab[:, CMASK:CMASK + P] = np.where(r[None, :] <= r[:, None], 0.0, -1.0e30)
    cab[:, HMASK:HMASK + 512] = r[:, None] % 32 == np.arange(512)[None, :] // HD
    cab[:, SELB:SELB + 4] = r[:, None] // 32 == np.arange(4)[None, :]
    for h in range(HEADS):
        cab[h, SELH + h * P:SELH + (h + 1) * P] = 1.0
    return cst, cab


def lay_out(x_prompt, x_sample, cache_k, cache_v, cache_logf, state_conv, page_table, w_in_ab, b_f, conv_w,
            w_o_ab, w_in_c, sg_ln_g, sg_ln_b, w_s, b_s, w_o_c, ln1_g, ln1_b, ln2_g, ln2_b,
            peer_wq, peer_keys, peer_u, peer_v):
    f = np.ascontiguousarray
    phys = cache_k.shape[0]

    def chunks(w):
        return w.reshape(KB, P, -1, P).transpose(2, 1, 0, 3)

    x = np.concatenate([x_prompt.reshape(SEQ, D_MODEL), x_sample.reshape(DEC, D_MODEL)])
    cols = 6 * AB * P
    vec = np.zeros((P, N_VEC), np.float32)
    for layer in range(DEPTH):
        for n, a in enumerate((ln1_g, ln1_b, ln2_g, ln2_b)):
            at = V_LN + 32 * layer + 8 * n
            vec[:, at:at + KB] = a[layer].reshape(KB, P).T
    vec[:, V_SG:V_SG + KB] = sg_ln_g[0].reshape(KB, P).T
    vec[:, V_SG + 8:V_SG + 8 + KB] = sg_ln_b[0].reshape(KB, P).T
    vec[:, V_W00:V_W00 + KB] = w_s[0, :, 0, 0][None, :]
    vec[:, V_B00:V_B00 + KB] = b_s[0, :, 0][None, :]
    vec[:, V_CONV:V_CONV + 3 * AB] = conv_w[0].reshape(3 * AB, P).T
    vec[0:HEADS, V_BF] = b_f[0]
    cst, cab = constants()
    return {
        "cst": cst,
        "cab": cab,
        "vec": vec,
        "xt": f(x.T.reshape(KB, P, N).transpose(1, 0, 2)),
        "wf": f(w_in_ab[0][:, cols:].reshape(KB, P, HEADS).transpose(1, 0, 2)),
        "w": f(np.concatenate([chunks(w_in_ab[0][:, :cols]), chunks(w_o_ab[0]), chunks(peer_wq[0]),
                               chunks(w_in_c[0]), chunks(w_o_c[0]), chunks(peer_wq[1])])),
        "u": f(peer_u.reshape(DEPTH * P, P, KB, P).transpose(0, 3, 2, 1)),
        "v": f(peer_v.reshape(DEPTH, NG, GROUP, P, KB, P).transpose(0, 1, 4, 3, 2, 5)).reshape(DEPTH * NG * KB, P, GROUP * P),
        "keys": f(peer_keys.transpose(0, 4, 1, 2, 3)).reshape(DEPTH, P, NPAIR, P),
        "pt": f(page_table.reshape(1, DEC * PAGES)),
        "state": f(state_conv[:, 0].transpose(2, 0, 1).reshape(AB, P, DEC, 2).transpose(1, 0, 2, 3)),
        "clf": f(cache_logf[:, 0]),
        "ck": f(cache_k[:, 0].reshape(phys, PAGE, AB, P).transpose(0, 3, 2, 1)).reshape(phys, P, 512),
        "cv": f(cache_v[:, 0].reshape(phys, PAGE, 512)),
        "ws": f(w_s[0].transpose(2, 0, 1)),
        "bs": f(np.broadcast_to(b_s[0], (P, KB, P))),
    }


def arrange(r):
    def rows(a):
        return a.transpose(2, 1, 0).reshape(a.shape[2], -1)

    y, k, v = rows(r["y"]), rows(r["k"]), rows(r["v"])
    lf = r["lf"].T
    cp = rows(r["cp"])
    cs = r["cs"].transpose(2, 3, 1, 0).reshape(DEC, 1, 2, 512)
    return (y[:SEQ].reshape(1, SEQ, D_MODEL), y[SEQ:].reshape(DEC, 1, D_MODEL),
            k[:SEQ].reshape(1, 1, SEQ, HEADS, HD), v[:SEQ].reshape(1, 1, SEQ, HEADS, HD), lf[:SEQ].reshape(1, 1, SEQ, HEADS),
            k[SEQ:].reshape(DEC, 1, 1, HEADS, HD), v[SEQ:].reshape(DEC, 1, 1, HEADS, HD), lf[SEQ:].reshape(DEC, 1, 1, HEADS),
            cp.reshape(1, 1, 2, 512), cs, rows(r["sgv"]).reshape(DEC, 1, 1, D_MODEL))


def kernel(**inputs):
    import concourse.bacc as bacc
    from concourse.bass_utils import run_bass_kernel_spmd

    arrays = lay_out(**{n: np.asarray(a) for n, a in inputs.items()})
    nc = bacc.Bacc("TRN2", target_bir_lowering=False, num_devices=1)
    ins = {n: nc.dram_tensor(f"in_{n}", a.shape, mybir.dt.from_np(a.dtype), kind="ExternalInput").ap() for n, a in arrays.items()}
    outs = {n: nc.dram_tensor(f"out_{n}", s, F32, kind="ExternalOutput").ap() for n, s in OUTS.items()}
    trunk(nc, ins, outs)
    r = run_bass_kernel_spmd(nc, [{f"in_{n}": a for n, a in arrays.items()}], core_ids=[0])
    return arrange({n: r.results[0][f"out_{n}"] for n in OUTS})
```

```python
from contextlib import ExitStack

import numpy as np

import concourse.bass as bass
from concourse import mybir

F32 = mybir.dt.float32
F32R = mybir.dt.float32r
U32 = mybir.dt.uint32
I32 = mybir.dt.int32
ALU = mybir.AluOpType
ACT = mybir.ActivationFunctionType
AX = mybir.AxisListType.X

P = 128
D_MODEL = 1024
KB = D_MODEL // P
SEQ = 512
DEC = 8
N = SEQ + DEC
HALF = N // 2
DEPTH = 2
ALPHA = (2.0 * DEPTH) ** 0.25
EPS = 1e-5
HEADS = 8
HD = 64
AB = 4
QT = SEQ // P
PAGES = 8
PAGE = 128
NPAIR = HEADS * 2
TOPK = 16
HJ = HEADS * TOPK
TT = 104
NT = N // TT
GH = 52
SUB = 4
GROUP = 4
NG = 128 // GROUP
PLAN = [(6, 0, 0), (0, 11, 1), (0, 11, 1), (0, 9, 2), (0, 9, 2), (0, 1, 6)]
TAIL = 5
GROUPS = TT // SUB
EXP_AT = 17
RANK_PARTS = 48
RANK_IN = 22
PIECES = 4
assert (sum(map(sum, PLAN)) + TAIL) * 2 == P and len(PLAN) == NT + 1
assert all(2 * one + 4 * two == GROUPS for _, one, two in PLAN[1:])
NEG = -3.0e38
SCALE = HD ** -0.5

N_AB, N_WO, N_WQ, N_U, N_INC = 24, 8, 16, 128, 16
C_AB = 0
C_WO0 = C_AB + N_AB
C_WQ = [C_WO0 + N_WO, 0]
C_U = [C_WQ[0] + N_WQ, 0]
C_INC = C_U[0] + N_U
C_WOC = C_INC + N_INC
C_WQ[1] = C_WOC + N_WO
C_U[1] = C_WQ[1] + N_WQ

SMP = {"operands": 0, "bias": 1, "keys": 2, "max": 17, "exp": 19, "norm": 19, "turn": 20, "turned": 20, "values": 21}
CONV_AT = [3, 6, 9, 12]

LN_OF = {2: 0, 3: 1, 5: 3}

IDENT, ONES, IOTA, UTRI, MEAN, N_CST = 0, 128, 256, 384, 512, 640
TRI, CMASK, HMASK, SELB, SELH = 0, 128, 256, 768, 800
N_CAB = SELH + HEADS * P
BH = DEC * HEADS
V_LN = 0
V_SG = 64
V_W00 = 80
V_B00 = 88
V_CONV = 96
V_BF = 108
V_EPS = 109
N_VEC = 112


class Steps:

    def __init__(self, engine, sem, count=0):
        self.engine, self.sem, self.count, self.marked = engine, sem, count, 0

    def mark(self, instruction):
        instruction.then_inc(self.sem, 1)
        self.count = self.count + 1
        self.marked += 1

    def settle(self):
        self.engine.wait_ge(self.sem, self.count)


def spread(ap, axis, shape):
    return ap.unsqueeze(axis).to_broadcast(list(shape))


def halves(ap):
    return ap.rearrange("p (h n) -> p h n", h=2)


def trunk(nc, i, o):
    with ExitStack() as ctx:
        used = [nc.sbuf_base + (-nc.sbuf_base) % 64]

        def place(name, shape, dtype, at=None):
            n = int(np.prod(shape[1:])) * 4
            if at is None:
                at = used[0]
                used[0] += (n + 31) // 32 * 32
            return nc.alloc_sbuf_tensor_at(name, list(shape), dtype, offset=at)

        cst = place("cst", [P, N_CST], F32)
        vec = place("vec", [P, N_VEC], F32)
        at_xt = used[0]
        xt = place("xt", [P, KB, N], F32)
        at_xh = used[0]
        xh = place("xh", [P, KB, N], F32R)
        xl = place("xl", [P, KB, N], F32R)
        res = place("res", [P, KB, N], F32)
        wraw = place("wraw", [P, 2, KB * P], F32)
        whi = place("whi", [P, 2, KB * P], F32R)
        wlo = place("wlo", [P, 2, KB * P], F32R)
        at_ln = used[0]
        used[0] += 8320
        rstd = place("rstd", [P, N], F32, at_ln)
        sq = place("sq", [P, 2, N], F32, at_ln + 4 * N)
        phase = used[0]

        kv = place("kv", [P, 2, PAGES * 512], F32, at_xh)
        cab = place("cab", [P, N_CAB], F32)
        proj = place("proj", [P, N_AB, N], F32)
        zp = place("zp", [P, AB, SEQ + 2], F32)
        zs = place("zs", [P, AB, DEC, 3], F32)
        wf = place("wf", [P, KB, HEADS], F32)
        lf = place("lf", [HEADS, N], F32)
        lt = place("lt", [HEADS, 2, N], F32)
        ncum = place("ncum", [HEADS, SEQ], F32)
        vn = place("vn", [P, QT, 512], F32)
        nb = place("nb", [P, 2, SEQ], F32)
        sc = place("sc", [P, 2, SEQ], F32)
        pr = place("pr", [P, 2, SEQ], F32)
        pt = place("pt", [P, 2, SEQ], F32)
        st = place("st", [P, 2, 4], F32)
        t1 = place("t1", [P, SEQ], F32)
        t2 = place("t2", [P, DEC], F32)
        pg = place("pg", [1, DEC * PAGES], I32)
        qd = place("qd", [P, DEC, AB, BH], F32, at_ln)
        prd = place("prd", [P, DEC, AB], F32)
        prdh = place("prdh", [P, AB, BH], F32)
        lfc = place("lfc", [P, PAGES, DEC, HEADS], F32)
        later = place("later", [P, PAGES, DEC, HEADS], F32, at_xt + 0)
        lfn = place("lfn", [HEADS, BH], F32, at_xt + 13312)
        ps = place("ps", [BH, PAGES * PAGE], F32, at_xt + 2048)
        psd = place("psd", [BH, BH], F32, at_xt + 13568)
        sm = place("sm", [BH, 8], F32)
        ptp = place("ptp", [P, PAGES, 96], F32, at_xt + 10240)
        om = place("om", [P, 2, 512], F32, at_xt + 6144)
        t3 = place("t3", [P, AB, DEC], F32)
        assert used[0] <= nc.sbuf_usable_end, used[0]
        used[0] = phase
        scores = place("scores", [P, NPAIR, P], F32, at_xt)
        keys = place("keys", [P, NPAIR, P], F32, at_xt + 8192)
        eq = place("eq", [P, HJ, TOPK], F32, at_ln)
        q_t = place("q_t", [P, NPAIR, N], F32)
        tv = place("tv", [P, NPAIR, TOPK], F32)
        ti = place("ti", [P, NPAIR, TOPK], U32)
        tif = place("tif", [P, NPAIR, TOPK], F32)
        bv = place("bv", [P, HEADS, TOPK], F32)
        bp = place("bp", [P, HJ], U32)
        bu = place("bu", [P, 2, HJ], U32)
        bf = place("bf", [P, 2, HJ], F32)
        pick = place("pick", [P, 3, HJ], F32)
        gs = place("gs", [P, 2, HEADS], F32)
        pickt = place("pickt", [P, 3, TT], F32)
        oh1 = place("oh1", [P, 2, SUB, P], F32)
        oh2 = place("oh2", [P, 2, SUB, P], F32)
        gst = place("gst", [P, 2, P, GH], F32)
        choice_end = used[0]
        used[0] = phase
        vraw = place("vraw", [P, 4, GROUP * P], F32)
        vhi = place("vhi", [P, 4, GROUP * P], F32R)
        vlo = place("vlo", [P, 4, GROUP * P], F32R)
        wth = place("wth", [P, 2, GROUP, N], F32R)
        wtl = place("wtl", [P, 2, GROUP, N], F32R)
        gc = place("gc", [P, GROUP, N], F32)
        hl = place("hl", [P, GROUP, N], F32)
        wt = place("wt", [P, 2, N], F32)
        hid = place("hid", [P, 2, N], F32, max(used[0], choice_end))
        used[0] = max(used[0], choice_end) + 2 * 4 * N
        assert used[0] <= nc.sbuf_usable_end, used[0]
        used[0] = phase
        uv = place("uv", [P, 2 * KB, N], F32)
        vnt = place("vnt", [P, 2, QT * P], F32)
        ws = place("ws", [P, KB, P], F32)
        bs = place("bs", [P, KB, P], F32)
        sps = place("sps", [P, KB, DEC], F32)
        assert used[0] <= nc.sbuf_usable_end, used[0]

        gates = [nc.dram_tensor(f"gates{n}", (P, P, N), F32, kind="Internal").ap() for n in range(DEPTH)]

        hidden = [nc.dram_tensor(f"hidden{n}", (P, P, N), F32, kind="Internal").ap() for n in range(DEPTH)]

        pstr = ctx.enter_context(nc.psum_tensor("pstr", [P, 2, 2, 512], F32))
        aux = ctx.enter_context(nc.psum_tensor("aux", [P, 4, 512], F32))

        def sem(name):
            return ctx.enter_context(nc.semaphore(name))

        setup_in = sem("setup_in")
        cab_in = sem("cab_in")
        pages_in = sem("pages_in")
        state_in = sem("state_in")
        logf_in = sem("logf_in")
        w_in = [sem(f"w_in{n}") for n in range(2)]
        kv_in = [[sem(f"kv_in{n}{half}") for half in range(2)] for n in range(2)]
        v_in = [sem(f"v_in{n}") for n in range(4)]
        g_in = [sem(f"g_in{n}") for n in range(4)]
        h_out = [sem(f"h_out{n}") for n in range(2)]
        h_in = [sem(f"h_in{n}") for n in range(GROUP)]
        keys_in = sem("keys_in")
        sgu_in = sem("sgu_in")
        out_done = sem("out_done")
        gates_out = [sem(f"gates_out{n}") for n in range(2)]
        y_out = sem("y_out")
        w_hi = sem("w_hi")
        w_lo = sem("w_lo")
        u_lo = sem("u_lo")
        chunk_done = sem("chunk_done")
        chunk_taken = sem("chunk_taken")
        x_hi = sem("x_hi")
        x_lo = sem("x_lo")
        res_ready = sem("res_ready")
        ln_mean = sem("ln_mean")
        ln_centred = sem("ln_centred")
        ln_sq = sem("ln_sq")
        ln_var = sem("ln_var")
        ln_root = sem("ln_root")
        ln_rstd = sem("ln_rstd")
        ln_normed = sem("ln_normed")
        ln_out = sem("ln_out")
        f_done = sem("f_done")
        f_abs = sem("f_abs")
        f_exp = sem("f_exp")
        f_ln = sem("f_ln")
        f_logf = sem("f_logf")
        f_ncum = sem("f_ncum")
        z_done = sem("z_done")
        vt_done = sem("vt_done")
        vn_ready = sem("vn_ready")
        nb_done = sem("nb_done")
        nb_ready = sem("nb_ready")
        qk_done = sem("qk_done")
        s_taken = sem("s_taken")
        max_ready = sem("max_ready")
        exp_done = sem("exp_done")
        p_ready = sem("p_ready")
        pt_done = sem("pt_done")
        pt_ready = sem("pt_ready")
        pv_done = sem("pv_done")
        o_taken = sem("o_taken")
        smp_in = sem("smp_in")
        smp_pe = sem("smp_pe")
        smp_act = sem("smp_act")
        kv_used = sem("kv_used")
        conv_out = sem("conv_out")
        cat_ready = sem("cat_ready")
        sc_done = sem("sc_done")
        sc_taken = sem("sc_taken")
        gate_shift = sem("gate_shift")
        gate_exp = sem("gate_exp")
        pick_ready = sem("pick_ready")
        pick_done = sem("pick_done")
        pick_taken = sem("pick_taken")
        oh_ready = sem("oh_ready")
        gate_done = sem("gate_done")
        gate_taken = sem("gate_taken")
        g_used = sem("g_used")
        wt_hi = sem("wt_hi")
        wt_lo = sem("wt_lo")
        v_hi = sem("v_hi")
        v_lo = sem("v_lo")
        v_done = sem("v_done")
        v_taken = sem("v_taken")
        ws_masked = sem("ws_masked")
        st_done = sem("st_done")
        st_ready = sem("st_ready")
        sg_done = sem("sg_done")
        mix_ready = sem("mix_ready")
        dve_step = sem("dve_step")
        topk_step = sem("topk_step")

        def c(at, n=P, rows=P):
            return cst[0:rows, at:at + n]

        def ca(at, rows=P):
            return cab[0:rows, at:at + P]

        def lo_ready(e, first, pair, slot):
            by_pool = P - 2
            if first in C_U and (not isinstance(pair, int) or pair > 0):
                e.wait_ge(u_lo, pair * 2 + (C_U.index(first) * by_pool + slot - 1))
            else:
                e.wait_ge(w_lo, pair * 2 + (first + slot + 1 - (by_pool if first > C_U[0] else 0)))

        def load_cached(e, b, slot, table, used_before):
            for g in range(PAGES):
                half = g // (PAGES // 2)
                if used_before is not None and g % (PAGES // 2) == 0:
                    e.wait_ge(kv_used, used_before + half)
                r = e.value_load(pg[0:1, bass.ds(b * PAGES + g, 1)], min_val=0, max_val=table.shape[0] - 1)
                e.dma_start(kv[:, slot, g * 512:(g + 1) * 512],
                            table[bass.ds(r, 1)].rearrange("a p c -> p (a c)")).then_inc(kv_in[slot][half], 16)

        def load_cache(e, slot):
            with e.Fori(1, DEC // 2) as p:
                load_cached(e, p * 2 + slot, slot, i["ck"], p * 4 + (2 * slot - 3))
            with e.Fori(0, DEC // 2) as p:
                load_cached(e, p * 2 + slot, slot, i["cv"], p * 4 + (2 * DEC + 2 * slot - 3))

        block = ctx.enter_context(nc.Block())

        @block.sync
        def _(e):
            for dst, src in ((xt[:], i["xt"]), (wf[:], i["wf"]), (vec[:], i["vec"]), (cst[:], i["cst"])):
                e.dma_start(dst, src).then_inc(setup_in, 16)

            def load_chunk(before, pair, slot, src):
                if before is not None:
                    lo_ready(e, *before, slot)
                e.dma_start(wraw[:, slot, :], src.rearrange("a p k c -> p (a k c)")).then_inc(w_in[slot], 16)

            def load_stage(first, count, table, row0, before, done=0):
                if not done:
                    for slot in range(2):
                        load_chunk(before, first // 2, slot, table[row0 + slot:row0 + slot + 1])
                if count == 2:
                    return
                with e.Fori(1, count // 2) as p:
                    for slot in range(2):
                        load_chunk((first, p - 1), p + first // 2, slot, table[bass.ds(p * 2 + (row0 + slot), 1)])

            def load_v(layer, g, v):
                at = g * 8 + (layer * NG * 8 + v)
                if v >= 4 or layer or not isinstance(g, int) or g > 0:
                    e.wait_ge(v_lo, at - 3)
                e.dma_start(vraw[:, v % 4, :], i["v"][bass.ds(at, 1)].rearrange("a p c -> p (a c)")).then_inc(v_in[v % 4], 16)

            def peer_tables(layer):
                subs = GH // SUB
                base = C_U[layer]

                def load_u(pair):
                    before = (C_WQ[layer], N_WQ // 2 - 1) if isinstance(pair, int) and pair == 0 else (base, pair - 1)
                    for slot in range(2):
                        load_chunk(before, pair + base // 2, slot, i["u"][bass.ds(pair * 2 + (layer * P + slot), 1)])

                def store_h(pair):
                    for slot in range(2):
                        e.wait_ge(chunk_taken, pair * 2 + (base + slot + 1))
                        e.dma_start(hidden[layer][bass.ds(pair * 2 + slot, 1)].rearrange("a p n -> p (a n)"),
                                    hid[:, slot, :]).then_inc(h_out[slot], 16)

                def store_gates(half, part):
                    n = P // PIECES
                    e.wait_ge(gate_taken, (half + 1 + layer * NT * 2) * subs)
                    e.dma_start(gates[layer][part * n:(part + 1) * n, :, half * GH:(half + 1) * GH].rearrange("a b n -> b a n"),
                                gst[:, half % 2, part * n:(part + 1) * n, :]).then_inc(gates_out[half % 2], 16)

                def load_h(g, j):
                    at = g * GROUP + (layer * P + j)
                    if layer or not isinstance(g, int) or g > 0:
                        e.wait_ge(g_used, at - 3)
                    e.dma_start(hl[:, j, :], hidden[layer][bass.ds(g * GROUP + j, 1)].rearrange("a p n -> p (a n)")).then_inc(h_in[j], 16)
                    e.dma_start(gc[:, j, :], gates[layer][bass.ds(g * GROUP + j, 1)].rearrange("a p n -> p (a n)")).then_inc(g_in[j], 16)

                load_u(0)
                store = {}
                start = 0
                for w, (zero, one, two) in enumerate(PLAN):
                    if w:
                        done = next(r for r in range(one + two) if 2 * (r + 1) + 2 * max(0, r + 1 - one) >= subs)
                        for part in range(PIECES):
                            store.setdefault(start + done + 1 + part // 2, []).append((2 * w - 2, part))
                            store.setdefault(start + one + two + part // 2, []).append((2 * w - 1, part))
                    start += zero + one + two
                pair = 0
                while pair < P // 2:
                    if pair + 1 < P // 2:
                        load_u(pair + 1)
                    for half, part in store.get(pair, ()):
                        store_gates(half, part)
                    if pair == P // 2 - 3:
                        for par in range(2):
                            e.wait_ge(gates_out[par], 16 * PIECES * NT * (layer + 1))
                        for j in range(GROUP):
                            load_h(0, j)
                        for v in range(4):
                            load_v(layer, 0, v)
                    store_h(pair)
                    pair += 1
                    if pair == 1:
                        with e.Fori(1, PLAN[0][0]) as p:
                            load_u(p + 1)
                            store_h(p)
                        pair = PLAN[0][0]

                for slot in range(2):
                    e.wait_ge(h_out[slot], 16 * (P // 2) * (layer + 1))

                def period(g, more):
                    for v in range(8):
                        if not (isinstance(g, int) and g == 0 and v < 4):
                            load_v(layer, g, v)
                        if more and v % 2 == 0:
                            load_h(g + 1, v // 2)

                period(0, True)
                with e.Fori(1, NG - 1) as g:
                    period(g, True)
                period(NG - 1, False)

            load_stage(C_AB, N_AB, i["w"], 0, None)
            load_stage(C_WO0, 2, i["w"], 24, (C_AB, N_AB // 2 - 1))
            e.wait_ge(pages_in, 16)
            e.wait_ge(chunk_done, C_WO0)
            load_cached(e, 0, 0, i["ck"], None)
            load_cache(e, 0)
            load_stage(C_WO0, N_WO, i["w"], 24, (C_AB, N_AB // 2 - 1), done=2)
            load_stage(C_WQ[0], N_WQ, i["w"], 32, (C_WO0, N_WO // 2 - 1))
            peer_tables(0)
            load_stage(C_INC, N_INC, i["w"], 48, (C_U[0], P // 2 - 1))
            load_stage(C_WOC, N_WO, i["w"], 64, (C_INC, N_INC // 2 - 1))
            load_stage(C_WQ[1], N_WQ, i["w"], 72, (C_WOC, N_WO // 2 - 1))
            peer_tables(1)
            for k in range(KB):
                e.wait_ge(ln_out, 8 * 4 + k + 1)
                e.dma_start(o["y"][:, k, :], xt[:, k, :]).then_inc(y_out, 16)
            e.wait_ge(y_out, 16 * KB)

        @block.gpsimd
        def _(e):
            e.dma_start(pg[:], i["pt"]).then_inc(pages_in, 16)
            e.dma_start(zs[:, :, :, 0:2], i["state"]).then_inc(state_in, 16)
            e.wait_ge(pages_in, 16)
            with e.Fori(0, DEC) as b:
                for g in range(PAGES):
                    r = e.value_load(pg[0:1, bass.ds(b * PAGES + g, 1)], min_val=0, max_val=i["clf"].shape[0] - 1)
                    e.dma_start(lfc[:, g, bass.ds(b, 1), :], i["clf"][bass.ds(r, 1)].rearrange("a p h -> p a h")).then_inc(logf_in, 16)

            e.dma_start(cab[:], i["cab"]).then_inc(cab_in, 16)

            def residual(n):
                for k in range(KB):
                    e.wait_ge(x_hi, 8 * n + k + 1)
                    if n:
                        e.wait_ge(ln_out, 8 * LN_OF[n] + k + 1)
                    e.tensor_scalar(res[:, k, :], xt[:, k, :], ALPHA, None, ALU.mult).then_inc(res_ready, 1)

            e.wait_ge(setup_in, 64)
            residual(0)
            e.wait_ge(chunk_done, C_WO0)
            load_cached(e, 1, 1, i["ck"], None)
            e.wait_ge(chunk_taken, C_WO0)
            e.dma_start(o["k"], proj[:, 16:20, :]).then_inc(out_done, 16)
            e.dma_start(o["v"], proj[:, 20:24, :]).then_inc(out_done, 16)
            e.wait_ge(f_logf, 1)
            e.dma_start(o["lf"], lf[:]).then_inc(out_done, 16)
            e.wait_ge(z_done, 2 * AB)
            e.wait_ge(state_in, 16)
            e.dma_start(o["cp"], zp[:, :, SEQ:SEQ + 2]).then_inc(out_done, 16)
            e.dma_start(o["cs"], zs[:, :, :, 1:3]).then_inc(out_done, 16)
            load_cache(e, 1)
            e.wait_ge(out_done, 16 * 5)

            def peer(layer):
                residual((2, 5)[layer])
                e.wait_ge(res_ready, 8 * (2, 4)[layer])
                lo_ready(e, C_WQ[layer], 1, 0)
                e.dma_start(keys[:], i["keys"][layer]).then_inc(keys_in, 16)
                with e.Fori(1, P // 2) as p:
                    for slot in range(2):
                        pair = p + C_U[layer] // 2
                        e.wait_ge(w_hi, pair * 2 + (slot + 1))
                        e.tensor_tensor(wlo[:, slot, :], wraw[:, slot, :], whi[:, slot, :].bitcast(F32),
                                        ALU.subtract).then_inc(u_lo, 1)

            peer(0)
            e.wait_ge(v_taken, NG * 8)
            e.dma_start(ws[:], i["ws"]).then_inc(sgu_in, 16)
            e.dma_start(bs[:], i["bs"]).then_inc(sgu_in, 16)
            residual(3)
            e.wait_ge(ln_out, 8 * 3)
            e.dma_start(o["sgv"], uv[:, KB:2 * KB, SEQ:N]).then_inc(out_done, 16)
            e.wait_ge(out_done, 16 * 6)
            peer(1)

        @block.scalar
        def _(e):
            def round_chunk(pair, slot):
                e.wait_ge(w_in[slot], 16 * pair + 16)
                if not (isinstance(pair, int) and pair == 0):
                    e.wait_ge(chunk_done, 2 * pair + (slot - 1))
                e.activation(whi[:, slot, :], wraw[:, slot, :], ACT.Copy).then_inc(w_hi, 1)

            def take_stage(first, count, dst, func, col):
                with e.Fori(0, count // 2) as p:
                    for slot in range(2):
                        e.wait_ge(chunk_done, 2 * p + (first + slot + 1))
                        out = dst[:, bass.ds(p * 2 + (col + slot), 1), :].rearrange("p a (h n) -> p (a h) n", h=2)
                        e.activation(out, pstr[:, slot, :, 0:HALF], func).then_inc(chunk_taken, 1)
                        round_chunk(p + (first // 2 + 1), slot)

            def round_stage(first, count):
                with e.Fori(0, count // 2) as p:
                    for slot in range(2):
                        round_chunk(p + (first // 2 + 1), slot)

            def round_x(src, blocks=range(KB)):
                for k in blocks:
                    e.activation(xh[:, k, :], src[:, k, :], ACT.Copy).then_inc(x_hi, 1)

            def norm(n, src, gcol, bcol, dst):
                for k in range(KB):
                    e.wait_ge(ln_centred, 8 * n + k + 1)
                    if k >= 2:
                        e.wait_ge(ln_var, 8 * n + k - 1)
                    e.activation(sq[:, k % 2, :], src[:, k, :], ACT.Square).then_inc(ln_sq, 1)
                e.wait_ge(ln_var, 8 * n + 8)
                e.activation(halves(rstd[:]), aux[:, 2:4, 0:HALF], ACT.Sqrt, bias=vec[:, V_EPS:V_EPS + 1]).then_inc(ln_root, 1)
                for k in range(KB):
                    e.wait_ge(ln_normed, 8 * n + k + 1)
                    bias, scale = vec[:, bcol + k:bcol + k + 1], vec[:, gcol + k:gcol + k + 1]
                    if n in LN_OF.values():
                        e.activation(xh[:, k, :], src[:, k, :], ACT.Identity, bias=bias, scale=scale).then_inc(x_hi, 1)
                    e.activation(dst[:, k, :], src[:, k, :], ACT.Identity, bias=bias, scale=scale).then_inc(ln_out, 1)

            e.wait_ge(setup_in, 64)
            round_x(xt)
            round_chunk(0, 0)
            round_chunk(0, 1)
            e.wait_ge(f_abs, 1)
            e.activation(lt[:, 0, :], lt[:, 0, :], ACT.Abs).then_inc(f_exp, 1)
            e.wait_ge(f_exp, 1)
            e.activation(lt[:, 0, :], lt[:, 0, :], ACT.Exp, scale=-1.0).then_inc(f_exp, 1)
            e.wait_ge(f_exp, 2)
            e.activation(lt[:, 0, :], lt[:, 0, :], ACT.Ln, bias=1.0).then_inc(f_ln, 1)

            take_stage(C_AB, N_AB, proj, ACT.Copy, 0)

            for t in range(QT):
                e.wait_ge(vt_done, t + 1)
                e.activation(vn[:, t, :], pstr[:, t // 2, t % 2, :], ACT.Copy).then_inc(vn_ready, 1)

            def take_nb(h):
                e.wait_ge(nb_done, h + 1)
                if h >= 2:
                    e.wait_ge(s_taken, QT * (h - 1))
                e.activation(nb[:, h % 2, :], pstr[:, 0, 1, :], ACT.Copy).then_inc(nb_ready, 1)

            def exp_unit(u):
                w = (u % QT + 1) * P
                e.wait_ge(max_ready, u + 1)
                if u >= 2:
                    e.wait_ge(pt_done, u - 1)
                e.activation(pr[:, u % 2, 0:w], sc[:, u % 2, 0:w], ACT.Exp, bias=st[:, u % 2, 0:1],
                             accum_out=st[:, u % 2, 1:2]).then_inc(exp_done, 1)

            def take_pt(u):
                w = (u % QT + 1) * P
                e.wait_ge(pt_done, u + 1)
                if u >= 2:
                    e.wait_ge(pv_done, u - 1)
                e.activation(pt[:, u % 2, 0:w], aux[:, 2 + u % 2, 0:w], ACT.Copy).then_inc(pt_ready, 1)

            def take_o(u):
                h, q = divmod(u, QT)
                rows = slice(HD * (h % 2), HD * (h % 2) + HD)
                e.wait_ge(pv_done, u + 1)
                e.activation(proj[rows, AB + h // 2, q * P:(q + 1) * P], pstr[rows, 0, 0, u % 2 * P:(u % 2 + 1) * P],
                             ACT.Copy).then_inc(o_taken, 1)

            units = HEADS * QT
            take_nb(0)
            exp_unit(0)
            for u in range(units):
                if (u + 2) % QT == 0 and (u + 2) // QT < HEADS:
                    take_nb((u + 2) // QT)
                if u + 1 < units:
                    exp_unit(u + 1)
                if u >= 1:
                    take_o(u - 1)
                take_pt(u)
                if u == SMP["exp"]:
                    e.wait_ge(smp_in, 2)
                    e.activation(ps[:], pstr[0:BH, 1, :, :].rearrange("p a n -> p (a n)"), ACT.Exp, bias=sm[:, 2:3],
                                 accum_out=sm[:, 3:4]).then_inc(smp_act, 1)
                    e.activation(sm[:, 4:5], sm[:, 0:1], ACT.Exp, bias=sm[:, 2:3]).then_inc(smp_act, 1)
            take_o(units - 1)

            e.wait_ge(conv_out, AB)
            e.wait_ge(kv_used, 4 * DEC - 2)
            round_x(proj, range(AB))
            e.wait_ge(kv_used, 4 * DEC)
            e.wait_ge(cat_ready, 1)
            round_x(proj, range(AB, 2 * AB))
            round_stage(C_WO0, N_WO)
            norm(0, res, V_LN, V_LN + 8, xt)

            def peer(layer):
                e.wait_ge(out_done, 16 * (5 + layer))
                take_stage(C_WQ[layer], N_WQ, q_t, ACT.Copy, 0)
                subs = GH // SUB
                base = C_U[layer]

                def hidden_one(pair, slot):
                    e.wait_ge(chunk_done, pair * 2 + (base + slot + 1))
                    if layer or not isinstance(pair, int) or pair > 0:
                        e.wait_ge(h_out[slot], pair * 16 + 16 * (layer * P // 2))
                    e.activation(halves(hid[:, slot, :]), pstr[:, slot, :, 0:HALF], ACT.Gelu_apprx_tanh).then_inc(chunk_taken, 1)
                    if not isinstance(pair, int) or pair + 1 < P // 2:
                        round_chunk(pair + (base // 2 + 1), slot)

                def hidden_pair(pair):
                    for slot in range(2):
                        hidden_one(pair, slot)

                def take_gates(tt, n):
                    half = tt * 2 + n // subs
                    if n % subs == 0 and half >= 2:
                        e.wait_ge(gates_out[half % 2], 16 * PIECES * (half // 2))
                    e.wait_ge(gate_done, tt * GROUPS + (n + 1))
                    e.activation(gst[:, half % 2, :, n % subs * SUB:(n % subs + 1) * SUB].rearrange("p a n -> p n a"),
                                 aux[:, n % 2, :].rearrange("p (n a) -> p n a", n=SUB), ACT.Copy).then_inc(gate_taken, 1)

                def gate_exponentials(tt):
                    e.wait_ge(gate_shift, tt + 1)
                    e.activation(bv[0:TT, :, :], bv[0:TT, :, :], ACT.Exp).then_inc(gate_exp, 1)

                pair = 0
                for w, (zero, one, two) in enumerate(PLAN):
                    tt = w + layer * NT
                    if w < NT:
                        for b in range(4):
                            e.wait_ge(sc_done, tt * 4 + b + 1)
                            e.activation(scores[0:TT, 4 * b:4 * b + 4, :].rearrange("p a k -> p (a k)"),
                                         aux[0:TT, 2 + b % 2, :], ACT.Copy).then_inc(sc_taken, 1)
                    if zero:
                        hidden_pair(pair)
                        with e.Fori(pair + 1, pair + zero - 2) as p:
                            hidden_pair(p)
                        gate_exponentials(tt)
                        for p in range(pair + zero - 2, pair + zero):
                            hidden_pair(p)
                    n = 0
                    for q in range(one + two):
                        for slot in range(2):
                            hidden_one(pair + zero + q, slot)
                            for _ in range(1 if q < one else 2):
                                if n == EXP_AT and w < NT:
                                    gate_exponentials(tt)
                                take_gates(tt - 1, n)
                                n += 1
                    if w < NT:
                        e.wait_ge(pick_done, tt + 1)
                        e.activation(pickt[:].rearrange("p a n -> p (a n)"), aux[:, 3, 0:3 * TT], ACT.Copy).then_inc(pick_taken, 1)
                    pair += zero + one + two
                with e.Fori(pair, P // 2 - 1) as p:
                    hidden_pair(p)

                for par in range(2):
                    e.wait_ge(gates_out[par], 16 * PIECES * NT * (layer + 1))

                def round_v(g, v):
                    at = g * 8 + (layer * NG * 8 + v)
                    e.wait_ge(v_in[v % 4], g * 32 + 16 * (layer * NG * 2 + v // 4 + 1))
                    if v >= 4 or layer or not isinstance(g, int) or g > 0:
                        e.wait_ge(v_done, at - 3)
                    e.activation(vhi[:, v % 4, :], vraw[:, v % 4, :], ACT.Copy).then_inc(v_hi, 1)

                def round_wt(g, j, par):
                    e.wait_ge(g_used, g * GROUP + (layer * P + j + 1))
                    if j == 0 and (not isinstance(g, int) or g > 1):
                        e.wait_ge(v_done, g * 8 + (layer * NG * 8 - 8))
                    e.activation(wth[:, par, j, :], wt[:, j % 2, :], ACT.Copy).then_inc(wt_hi, 1)

                def period(g, par, more):
                    for v in range(8):
                        if more and v % 2 == 0:
                            round_wt(g + 1, v // 2, 1 - par)
                        if v < 6:
                            round_v(g, v + 2)
                        elif more:
                            round_v(g + 1, v - 6)

                for j in range(GROUP):
                    round_wt(0, j, 0)
                round_v(0, 0)
                round_v(0, 1)
                hidden_pair(P // 2 - 1)
                period(0, 0, True)
                with e.Fori(0, NG // 2 - 1) as q:
                    period(q * 2 + 1, 1, True)
                    period(q * 2 + 2, 0, True)
                period(NG - 1, 1, False)
                if layer + 1 < DEPTH:
                    for slot in range(2):
                        round_chunk(C_INC // 2, slot)

            peer(0)
            norm(1, res, V_LN + 16, V_LN + 24, xt)
            take_stage(C_INC, N_INC, uv, ACT.Gelu_apprx_tanh, 0)
            norm(2, uv[:, KB:2 * KB, :], V_SG, V_SG + 8, uv[:, KB:2 * KB, :])
            for g in range(KB + 2):
                if g < KB:
                    e.wait_ge(st_done, g + 1)
                    if g >= 2:
                        e.wait_ge(sg_done, g - 1)
                    e.activation(vnt[:, g % 2, :], aux[:, g % 2, :], ACT.Copy).then_inc(st_ready, 1)
                if g >= 2:
                    e.wait_ge(mix_ready, KB + g - 1)
                    round_x(uv, [g - 2])
            round_stage(C_WOC, N_WO)
            norm(3, res, V_LN + 32, V_LN + 40, xt)
            peer(1)
            norm(4, res, V_LN + 48, V_LN + 56, xt)

        @block.vector
        def _(e):
            own = Steps(e, dve_step)

            def split_chunk(pair, slot):
                e.wait_ge(w_hi, 2 * pair + (slot + 1))
                e.tensor_tensor(wlo[:, slot, :], wraw[:, slot, :], whi[:, slot, :].bitcast(F32), ALU.subtract).then_inc(w_lo, 1)

            def split_stage(first, count):
                with e.Fori(0, count // 2) as p:
                    for slot in range(2):
                        split_chunk(p + (first // 2 + 1), slot)

            def split_x(n, src, blocks=range(KB)):
                for k in blocks:
                    e.wait_ge(x_hi, 8 * n + k + 1)
                    if n in LN_OF:
                        e.wait_ge(ln_out, 8 * LN_OF[n] + k + 1)
                    e.tensor_tensor(xl[:, k, :], src[:, k, :], xh[:, k, :].bitcast(F32), ALU.subtract).then_inc(x_lo, 1)

            def add_stage(first):
                e.wait_ge(res_ready, 8 if first == C_WO0 else 24)
                with e.Fori(0, N_WO // 2) as p:
                    for slot in range(2):
                        e.wait_ge(chunk_done, 2 * p + (first + slot + 1))
                        r = res[:, bass.ds(p * 2 + slot, 1), :].rearrange("p a (h n) -> p (a h) n", h=2)
                        e.tensor_tensor(r, r, pstr[:, slot, :, 0:HALF], ALU.add).then_inc(chunk_taken, 1)
                        split_chunk(p + (first // 2 + 1), slot)

            def norm(n, src, mean, split=None):
                e.wait_ge(ln_mean, n + 1)
                for k in range(KB):
                    s = halves(src[:, k, :])
                    e.tensor_tensor(s, s, mean[:, :, 0:HALF], ALU.subtract).then_inc(ln_centred, 1)
                e.wait_ge(ln_root, n + 1)
                e.reciprocal(rstd[:], rstd[:]).then_inc(ln_rstd, 1)
                e.wait_ge(ln_rstd, n + 1)
                for k in range(KB):
                    e.tensor_tensor(src[:, k, :], src[:, k, :], rstd[:], ALU.mult).then_inc(ln_normed, 1)
                    if split and k >= 2:
                        split_x(split, xt, [k - 2])
                if split:
                    split_x(split, xt, [KB - 2, KB - 1])

            e.wait_ge(setup_in, 64)
            for zero in (qd, prdh):
                own.mark(e.memset(zero[:], 0.0))
            split_x(0, xt)
            split_chunk(0, 0)
            split_chunk(0, 1)
            e.wait_ge(f_done, 1)
            for r in range(2):
                own.mark(e.tensor_scalar(halves(lt[:, r, :]), aux[0:HEADS, 0:2, 0:HALF], vec[0:HEADS, V_BF:V_BF + 1], None, ALU.add))
            own.settle()
            e.tensor_scalar(lt[:, 1, :], lt[:, 1, :], 0.0, None, ALU.min).then_inc(f_abs, 1)
            e.wait_ge(f_abs, 1)
            e.wait_ge(f_ln, 1)
            e.tensor_tensor(lf[:], lt[:, 1, :], lt[:, 0, :], ALU.subtract).then_inc(f_logf, 1)
            e.wait_ge(f_logf, 1)
            own.mark(e.tensor_tensor_scan(ncum[:], cst[0:HEADS, ONES:ONES + 1].to_broadcast([HEADS, SEQ]), lf[:, 0:SEQ],
                                          0.0, ALU.mult, ALU.add))
            own.settle()
            e.tensor_scalar(ncum[:], ncum[:], -1.0, None, ALU.mult).then_inc(f_ncum, 1)

            split_stage(C_AB, N_AB)

            def unit_max(u):
                h, q = divmod(u, QT)
                w = (q + 1) * P
                e.wait_ge(qk_done, u + 1)
                if q == 0:
                    e.wait_ge(nb_ready, h + 1)
                if u >= 2:
                    e.wait_ge(exp_done, u - 1)
                s = sc[:, u % 2, 0:w]
                e.scalar_tensor_tensor(s, aux[:, u % 2, 0:w], SCALE, nb[:, h % 2, 0:w], ALU.mult, ALU.add).then_inc(s_taken, 1)
                e.wait_ge(s_taken, u + 1)
                diag = sc[:, u % 2, w - P:w]
                own.mark(e.tensor_tensor(diag, diag, ca(CMASK), ALU.add))
                own.settle()
                own.mark(e.tensor_reduce(st[:, u % 2, 2:3], s, AX, ALU.max))
                own.settle()
                e.tensor_scalar(st[:, u % 2, 0:1], st[:, u % 2, 2:3], -1.0, None, ALU.mult).then_inc(max_ready, 1)

            def unit_norm(u):
                w = (u % QT + 1) * P
                e.wait_ge(exp_done, u + 1)
                own.mark(e.reciprocal(st[:, u % 2, 3:4], st[:, u % 2, 1:2]))
                own.settle()
                p = pr[:, u % 2, 0:w]
                e.tensor_scalar(p, p, st[:, u % 2, 3:4], None, ALU.mult).then_inc(p_ready, 1)

            e.wait_ge(cab_in, 16)
            e.wait_ge(chunk_taken, C_WO0)
            e.wait_ge(state_in, 16)
            own.mark(e.memset(zp[:, :, 0:2], 0.0))
            for b in range(AB):
                e.tensor_tensor(zp[:, b, 2:SEQ + 2], proj[:, AB + b, 0:SEQ], proj[:, 2 * AB + b, 0:SEQ], ALU.mult).then_inc(z_done, 1)
                e.tensor_tensor(zs[:, b, :, 2], proj[:, AB + b, SEQ:N], proj[:, 2 * AB + b, SEQ:N], ALU.mult).then_inc(z_done, 1)
            own.settle()

            def conv(b):
                e.wait_ge(z_done, 2 * (b + 1))
                if b:
                    e.wait_ge(conv_out, b)
                for dst, taps, gate in ((t1[:], [zp[:, b, j:j + SEQ] for j in range(3)], proj[:, b, 0:SEQ]),
                                        (t2[:], [zs[:, b, :, j] for j in range(3)], proj[:, b, SEQ:N])):
                    for j in range(3):
                        w = vec[:, V_CONV + j * AB + b:V_CONV + j * AB + b + 1]
                        if j == 0:
                            own.mark(e.tensor_scalar(dst, taps[j], w, None, ALU.mult))
                        else:
                            own.mark(e.scalar_tensor_tensor(dst, taps[j], w, dst, ALU.mult, ALU.add))
                        own.settle()
                    if gate.shape[-1] == SEQ:
                        own.mark(e.tensor_tensor(gate, gate, dst, ALU.mult))
                    else:
                        own.settle()
                        e.tensor_tensor(gate, gate, dst, ALU.mult).then_inc(conv_out, 1)

            cached = pstr[:, 1, :, :]
            small = pstr[:, 0, 0, 2 * P:4 * P]

            def sample_operands():
                q_s = proj[:, 3 * AB:4 * AB, SEQ:N].rearrange("p k b -> p b k")
                k_s = proj[:, 4 * AB:5 * AB, SEQ:N].rearrange("p k b -> p b k")
                e.wait_ge(logf_in, 16 * DEC * PAGES)
                e.wait_ge(res_ready, KB)
                own.mark(e.memset(ptp[:], 0.0))
                own.mark(e.memset(later[:, PAGES - 1, :, :], 0.0))
                own.mark(e.scalar_tensor_tensor(prd[:], q_s, SCALE, k_s, ALU.mult, ALU.mult))
                own.settle()
                for par in range(2):
                    rows = slice(HD * par, HD * par + HD)
                    for b in range(DEC):
                        at = b * HEADS + par
                        own.mark(e.tensor_scalar(qd[rows, b].rearrange("p k c -> p (k c)")[:, at:at + 3 * BH + 7:BH + 2],
                                                 q_s[rows, b], SCALE, None, ALU.mult))
                    for k in range(AB):
                        at = 2 * k + par
                        own.mark(e.tensor_copy(prdh[rows, k, at:BH:HEADS], prd[rows, :, k]))
                for g in range(PAGES - 2, -1, -1):
                    own.mark(e.tensor_tensor(later[:, g], later[:, g + 1], lfc[:, g + 1], ALU.add))
                    own.settle()
                e.tensor_tensor(lfn[:].rearrange("p (b h) -> p b h", b=DEC),
                                spread(lf[:, SEQ:N], 2, (HEADS, DEC, HEADS)),
                                spread(cst[0:HEADS, IDENT:IDENT + HEADS], 1, (HEADS, DEC, HEADS)), ALU.mult).then_inc(smp_in, 1)

            def sample_max():
                e.wait_ge(smp_pe, 1)
                e.wait_ge(kv_used, 2 * DEC)
                own.mark(e.tensor_copy(sm[:, 0:1], small[0:BH, 0:1]))
                own.mark(e.tensor_reduce(sm[:, 1:2], cached[0:BH].rearrange("p a n -> p (a n)"), AX, ALU.max))
                own.settle()
                own.mark(e.tensor_tensor(sm[:, 1:2], sm[:, 1:2], sm[:, 0:1], ALU.max))
                own.settle()
                e.tensor_scalar(sm[:, 2:3], sm[:, 1:2], -1.0, None, ALU.mult).then_inc(smp_in, 1)

            def sample_norm():
                e.wait_ge(smp_act, 2)
                own.mark(e.tensor_tensor(sm[:, 5:6], sm[:, 3:4], sm[:, 4:5], ALU.add))
                own.settle()
                own.mark(e.reciprocal(sm[:, 6:7], sm[:, 5:6]))
                own.settle()
                e.tensor_scalar(ps[:], ps[:], sm[:, 6:7], None, ALU.mult).then_inc(smp_in, 1)
                own.mark(e.tensor_tensor(sm[:, 7:8], sm[:, 4:5], sm[:, 6:7], ALU.mult))
                own.settle()
                e.tensor_scalar(psd[:], cst[0:BH, IDENT:IDENT + BH], sm[:, 7:8], None, ALU.mult).then_inc(smp_in, 1)

            def sample_turned():
                e.wait_ge(smp_pe, 2)
                e.tensor_copy(ptp[:, :, 0:BH], cached[:, 0, :].rearrange("p (g c) -> p g c", g=PAGES)).then_inc(smp_in, 1)
                e.wait_ge(smp_pe, 3)
                own_p = small[:, 0:BH].rearrange("p (b k r) -> p k b r", b=DEC, r=2)
                for par in range(2):
                    rows = slice(HD * par, HD * par + HD)
                    own.mark(e.tensor_tensor(t3[rows], proj[rows, 5 * AB:6 * AB, SEQ:N], own_p[rows, :, :, par], ALU.mult))

            units = HEADS * QT
            sample = {SMP["operands"]: sample_operands, SMP["max"]: sample_max, SMP["norm"]: sample_norm,
                      SMP["turned"]: sample_turned}
            unit_max(0)
            for u in range(units):
                if u + 1 < units:
                    unit_max(u + 1)
                unit_norm(u)
                if u in sample:
                    sample[u]()
                elif u in CONV_AT:
                    conv(CONV_AT.index(u))
            own.settle()
            e.wait_ge(kv_used, 4 * DEC)
            e.wait_ge(o_taken, units)
            e.tensor_tensor(om[:], cached, spread(cab[:, HMASK:HMASK + 512], 1, (P, 2, 512)), ALU.mult).then_inc(smp_in, 1)
            split_x(1, proj, range(AB))
            e.wait_ge(smp_pe, 4)
            e.tensor_tensor(proj[:, AB:2 * AB, SEQ:N], t3[:], aux[:, 3, 0:AB * DEC].rearrange("p (k b) -> p k b", k=AB),
                            ALU.add).then_inc(cat_ready, 1)

            split_x(1, proj, range(AB, 2 * AB))
            add_stage(C_WO0)
            norm(0, res, aux[:, 0:2], 2)

            def peer(layer):
                split_stage(C_WQ[layer], N_WQ)
                e.wait_ge(res_ready, 8 * (2, 4)[layer])
                per = 5 * NPAIR + 5 * HEADS + 14
                for w in range(NT + 1):
                    tt = w + layer * NT
                    ranking = topk(tt, Steps(e, topk_step, tt * per), per) if w < NT else iter(())
                    if w:
                        e.wait_ge(pick_taken, tt)
                        for n in range(GROUPS):
                            one_hots((tt - 1) * GROUPS + n, n % 2, n * SUB)
                            for _ in range((n + 1) * RANK_PARTS // RANK_IN - n * RANK_PARTS // RANK_IN):
                                next(ranking, None)
                    for _ in ranking:
                        pass

                def split_v(g, v):
                    e.wait_ge(v_hi, g * 8 + (layer * NG * 8 + v + 1))
                    e.tensor_tensor(vlo[:, v % 4, :], vraw[:, v % 4, :], vhi[:, v % 4, :].bitcast(F32), ALU.subtract).then_inc(v_lo, 1)

                def gated(g, j):
                    at = g * GROUP + (layer * P + j)
                    e.wait_ge(g_in[j], g * 16 + 16 * (layer * NG + 1))
                    e.wait_ge(h_in[j], g * 16 + 16 * (layer * NG + 1))
                    if j >= 2 or layer or not isinstance(g, int) or g > 0:
                        e.wait_ge(wt_lo, at - 1)
                    e.tensor_tensor(wt[:, j % 2, :], hl[:, j, :], gc[:, j, :], ALU.mult).then_inc(g_used, 1)

                def split_wt(g, j, par):
                    e.wait_ge(wt_hi, g * GROUP + (layer * P + j + 1))
                    e.tensor_tensor(wtl[:, par, j, :], wt[:, j % 2, :], wth[:, par, j, :].bitcast(F32), ALU.subtract).then_inc(wt_lo, 1)

                def take_v(g, v):
                    at = g * 8 + (layer * NG * 8 + v)
                    e.wait_ge(v_done, at + 1)
                    if not (isinstance(g, int) and g == 0):
                        e.wait_ge(v_taken, at - 7)
                    r = halves(res[:, v, :])
                    e.tensor_tensor(r, r, aux[:, 2 * (v % 2):2 * (v % 2) + 2, 0:HALF], ALU.add).then_inc(v_taken, 1)

                def period(g, par, more):
                    for v in range(8):
                        if more and v % 2 == 0:
                            gated(g + 1, v // 2)
                        elif more:
                            split_wt(g + 1, v // 2, 1 - par)
                        if v < 6:
                            split_v(g, v + 2)
                        elif more:
                            split_v(g + 1, v - 6)
                        take_v(g, v)

                for j in range(GROUP):
                    gated(0, j)
                    if j:
                        split_wt(0, j - 1, 0)
                split_wt(0, GROUP - 1, 0)
                split_v(0, 0)
                split_v(0, 1)
                period(0, 0, True)
                with e.Fori(0, NG // 2 - 1) as q:
                    period(q * 2 + 1, 1, True)
                    period(q * 2 + 2, 0, True)
                period(NG - 1, 1, False)
                if layer + 1 < DEPTH:
                    for slot in range(2):
                        split_chunk(C_INC // 2, slot)

            def topk(tt, s, per):
                R = slice(0, TT)
                e.wait_ge(sc_taken, 4 * (tt + 1))
                for q in range(NPAIR):
                    if q % 4 == 0:
                        yield
                    s.mark(e.max(tv[R, q, 0:8], scores[R, q, :]))
                s.settle()
                for q in range(NPAIR):
                    if q % 4 == 0:
                        yield
                    s.mark(e.max_index(ti[R, q, 0:8], tv[R, q, 0:8], scores[R, q, :]))
                s.settle()
                for q in range(NPAIR):
                    if q % 4 == 0:
                        yield
                    s.mark(e.match_replace(scores[R, q, :], tv[R, q, 0:8], scores[R, q, :], NEG))
                s.settle()
                for q in range(NPAIR):
                    if q % 4 == 0:
                        yield
                    s.mark(e.max(tv[R, q, 8:16], scores[R, q, :]))
                s.settle()
                for q in range(NPAIR):
                    if q % 4 == 0:
                        yield
                    s.mark(e.max_index(ti[R, q, 8:16], tv[R, q, 8:16], scores[R, q, :]))
                s.settle()
                yield
                s.mark(e.tensor_copy(tif[R], ti[R]))
                pairs = tv[R].rearrange("p (h a) k -> p h a k", a=2)
                cand = scores[R].rearrange("p (h x) k -> p h (x k)", x=2)
                s.mark(e.tensor_tensor(cand.rearrange("p h (a b) -> p h a b", a=TOPK),
                                       spread(pairs[:, :, 0, :], 3, (TT, HEADS, TOPK, TOPK)),
                                       spread(pairs[:, :, 1, :], 2, (TT, HEADS, TOPK, TOPK)), ALU.add))
                s.settle()
                for h in range(HEADS):
                    if h % 2 == 0:
                        yield
                    s.mark(e.max(bv[R, h, 0:8], cand[:, h, :]))
                s.settle()
                for h in range(HEADS):
                    if h % 2 == 0:
                        yield
                    s.mark(e.max_index(bp[R, h * TOPK:h * TOPK + 8], bv[R, h, 0:8], cand[:, h, :]))
                s.settle()
                for h in range(HEADS):
                    if h % 2 == 0:
                        yield
                    s.mark(e.match_replace(cand[:, h, :], bv[R, h, 0:8], cand[:, h, :], NEG))
                s.settle()
                for h in range(HEADS):
                    if h % 2 == 0:
                        yield
                    s.mark(e.max(bv[R, h, 8:16], cand[:, h, :]))
                s.settle()
                for h in range(HEADS):
                    if h % 2 == 0:
                        yield
                    s.mark(e.max_index(bp[R, h * TOPK + 8:h * TOPK + 16], bv[R, h, 8:16], cand[:, h, :]))
                s.settle()
                s.mark(e.tensor_copy(gs[R, 0, :], bv[R, :, 0]))
                s.settle()
                e.tensor_tensor(bv[R], bv[R], spread(gs[R, 0, :], 2, (TT, HEADS, TOPK)), ALU.subtract).then_inc(gate_shift, 1)
                s.mark(e.tensor_scalar(bu[R, 0, :], bp[R], 4, None, ALU.logical_shift_right))
                s.mark(e.tensor_scalar(bu[R, 1, :], bp[R], 15, None, ALU.bitwise_and))
                s.settle()
                s.mark(e.tensor_copy(bf[R], bu[R]))
                s.settle()
                lists = tif[R].rearrange("p (h a) k -> p h a k", a=2)
                for a in range(2):
                    yield
                    s.mark(e.tensor_tensor(eq[R], spread(cst[R, IOTA:IOTA + TOPK], 1, (TT, HJ, TOPK)),
                                           spread(bf[R, a, :], 2, (TT, HJ, TOPK)), ALU.is_equal))
                    s.settle()
                    yield
                    by_head = eq[R].rearrange("p (h r) k -> p h r k", h=HEADS)
                    s.mark(e.tensor_tensor(by_head, by_head, spread(lists[:, :, a, :], 2, (TT, HEADS, TOPK, TOPK)), ALU.mult))
                    s.settle()
                    yield
                    s.mark(e.tensor_reduce(pick[R, a, :], eq[R], AX, ALU.add))
                    s.settle()
                yield
                e.wait_ge(gate_exp, tt + 1)
                s.mark(e.tensor_reduce(gs[R, 0, :], bv[R], AX, ALU.add))
                s.settle()
                s.mark(e.reciprocal(gs[R, 1, :], gs[R, 0, :]))
                s.settle()
                e.tensor_tensor(pick[R, 2, :].rearrange("p (h r) -> p h r", h=HEADS), bv[R],
                                spread(gs[R, 1, :], 2, (TT, HEADS, TOPK)), ALU.mult).then_inc(pick_ready, 1)
                assert s.marked == per

            def one_hots(n, slot, at):
                shape = (P, SUB, P)
                if n >= 2:
                    e.wait_ge(gate_done, n - 1)
                e.tensor_tensor(oh2[:, slot], spread(c(IOTA), 1, shape), spread(pickt[:, 1, at:at + SUB], 2, shape),
                                ALU.is_equal).then_inc(oh_ready, 1)
                for r in range(SUB):
                    e.tensor_scalar(oh1[:, slot, r, :], c(IOTA), pickt[:, 0, at + r:at + r + 1],
                                    pickt[:, 2, at + r:at + r + 1], ALU.is_equal, ALU.mult).then_inc(oh_ready, 1)

            peer(0)
            norm(1, res, pstr[:, 1], 3)
            split_stage(C_INC, N_INC)
            e.wait_ge(sgu_in, 32)
            e.tensor_tensor(ws[:], ws[:], spread(c(UTRI), 1, (P, KB, P)), ALU.mult).then_inc(ws_masked, 1)
            norm(2, uv[:, KB:2 * KB, :], aux[:, 0:2])
            for g in range(KB):
                e.wait_ge(ln_out, 8 * 2 + g + 1)
                own.mark(e.tensor_scalar(sps[:, g, :], uv[:, KB + g, SEQ:N], vec[:, V_W00 + g:V_W00 + g + 1],
                                         vec[:, V_B00 + g:V_B00 + g + 1], ALU.mult, ALU.add))
            own.settle()
            for g in range(KB):
                e.tensor_tensor(uv[:, g, SEQ:N], uv[:, g, SEQ:N], sps[:, g, :], ALU.mult).then_inc(mix_ready, 1)
            for g in range(KB):
                e.wait_ge(sg_done, g + 1)
                e.tensor_tensor(uv[:, g, 0:SEQ], uv[:, g, 0:SEQ], aux[:, 2 + g % 2, :], ALU.mult).then_inc(mix_ready, 1)
                if g >= 3:
                    split_x(4, uv, [g - 3])
            split_x(4, uv, range(KB - 3, KB))
            add_stage(C_WOC)
            norm(3, res, aux[:, 0:2], 5)
            peer(1)
            norm(4, res, pstr[:, 1])

        @block.tensor
        def _(e):
            def chunk(first, pair, slot, split=None):
                lo_ready(e, first, pair, slot)
                if first or not isinstance(pair, int) or pair > 0:
                    e.wait_ge(chunk_taken, pair * 2 + (first + slot - 1))
                for k in range(KB):
                    if split is not None:
                        e.wait_ge(x_lo, 8 * split + k + 1)
                    for w, x in ((whi, xh), (whi, xl), (wlo, xh)):
                        for h in range(2):
                            mm = e.matmul(pstr[:, slot, h, 0:HALF], w[:, slot, k * P:(k + 1) * P],
                                          x[:, k, h * HALF:(h + 1) * HALF],
                                          start=k == 0 and w is whi and x is xh, stop=k == KB - 1 and w is wlo)
                mm.then_inc(chunk_done, 1)

            def stage(first, count, split, means=None):
                chunk(first, 0, 0, split)
                chunk(first, 0, 1)
                start = count // 2 - 3
                if not means or start > 1:
                    with e.Fori(1, start if means else count // 2) as p:
                        for slot in range(2):
                            chunk(first, p, slot)
                if means:
                    src, n = means
                    for slot in range(2):
                        chunk(first, start, slot)
                        mean_block(src, slot, aux[:, 0:2])
                    with e.Fori(start + 1, count // 2) as p:
                        for slot in range(2):
                            chunk(first, p, slot)
                            mean_block(src, p * 2 + (slot - 2 * start), aux[:, 0:2])
                    for k in (6, 7):
                        e.wait_ge(chunk_taken, first + count + k - 7)
                        mm = mean_block(src, k, aux[:, 0:2])
                    mm.then_inc(ln_mean, 1)

            def mean_block(src, k, mean):
                for h in range(2):
                    x = src[:, k, h * HALF:(h + 1) * HALF] if isinstance(k, int) else \
                        src[:, bass.ds(k, 1), h * HALF:(h + 1) * HALF].rearrange("p a n -> p (a n)")
                    mm = e.matmul(mean[:, h, 0:HALF], c(MEAN), x, start=isinstance(k, int) and k == 0,
                                  stop=isinstance(k, int) and k == KB - 1)
                return mm

            def variance(n):
                for k in range(KB):
                    e.wait_ge(ln_sq, 8 * n + k + 1)
                    for h in range(2):
                        mm = e.matmul(aux[:, 2 + h, 0:HALF], c(MEAN), sq[:, k % 2, h * HALF:(h + 1) * HALF],
                                      start=k == 0, stop=k == KB - 1)
                    mm.then_inc(ln_var, 1)

            e.wait_ge(setup_in, 64)
            for h in range(2):
                for k in range(KB):
                    mm = e.matmul(aux[0:HEADS, h, 0:HALF], wf[:, k, :], xt[:, k, h * HALF:(h + 1) * HALF],
                                  start=k == 0, stop=k == KB - 1)
            mm.then_inc(f_done, 1)
            stage(C_AB, N_AB, 0)

            e.wait_ge(chunk_taken, C_WO0)
            for t in range(QT):
                for b in range(AB):
                    mm = e.transpose(pstr[:, t // 2, t % 2, b * P:(b + 1) * P], proj[:, 5 * AB + b, t * P:(t + 1) * P], c(IDENT))
                mm.then_inc(vt_done, 1)

            def spread_ncum(h):
                if h == 0:
                    e.wait_ge(cab_in, 16)
                    e.wait_ge(f_ncum, 1)
                    e.wait_ge(vn_ready, QT)
                else:
                    e.wait_ge(nb_ready, h)
                e.matmul(pstr[:, 0, 1, :], ca(SELH + h * P, HEADS), ncum[:], start=True, stop=True).then_inc(nb_done, 1)

            def scores_unit(u):
                h, q = divmod(u, QT)
                rows = slice(HD * (h % 2), HD * (h % 2) + HD)
                if u >= 2:
                    e.wait_ge(s_taken, u - 1)
                e.matmul(aux[:, u % 2, 0:(q + 1) * P], proj[rows, 3 * AB + h // 2, q * P:(q + 1) * P],
                         proj[rows, 4 * AB + h // 2, 0:(q + 1) * P], start=True, stop=True).then_inc(qk_done, 1)

            def values_unit(u):
                h, q = divmod(u, QT)
                rows = slice(HD * (h % 2), HD * (h % 2) + HD)
                e.wait_ge(p_ready, u + 1)
                if u >= 2:
                    e.wait_ge(pt_ready, u - 1)
                for b in range(q + 1):
                    mm = e.transpose(aux[:, 2 + u % 2, b * P:(b + 1) * P], pr[:, u % 2, b * P:(b + 1) * P], c(IDENT))
                mm.then_inc(pt_done, 1)

            def out_unit(u):
                h, q = divmod(u, QT)
                rows = slice(HD * (h % 2), HD * (h % 2) + HD)
                e.wait_ge(pt_ready, u + 1)
                if u >= 2:
                    e.wait_ge(o_taken, u - 1)
                for b in range(q + 1):
                    mm = e.matmul(pstr[rows, 0, 0, u % 2 * P:(u % 2 + 1) * P], vn[:, b, h * HD:(h + 1) * HD], pt[:, u % 2, b * P:(b + 1) * P],
                                  start=b == 0, stop=b == q)
                mm.then_inc(pv_done, 1)

            cached = pstr[:, 1, :, :]
            small = pstr[:, 0, 0, 2 * P:4 * P]

            def sample_bias():
                e.wait_ge(smp_in, 1)
                for half in range(2):
                    e.matmul(cached[0:BH, half, :], lfn[:], cst[0:HEADS, ONES:ONES + 1].to_broadcast([HEADS, 512]),
                             start=True, stop=False)
                for g in range(PAGES):
                    dst = cached[0:BH, g // 4, g % 4 * P:(g % 4 + 1) * P]
                    e.matmul(dst, lfc[:, g].rearrange("p b h -> p (b h)"), ca(TRI), start=False, stop=False)
                    e.matmul(dst, later[:, g].rearrange("p b h -> p (b h)"), c(ONES), start=False, stop=False)
                for k in range(AB):
                    mm = e.matmul(small[0:BH, 0:1], prdh[:, k, :], c(ONES, 1), start=k == 0, stop=k == AB - 1)
                mm.then_inc(smp_pe, 1)

            def sample_keys(b, half):
                e.wait_ge(kv_in[b % 2][half], 16 * PAGES // 2 * (b // 2 + 1))
                pages = kv[:, b % 2, half * 4 * 512:(half + 1) * 4 * 512].rearrange("p (g c) -> p g c", g=4)
                for k in range(AB):
                    mm = e.matmul(cached[0:BH, half, :].rearrange("p (g c) -> p g c", g=4), qd[:, b, k, :],
                                  pages[:, :, k * P:(k + 1) * P], start=False, stop=b == DEC - 1 and k == AB - 1)
                mm.then_inc(kv_used, 1)

            def sample_turn():
                e.wait_ge(smp_in, 3)
                for g in range(PAGES):
                    mm = e.transpose(cached[:, 0, g * BH:(g + 1) * BH], ps[:, g * P:(g + 1) * P], cst[0:BH, IDENT:IDENT + BH])
                mm.then_inc(smp_pe, 1)
                e.wait_ge(smp_in, 4)
                e.matmul(small[:, 0:BH], c(ONES, P, BH), psd[:], start=True, stop=True).then_inc(smp_pe, 1)

            def sample_values(b, half):
                if b == 0:
                    e.wait_ge(smp_in, 5)
                e.wait_ge(kv_in[b % 2][half], 16 * PAGES // 2 * (b // 2 + 1 + DEC // 2))
                rows = slice(32 * (b % 4), 32 * (b % 4) + 32)
                for g in range(half * 4, half * 4 + 4):
                    mm = e.matmul(cached[rows, b // 4, :], ptp[:, g, b * HEADS:b * HEADS + 32], kv[:, b % 2, g * 512:(g + 1) * 512],
                                  start=g == 0, stop=g == PAGES - 1)
                mm.then_inc(kv_used, 1)

            units = HEADS * QT
            spread_ncum(0)
            scores_unit(0)
            scores_unit(1)
            for u in range(units):
                values_unit(u)
                if (u + 2) % QT == 0 and u + 2 < units:
                    spread_ncum((u + 2) // QT)
                if u + 2 < units:
                    scores_unit(u + 2)
                out_unit(u)
                if u == SMP["bias"]:
                    sample_bias()
                if SMP["keys"] <= u < SMP["keys"] + 2 * DEC:
                    sample_keys(*divmod(u - SMP["keys"], 2))
                if u == SMP["turn"]:
                    sample_turn()
                if u >= SMP["values"]:
                    sample_values(*divmod(u - SMP["values"], 2))
            for n in range(units - SMP["values"], 2 * DEC):
                sample_values(*divmod(n, 2))
            e.wait_ge(smp_in, 6)
            for k in range(AB):
                for half in range(2):
                    at = (k * 2 + half) * 4
                    mm = e.matmul(aux[:, 3, at:at + 4], om[:, half, k * P:(k + 1) * P], cab[:, SELB:SELB + 4],
                                  start=True, stop=True)
            mm.then_inc(smp_pe, 1)

            stage(C_WO0, N_WO, 1, (res, 0))
            variance(0)

            def peer(layer, split):
                stage(C_WQ[layer], N_WQ, split)
                e.wait_ge(chunk_taken, C_WQ[layer] + N_WQ)
                e.wait_ge(keys_in, 16 * (layer + 1))

                def gate_group(n, slot):
                    e.wait_ge(oh_ready, (n + 1) * (SUB + 1))
                    if not isinstance(n, int) or n >= 2:
                        e.wait_ge(gate_taken, n - 1)
                    for r in range(SUB):
                        mm = e.matmul(aux[:, slot, r * P:(r + 1) * P], oh2[:, slot, r, :], oh1[:, slot, r, :],
                                      start=True, stop=True)
                    mm.then_inc(gate_done, 1)

                def first_table(pair):
                    for slot in range(2):
                        chunk(C_U[layer], pair, slot)

                pair = 0
                for w, (zero, one, two) in enumerate(PLAN):
                    tt = w + layer * NT
                    if w < NT:
                        for b in range(4):
                            if b == 1 and tt:
                                e.wait_ge(pick_taken, tt)
                            elif tt or b >= 2:
                                e.wait_ge(sc_taken, tt * 4 + b - 1)
                            for q in range(4 * b, 4 * b + 4):
                                mm = e.matmul(aux[0:TT, 2 + b % 2, q % 4 * P:(q % 4 + 1) * P],
                                              q_t[:, q, w * TT:(w + 1) * TT], keys[:, q, :], start=True, stop=True)
                            mm.then_inc(sc_done, 1)
                    if zero:
                        first_table(pair)
                        with e.Fori(pair + 1, pair + zero) as p:
                            first_table(p)
                        pair += zero
                    n = (tt - 1) * GROUPS
                    if one:
                        def one_group_each(q):
                            for slot in range(2):
                                chunk(C_U[layer], q + pair, slot)
                                gate_group(q * 2 + (n + slot), slot)

                        if n == 0:
                            one_group_each(0)
                        with e.Fori(1 if n == 0 else 0, one) as q:
                            one_group_each(q)
                        pair += one
                        n += 2 * one
                    if two:
                        with e.Fori(0, two) as q:
                            for slot in range(2):
                                chunk(C_U[layer], q + pair, slot)
                                for k in range(2):
                                    gate_group(q * 4 + (n + 2 * slot + k), k)
                        pair += two
                    if w < NT:
                        e.wait_ge(pick_ready, tt + 1)
                        for a in range(3):
                            mm = e.transpose(aux[:, 3, a * TT:(a + 1) * TT], pick[0:TT, a, :], cst[0:TT, IDENT:IDENT + TT])
                        mm.then_inc(pick_done, 1)
                with e.Fori(pair, P // 2) as p:
                    first_table(p)

                def second_table(g, v, par):
                    at = g * 8 + (layer * NG * 8 + v)
                    e.wait_ge(v_lo, at + 1)
                    if v == 0:
                        e.wait_ge(wt_lo, g * GROUP + (layer * P + GROUP))
                    if v >= 2 or layer or not isinstance(g, int) or g > 0:
                        e.wait_ge(v_taken, at - 1)
                    for j in range(GROUP):
                        for w, x in ((vhi, wth), (vhi, wtl), (vlo, wth)):
                            for h in range(2):
                                mm = e.matmul(aux[:, 2 * (v % 2) + h, 0:HALF], w[:, v % 4, j * P:(j + 1) * P],
                                              x[:, par, j, h * HALF:(h + 1) * HALF],
                                              start=j == 0 and w is vhi and x is wth, stop=j == GROUP - 1 and w is vlo)
                    mm.then_inc(v_done, 1)

                def period(g, par):
                    for v in range(8):
                        second_table(g, v, par)

                period(0, 0)
                with e.Fori(0, NG // 2 - 1) as q:
                    period(q * 2 + 1, 1)
                    period(q * 2 + 2, 0)
                for v in range(8):
                    second_table(NG - 1, v, 1)
                    if v >= 2:
                        mean_block(res, v - 2, pstr[:, 1])
                for v in (6, 7):
                    e.wait_ge(v_taken, (layer + 1) * NG * 8 + v - 7)
                    mm = mean_block(res, v, pstr[:, 1])
                mm.then_inc(ln_mean, 1)

            peer(0, 2)
            variance(1)
            stage(C_INC, N_INC, 3, (uv[:, KB:2 * KB, :], 2))
            variance(2)
            e.wait_ge(ws_masked, 1)

            def turn(g):
                e.wait_ge(ln_out, 8 * 2 + g + 1)
                if g >= 2:
                    e.wait_ge(st_ready, g - 1)
                for t in range(QT):
                    mm = e.transpose(aux[:, g % 2, t * P:(t + 1) * P], uv[:, KB + g, t * P:(t + 1) * P], c(IDENT))
                mm.then_inc(st_done, 1)

            turn(0)
            for g in range(KB):
                if g + 1 < KB:
                    turn(g + 1)
                e.wait_ge(st_ready, g + 1)
                if g >= 2:
                    e.wait_ge(mix_ready, KB + g - 1)
                for t in range(QT):
                    dst = aux[:, 2 + g % 2, t * P:(t + 1) * P]
                    e.matmul(dst, vnt[:, g % 2, t * P:(t + 1) * P], ws[:, g, :], start=True, stop=False)
                    mm = e.matmul(dst, c(ONES, P, 1), bs[0:1, g, :], start=False, stop=True)
                mm.then_inc(sg_done, 1)
            stage(C_WOC, N_WO, 4, (res, 3))
            variance(3)
            peer(1, 5)
            variance(4)


OUTS = {"y": (P, KB, N), "k": (P, AB, N), "v": (P, AB, N), "lf": (HEADS, N), "cp": (P, AB, 2),
        "cs": (P, AB, DEC, 2), "sgv": (P, KB, DEC)}


def constants():
    cst = np.zeros((P, N_CST), np.float32)
    cab = np.zeros((P, N_CAB), np.float32)
    r = np.arange(P)
    cst[:, IDENT:IDENT + P] = np.eye(P)
    cst[:, ONES:ONES + P] = 1.0
    cst[:, IOTA:IOTA + P] = r[None, :]
    cst[:, UTRI:UTRI + P] = r[None, :] >= r[:, None]
    cst[:, MEAN:MEAN + P] = 1.0 / D_MODEL
    cab[:, TRI:TRI + P] = r[:, None] > r[None, :]
    cab[:, CMASK:CMASK + P] = np.where(r[None, :] <= r[:, None], 0.0, -1.0e30)
    cab[:, HMASK:HMASK + 512] = r[:, None] % 32 == np.arange(512)[None, :] // HD
    cab[:, SELB:SELB + 4] = r[:, None] // 32 == np.arange(4)[None, :]
    for h in range(HEADS):
        cab[h, SELH + h * P:SELH + (h + 1) * P] = 1.0
    return cst, cab


def lay_out(x_prompt, x_sample, cache_k, cache_v, cache_logf, state_conv, page_table, w_in_ab, b_f, conv_w,
            w_o_ab, w_in_c, sg_ln_g, sg_ln_b, w_s, b_s, w_o_c, ln1_g, ln1_b, ln2_g, ln2_b,
            peer_wq, peer_keys, peer_u, peer_v):
    f = np.ascontiguousarray
    phys = cache_k.shape[0]

    def chunks(w):
        return w.reshape(KB, P, -1, P).transpose(2, 1, 0, 3)

    x = np.concatenate([x_prompt.reshape(SEQ, D_MODEL), x_sample.reshape(DEC, D_MODEL)])
    cols = 6 * AB * P
    vec = np.zeros((P, N_VEC), np.float32)
    for layer in range(DEPTH):
        for n, a in enumerate((ln1_g, ln1_b, ln2_g, ln2_b)):
            at = V_LN + 32 * layer + 8 * n
            vec[:, at:at + KB] = a[layer].reshape(KB, P).T
    vec[:, V_SG:V_SG + KB] = sg_ln_g[0].reshape(KB, P).T
    vec[:, V_SG + 8:V_SG + 8 + KB] = sg_ln_b[0].reshape(KB, P).T
    vec[:, V_W00:V_W00 + KB] = w_s[0, :, 0, 0][None, :]
    vec[:, V_B00:V_B00 + KB] = b_s[0, :, 0][None, :]
    vec[:, V_CONV:V_CONV + 3 * AB] = conv_w[0].reshape(3 * AB, P).T
    vec[0:HEADS, V_BF] = b_f[0]
    vec[:, V_EPS] = EPS
    cst, cab = constants()
    return {
        "cst": cst,
        "cab": cab,
        "vec": vec,
        "xt": f(x.T.reshape(KB, P, N).transpose(1, 0, 2)),
        "wf": f(w_in_ab[0][:, cols:].reshape(KB, P, HEADS).transpose(1, 0, 2)),
        "w": f(np.concatenate([chunks(w_in_ab[0][:, :cols]), chunks(w_o_ab[0]), chunks(peer_wq[0]),
                               chunks(w_in_c[0]), chunks(w_o_c[0]), chunks(peer_wq[1])])),
        "u": f(peer_u.reshape(DEPTH * P, P, KB, P).transpose(0, 3, 2, 1)),
        "v": f(peer_v.reshape(DEPTH, NG, GROUP, P, KB, P).transpose(0, 1, 4, 3, 2, 5)).reshape(DEPTH * NG * KB, P, GROUP * P),
        "keys": f(peer_keys.transpose(0, 4, 1, 2, 3)).reshape(DEPTH, P, NPAIR, P),
        "pt": f(page_table.reshape(1, DEC * PAGES)),
        "state": f(state_conv[:, 0].transpose(2, 0, 1).reshape(AB, P, DEC, 2).transpose(1, 0, 2, 3)),
        "clf": f(cache_logf[:, 0]),
        "ck": f(cache_k[:, 0].reshape(phys, PAGE, AB, P).transpose(0, 3, 2, 1)).reshape(phys, P, 512),
        "cv": f(cache_v[:, 0].reshape(phys, PAGE, 512)),
        "ws": f(w_s[0].transpose(2, 0, 1)),
        "bs": f(np.broadcast_to(b_s[0], (P, KB, P))),
    }


def arrange(r):
    def rows(a):
        return a.transpose(2, 1, 0).reshape(a.shape[2], -1)

    y, k, v = rows(r["y"]), rows(r["k"]), rows(r["v"])
    lf = r["lf"].T
    cp = rows(r["cp"])
    cs = r["cs"].transpose(2, 3, 1, 0).reshape(DEC, 1, 2, 512)
    return (y[:SEQ].reshape(1, SEQ, D_MODEL), y[SEQ:].reshape(DEC, 1, D_MODEL),
            k[:SEQ].reshape(1, 1, SEQ, HEADS, HD), v[:SEQ].reshape(1, 1, SEQ, HEADS, HD), lf[:SEQ].reshape(1, 1, SEQ, HEADS),
            k[SEQ:].reshape(DEC, 1, 1, HEADS, HD), v[SEQ:].reshape(DEC, 1, 1, HEADS, HD), lf[SEQ:].reshape(DEC, 1, 1, HEADS),
            cp.reshape(1, 1, 2, 512), cs, rows(r["sgv"]).reshape(DEC, 1, 1, D_MODEL))


def kernel(**inputs):
    import concourse.bacc as bacc
    from concourse.bass_utils import run_bass_kernel_spmd

    arrays = lay_out(**{n: np.asarray(a) for n, a in inputs.items()})
    nc = bacc.Bacc("TRN2", target_bir_lowering=False, num_devices=1)
    ins = {n: nc.dram_tensor(f"in_{n}", a.shape, mybir.dt.from_np(a.dtype), kind="ExternalInput").ap() for n, a in arrays.items()}
    outs = {n: nc.dram_tensor(f"out_{n}", s, F32, kind="ExternalOutput").ap() for n, s in OUTS.items()}
    trunk(nc, ins, outs)
    r = run_bass_kernel_spmd(nc, [{f"in_{n}": a for n, a in arrays.items()}], core_ids=[0])
    return arrange({n: r.results[0][f"out_{n}"] for n in OUTS})
```
